# Optimizing a Trainium2 kernel written in Bass

```python
import jax, jax.numpy as jnp
from jax import lax
import numpy as np

D_MODEL = 1024
BATCH = 1
SEQ = 512
DEPTH = 2

GRID_W = 64
CTX_LEN = 256
EPS = 1e-6
N_Q_HEADS = 8
N_KV_HEADS = 2
HEAD_DIM = 64
WINDOW = 128
BLOCK = 128
ROPE_BASE = 10000.0
SCONV_DIM = 512
SCONV_WIDTH = 3
POOL_DIM = 512
N_POOL_GROUPS = 4
POOL_GROUP = POOL_DIM // N_POOL_GROUPS
POOL_WINDOWS = (2, 4, 8, 16)
FFT_DIM = 512
N_FFT_GROUPS = 4
FFT_GROUP = FFT_DIM // N_FFT_GROUPS
D_FF = 2816
FFN_CONV_WIDTH = 3

Q_DIM = N_Q_HEADS * HEAD_DIM
KV_DIM = N_KV_HEADS * HEAD_DIM
ATT_IN = Q_DIM + 2 * KV_DIM + 3 * SCONV_DIM
EVEN_SPLITS = (Q_DIM, Q_DIM + KV_DIM, Q_DIM + 2 * KV_DIM, Q_DIM + 2 * KV_DIM + SCONV_DIM, Q_DIM + 2 * KV_DIM + 2 * SCONV_DIM)
MIX_OUT_EVEN = Q_DIM + SCONV_DIM
MIX_IN_ODD = POOL_DIM + FFT_DIM
N_EVEN = (DEPTH + 1) // 2
N_ODD = DEPTH // 2

kernel_name = 'hybrid_swa_sconv_pool_fourier_dit'

def rmsnorm(x, g):
    xf = x.astype(jnp.float32)
    y = xf * lax.rsqrt(jnp.mean(xf * xf, axis=-1, keepdims=True) + EPS)
    return (y * g.astype(jnp.float32)).astype(x.dtype)

def dwconv_centred(u, w):
    k = w.shape[0]
    half = k // 2
    t = u.shape[1]
    up = jnp.pad(u, ((0, 0), (half, k - 1 - half), (0, 0)))
    return sum(up[:, j:j + t] * w[j] for j in range(k))

def _rotate(x, ang):
    f = ang.shape[-1]
    cos = jnp.cos(ang)[:, None, :].astype(x.dtype)
    sin = jnp.sin(ang)[:, None, :].astype(x.dtype)
    x1, x2 = x[..., :f], x[..., f:]
    return jnp.concatenate([x1 * cos - x2 * sin, x2 * cos + x1 * sin], axis=-1)

def rope_2d(x, row, col):
    half = HEAD_DIM // 2
    nf = half // 2
    inv = ROPE_BASE ** (-jnp.arange(nf, dtype=jnp.float32) / nf)
    ang_r = row.astype(jnp.float32)[:, None] * inv
    ang_c = col.astype(jnp.float32)[:, None] * inv
    return jnp.concatenate([_rotate(x[..., :half], ang_r), _rotate(x[..., half:], ang_c)], axis=-1)

def sink_softmax(logits, sink_b):
    m = jnp.maximum(jnp.max(logits, axis=-1, keepdims=True), sink_b)
    e = jnp.exp(logits - m)
    return e / (jnp.sum(e, axis=-1, keepdims=True) + jnp.exp(sink_b - m))

def window_attention(q, k, v, kc, vc, sink):
    b, s = q.shape[:2]
    nb = s // BLOCK
    g = N_Q_HEADS // N_KV_HEADS
    scale = HEAD_DIM ** -0.5
    qb = q.reshape(b, nb, BLOCK, N_KV_HEADS, g, HEAD_DIM)

    def band(t):
        tp = jnp.pad(t, ((0, 0), (BLOCK, BLOCK), (0, 0), (0, 0))).reshape(b, nb + 2, BLOCK, N_KV_HEADS, HEAD_DIM)
        return jnp.concatenate([tp[:, :-2], tp[:, 1:-1], tp[:, 2:]], axis=2)

    kb, vb = band(k), band(v)
    s_win = jnp.einsum('bnqhgd,bnkhd->bnhgqk', qb, kb).astype(jnp.float32) * scale
    qpos = jnp.arange(nb)[:, None] * BLOCK + jnp.arange(BLOCK)[None, :]
    kpos = jnp.arange(nb)[:, None] * BLOCK - BLOCK + jnp.arange(3 * BLOCK)[None, :]
    valid = (jnp.abs(qpos[:, :, None] - kpos[:, None, :]) <= WINDOW) & (kpos[:, None, :] >= 0) & (kpos[:, None, :] < s)
    s_win = jnp.where(valid[None, :, None, None, :, :], s_win, -jnp.inf)
    s_ctx = jnp.einsum('bnqhgd,blhd->bnhgql', qb, kc).astype(jnp.float32) * scale
    sink_b = sink.astype(jnp.float32).reshape(1, 1, N_KV_HEADS, g, 1, 1)
    p = sink_softmax(jnp.concatenate([s_win, s_ctx], axis=-1), sink_b).astype(v.dtype)
    o = (jnp.einsum('bnhgqk,bnkhd->bnqhgd', p[..., :3 * BLOCK], vb)
         + jnp.einsum('bnhgql,blhd->bnqhgd', p[..., 3 * BLOCK:], vc))
    return o.reshape(b, s, Q_DIM)

def context_attention(q, k, v, sink):
    b, l = q.shape[:2]
    g = N_Q_HEADS // N_KV_HEADS
    qg = q.reshape(b, l, N_KV_HEADS, g, HEAD_DIM)
    s = jnp.einsum('blhgd,bmhd->bhglm', qg, k).astype(jnp.float32) * (HEAD_DIM ** -0.5)
    sink_b = sink.astype(jnp.float32).reshape(1, N_KV_HEADS, g, 1, 1)
    p = sink_softmax(s, sink_b).astype(v.dtype)
    o = jnp.einsum('bhglm,bmhd->blhgd', p, v)
    return o.reshape(b, l, Q_DIM)

def even_mixer(hx, hc, w_in, sink, conv_w, w_out, row, col, ctx_out):
    b, s = hx.shape[:2]
    l = hc.shape[1]
    qx, kx, vx, bx, cx, zx = jnp.split(hx @ w_in, EVEN_SPLITS, axis=-1)
    qx = rope_2d(qx.reshape(b, s, N_Q_HEADS, HEAD_DIM), row, col)
    kx = rope_2d(kx.reshape(b, s, N_KV_HEADS, HEAD_DIM), row, col)
    vx = vx.reshape(b, s, N_KV_HEADS, HEAD_DIM)
    if ctx_out:
        qc, kc, vc, bc, cc, zc = jnp.split(hc @ w_in, EVEN_SPLITS, axis=-1)
    else:
        kc, vc = jnp.split(hc @ w_in[:, Q_DIM:Q_DIM + 2 * KV_DIM], 2, axis=-1)
    kc = kc.reshape(b, l, N_KV_HEADS, HEAD_DIM)
    vc = vc.reshape(b, l, N_KV_HEADS, HEAD_DIM)
    ax = window_attention(qx, kx, vx, kc, vc, sink)
    sx = bx * dwconv_centred(cx * zx, conv_w)
    yx = jnp.concatenate([ax, sx], axis=-1) @ w_out
    if not ctx_out:
        return yx, None
    ac = context_attention(qc.reshape(b, l, N_Q_HEADS, HEAD_DIM), kc, vc, sink)
    s_c = bc * dwconv_centred(cc * zc, conv_w)
    yc = jnp.concatenate([ac, s_c], axis=-1) @ w_out
    return yx, yc

def pool_mix(u, w_grp, scale):
    b, t = u.shape[:2]
    uf = u.astype(jnp.float32)
    cs = jnp.pad(jnp.cumsum(uf, axis=1), ((0, 0), (1, 0), (0, 0)))
    pos = jnp.arange(t)
    outs = []
    for gi, w in enumerate(POOL_WINDOWS):
        lo = jnp.clip(pos - w // 2, 0, t)
        hi = jnp.clip(pos + w - w // 2, 0, t)
        sl = slice(gi * POOL_GROUP, (gi + 1) * POOL_GROUP)
        seg = cs[:, :, sl]
        mean = (seg[:, hi] - seg[:, lo]) / (hi - lo).astype(jnp.float32)[:, None]
        outs.append(mean - uf[:, :, sl])
    p = jnp.stack(outs, axis=2).astype(u.dtype)
    y = jnp.einsum('btgc,gcd->btgd', p, w_grp).reshape(b, t, POOL_DIM)
    return y * scale

def fourier_mix(u):
    b, t = u.shape[:2]
    ug = u.astype(jnp.float32).reshape(b, t, N_FFT_GROUPS, FFT_GROUP)
    f = jnp.fft.fftn(ug, axes=(1, 3), norm='ortho').real
    return f.reshape(b, t, FFT_DIM).astype(u.dtype)

def odd_mixer(h, w_in, w_grp, scale, w_out):
    u = h @ w_in
    y = jnp.concatenate([pool_mix(u[..., :POOL_DIM], w_grp, scale), fourier_mix(u[..., POOL_DIM:])], axis=-1)
    return y @ w_out

def conv_ffn(h, w_up, conv_w, w_down):
    gate, val = jnp.split(h @ w_up, 2, axis=-1)
    return (jax.nn.silu(dwconv_centred(gate, conv_w)) * val) @ w_down

def setup_inputs(seed: int = 0) -> dict:
    key = jax.random.key(seed)
    ks = jax.random.split(key, 18)

    def nrm(k, shape, s):
        return jax.random.normal(k, shape, jnp.float32) * s

    return {
        'x': nrm(ks[0], (BATCH, SEQ, D_MODEL), 1.0),
        'c': nrm(ks[1], (BATCH, D_MODEL), 1.0),
        'ctx': nrm(ks[2], (BATCH, CTX_LEN, D_MODEL), 1.0),
        'c_ctx': nrm(ks[3], (D_MODEL,), 1.0),
        'mod_w': nrm(ks[4], (DEPTH, D_MODEL, 6 * D_MODEL), 0.5 * D_MODEL ** -0.5),
        'mod_b': nrm(ks[5], (DEPTH, 6 * D_MODEL), 0.01),
        'norm_g': 1.0 + nrm(ks[6], (DEPTH, 4, D_MODEL), 0.05),
        'att_w_in': nrm(ks[7], (N_EVEN, D_MODEL, ATT_IN), D_MODEL ** -0.5),
        'att_sink': nrm(ks[8], (N_EVEN, N_Q_HEADS), 0.5),
        'sconv_w': nrm(ks[9], (N_EVEN, SCONV_WIDTH, SCONV_DIM), SCONV_WIDTH ** -0.5),
        'att_w_out': nrm(ks[10], (N_EVEN, MIX_OUT_EVEN, D_MODEL), MIX_OUT_EVEN ** -0.5),
        'mix_w_in': nrm(ks[11], (N_ODD, D_MODEL, MIX_IN_ODD), D_MODEL ** -0.5),
        'pool_w_grp': nrm(ks[12], (N_ODD, N_POOL_GROUPS, POOL_GROUP, POOL_GROUP), POOL_GROUP ** -0.5),
        'pool_scale': 1.0 + nrm(ks[13], (N_ODD, POOL_DIM), 0.1),
        'mix_w_out': nrm(ks[14], (N_ODD, MIX_IN_ODD, D_MODEL), MIX_IN_ODD ** -0.5),
        'ffn_w_up': nrm(ks[15], (DEPTH, D_MODEL, 2 * D_FF), D_MODEL ** -0.5),
        'ffn_conv': nrm(ks[16], (DEPTH, FFN_CONV_WIDTH, D_FF), FFN_CONV_WIDTH ** -0.5),
        'ffn_w_down': nrm(ks[17], (DEPTH, D_FF, D_MODEL), D_FF ** -0.5),
    }

def reference(x, c, ctx, c_ctx, mod_w, mod_b, norm_g, att_w_in, att_sink, sconv_w, att_w_out,
              mix_w_in, pool_w_grp, pool_scale, mix_w_out, ffn_w_up, ffn_conv, ffn_w_down):
    s = x.shape[1]
    rows = s // GRID_W
    row = jnp.repeat(jnp.arange(rows), GRID_W)
    col = jnp.tile(jnp.arange(GRID_W), rows)
    silu_c = jax.nn.silu(c)
    silu_cc = jax.nn.silu(c_ctx)
    hctx = ctx
    for i in range(DEPTH):
        even = i % 2 == 0
        ctx_live = any(j % 2 == 0 for j in range(i + 1, DEPTH))
        gains = norm_g[i]
        mod_x = (silu_c @ mod_w[i] + mod_b[i])[:, None, :]
        sh1, sc1, g1, sh2, sc2, g2 = jnp.split(mod_x, 6, axis=-1)
        hx = rmsnorm(x, gains[0]) * (1.0 + sc1) + sh1
        if even or ctx_live:
            mod_c = silu_cc @ mod_w[i] + mod_b[i]
            csh1, csc1, cg1, csh2, csc2, cg2 = jnp.split(mod_c, 6, axis=-1)
            hc = rmsnorm(hctx, gains[0]) * (1.0 + csc1) + csh1
        if even:
            e = i // 2
            yx, yc = even_mixer(hx, hc, att_w_in[e], att_sink[e], sconv_w[e], att_w_out[e], row, col, ctx_live)
        else:
            o = i // 2
            yx = odd_mixer(hx, mix_w_in[o], pool_w_grp[o], pool_scale[o], mix_w_out[o])
            yc = odd_mixer(hc, mix_w_in[o], pool_w_grp[o], pool_scale[o], mix_w_out[o]) if ctx_live else None
        x = x + g1 * rmsnorm(yx, gains[1])
        hx2 = rmsnorm(x, gains[2]) * (1.0 + sc2) + sh2
        x = x + g2 * rmsnorm(conv_ffn(hx2, ffn_w_up[i], ffn_conv[i], ffn_w_down[i]), gains[3])
        if ctx_live:
            hctx = hctx + cg1 * rmsnorm(yc, gains[1])
            hc2 = rmsnorm(hctx, gains[2]) * (1.0 + csc2) + csh2
            hctx = hctx + cg2 * rmsnorm(conv_ffn(hc2, ffn_w_up[i], ffn_conv[i], ffn_w_down[i]), gains[3])
    return x


_drawn_inputs = setup_inputs


def setup_inputs(seed=0):
    import zlib

    import numpy as np

    out = dict(_drawn_inputs(seed))
    spreads = {}
    factors = {'ctx': 11.101, 'mod_b': 2.676, 'att_sink': 64.0, 'pool_scale': 2.689}
    for name, (base, spread) in spreads.items():
        noise = np.random.default_rng([zlib.crc32(name.encode()), seed]).standard_normal(out[name].shape)
        drawn = base * np.exp(spread * noise) if base else spread * noise
        out[name] = __import__('jax').numpy.asarray(drawn.astype(out[name].dtype))
    for name, factor in factors.items():
        out[name] = (out[name] * factor).astype(out[name].dtype)
    return out
```

```python
from contextlib import ExitStack

import numpy as np

import concourse.bass as bass
from concourse import mybir

F32 = mybir.dt.float32
F32R = mybir.dt.float32r
ALU = mybir.AluOpType
ACT = mybir.ActivationFunctionType

P = 128
D = 1024
T = 512
TC = 256
NT = T // P
NTC = TC // P
KT = D // P
DFF = 2816
NJ = DFF // P
NPAIR = NJ // 2
HEADS, KVH, HD = 8, 2, 64
QKV = (HEADS + 2 * KVH) * HD
SCD = 512
EPS = 1e-6
SCALE = HD ** -0.5
MASKED = -1e30
WINDOWS = (2, 4, 8, 16)
GRID_W = 64
RING = 3
HALF = 1024
MC = 1024
KB = 1024

U_L0 = 13
U_FFN = 3 * NPAIR
U_L1 = 11
B_FFN0 = 2 * U_L0
B_L1 = B_FFN0 + 2 * U_FFN
B_FFN1 = B_L1 + 2 * U_L1


def constants():
    t = np.arange(T)
    nf = HD // 4
    inv = (10000.0 ** (-np.arange(nf, dtype=np.float32) / nf)).astype(np.float32)
    ang = [(v.astype(np.float32)[:, None] * inv).astype(np.float32).astype(np.float64) for v in (t // GRID_W, t % GRID_W)]
    cos = np.concatenate([np.concatenate([np.cos(a)] * 2, 1) for a in ang], 1)
    sin = np.concatenate([np.concatenate([-np.sin(a), np.sin(a)], 1) for a in ang], 1)
    q, k = np.arange(P)[:, None], np.arange(P)[None, :]
    before = np.where(k >= q, 0.0, MASKED)
    after = np.where(k <= q, 0.0, MASKED)
    z = np.zeros((P, P))
    mask = np.concatenate([before, z, after, z, z, before, z, z, z], 1)
    a = 2 * np.pi * np.outer(t, t) % (2 * np.pi * T) / T
    norm = 1.0 / np.sqrt(T * P)
    c = np.arange(P)
    b = 2 * np.pi * (np.outer(c, c) % P) / P
    a = 2 * np.pi * (np.outer(t, t) % T) / T
    edge = np.zeros((4, 16))
    for g, w in enumerate(WINDOWS):
        for n, p in enumerate(list(range(8)) + list(range(T - 8, T))):
            edge[g, n] = w / (min(p + w - w // 2, T) - max(p - w // 2, 0))
    f = np.float32
    return {
        "rope_cos": np.tile(cos, (1, 4)).astype(f), "rope_sin": np.tile(sin, (1, 4)).astype(f),
        "attn_mask": mask.astype(f), "identity": np.eye(P, dtype=f),
        "dft_time": (np.concatenate([np.cos(a), -np.sin(a)], 0) * norm).astype(f),
        "dft_chan": np.concatenate([np.cos(b), np.sin(b)], 1).astype(f),
        "pool_edge": edge.astype(f),
    }


class Chain:

    def __init__(self, eng, sem):
        self.eng, self.sem, self.n, self.extra = eng, sem, 0, None

    def link(self, ins):
        ins.then_inc(self.sem, 1)
        self.n += 1
        self.eng.wait_ge(self.sem, self.n if self.extra is None else self.n + self.extra)

    def loop(self, lo, hi, per, body):
        n0 = self.n
        with self.eng.Fori(lo, hi) as i:
            self.extra = (i - lo) * per
            body(i)
            assert self.n - n0 == per, (self.n - n0, per)
        self.extra = None
        self.n = n0 + per * (hi - lo)


def attention_jobs():
    fm = [(kind, jj, a) for jj in range(2) for kind in "czb" for a in range(2)]
    jobs = []
    for n, j in enumerate(fm):
        jobs.append(j)
        if n in (4, 8, 11):
            m = {4: 2, 8: 3, 11: 4}[n]
            jobs += [("m", m, 0), ("m", m, 1)]
    at, out = 0, []
    for j in jobs:
        first = at
        at += 4 if j[0] == "m" else 3 * KT
        out.append((j, first, at))
    return out


JOBS = attention_jobs()
STEPS = 4 * HEADS
PER_STEP = -(-JOBS[-1][2] // STEPS)


def job_end(n):
    return (JOBS[n][2] - 1) // PER_STEP


def mod_start(m):
    return min(job_end(n) for n, (j, _, _) in enumerate(JOBS) if j[:2] == ("m", m)) - 5


def attention_loads():
    split_at = {h: -1 for h in range(9)}
    ends = [job_end(n) + 1 for n, (j, _, _) in enumerate(JOBS) if j[0] != "m"]
    split_at.update({9 + n: s for n, s in enumerate(ends)})
    used_at = [mod_start(m) + k // 2 for m in (2, 3, 4) for k in range(KT)]
    loads = [((split_at.get(2 * u - 3, STEPS + 4), 0, u), ("unit", u)) for u in range(5, 13)]
    loads += [((used_at[n - 2] if n >= 2 else -1, 1, n), ("mod", 2 + n // KT, n % KT)) for n in range(3 * KT)]
    return [what for _, what in sorted(loads)]


def step_of(s):
    return s // 8, (s // 4) % 2, (s // 2) % 2, s % 2


def keys_of(b):
    lo, hi = max(b - 1, 0), min(b + 1, NT - 1)
    return lo, hi - lo + 1


def build(nc, x, c, ctx, c_ctx, mod_w, mod_b, norm_g, att_w_in, att_sink, sconv_w, att_w_out, mix_w_in,
          pool_w_grp, pool_scale, mix_w_out, ffn_w_up, ffn_conv, ffn_w_down, rope_cos, rope_sin,
          attn_mask, identity, dft_time, dft_chan, pool_edge, out):
    ctxs = ExitStack()
    base = -(-nc.sbuf_base // 64) * 64

    def at(name, shape, dt, kb):
        return nc.alloc_sbuf_tensor_at(name, shape, dt, offset=base + int(kb * KB))

    with ctxs:
        hTh = at("hTh", [P, KT, T], F32R, 0)
        hTl = at("hTl", [P, KT, T], F32R, 16)
        wh = at("wh", [P, RING, HALF], F32R, 32)
        wl = at("wl", [P, RING, HALF], F32R, 44)
        mstage = at("mstage", [P, 2, MC], F32, 56)
        macc0 = at("macc0", [P, MC], F32, 64)
        mbias = at("mbias", [P, MC], F32, 68)
        gate = at("gate", [P, D], F32, 72)
        ident = at("ident", [P, P], F32, 76)
        ones = at("ones", [P, P], F32, 76.5)
        junkc = at("junkc", [P, 4, P], F32, 77)
        vecs = at("vecs", [P, P], F32, 77.5)
        vecf = at("vecf", [P, 2, P], F32, 78)
        cols = at("cols", [P, 96], F32, 79)
        convc = at("convc", [P, 2, NJ, 3], F32, 79.375)
        cw = at("cw", [P, 6], F32, 80)
        siluc = at("siluc", [P, 16], F32, 80.0625)
        modc = at("modc", [P, 16, 2], F32, 80.125)
        scl = at("scl", [P, 5, KT], F32, 80.25)
        shf = at("shf", [P, 5, KT], F32, 80.4375)
        mcol = at("mcol", [P, KT], F32, 80.625)
        sink = at("sink", [P, HEADS], F32, 80.6875)
        nsink = at("nsink", [P, HEADS], F32, 80.75)
        stat = at("stat", [P, 8, 24], F32, 80.8125)
        mhalf = at("mhalf", [P, 1], F32, 81.6875)
        edge = at("edge", [P, 4, 16], F32, 81.71875)
        raw = [at("raw0", [P, 2, HALF], F32, 82), at("raw1", [P, 2, HALF], F32, 90), at("raw2", [P, 2, HALF], F32, 98)]
        xs = at("xs", [P, NT, D], F32, 106)
        ys = at("ys", [P, NT, D], F32, 122)
        hf = at("hf", [P, 2, 4, P], F32, 203.5625)
        junk = at("junk", [P, D], F32, 199.53125)
        qT = at("qT", [P, HEADS, T], F32R, 98)
        kH = at("kH", [P, KVH, T + TC], F32R, 114)
        kL = at("kL", [P, KVH, T + TC], F32R, 120)
        vH = at("vH", [P, NT + NTC, 320], F32R, 126)
        vL = at("vL", [P, NT + NTC, 320], F32R, 133.5)
        mask = at("mask", [P, 9 * P], F32, 141)
        aTh = at("aTh", [P, KT, T], F32R, 146)
        aTl = at("aTl", [P, KT, T], F32R, 162)
        prob = at("prob", [P, 3, 640], F32, 178)
        pTh = at("pTh", [P, 5, 2, P], F32R, 185.5)
        pTl = at("pTl", [P, 5, 2, P], F32R, 190.5)
        czb = at("czb", [P, 2, T + 2], F32, 195.5)
        cvt = at("cvt", [P, 2, T], F32, 199.53125)
        att = at("att", [P, STEPS, 4], F32, 145.5)
        xc = at("xc", [P, NTC, D], F32, 98)
        mfirst = at("mfirst", [P, 4, 2 * MC], F32, 146)
        hcTh = at("hcTh", [P, KT, TC], F32R, 146)
        hcTl = at("hcTl", [P, KT, TC], F32R, 154)
        mrow = at("mrow", [2, 2 * MC], F32, 178)
        brow = at("brow", [2, 2 * MC], F32, 186)
        rcos = at("rcos", [P, NT, 256], F32, 56)
        rsin = at("rsin", [P, NT, 256], F32, 60)
        rt = at("rt", [P, 2, 256], F32, 186)
        qd = at("qd", [P, 4, 4, P], F32, 188)
        actH = at("actH", [P, 2, T], F32R, 138)
        actL = at("actL", [P, 2, T], F32R, 142)
        conv = at("conv", [P, 2, T], F32, 146)
        sil = at("sil", [P, 2, T], F32, 150)
        actF = at("actF", [P, 2, T], F32, 154)
        macc = at("macc", [P, 7, MC], F32, 158)
        bTh = at("bTh", [P, KT, T], F32R, 138)
        bTl = at("bTl", [P, KT, T], F32R, 154)
        xcsH = at("xcsH", [P, 8, T], F32R, 170)
        xcsL = at("xcsL", [P, 8, T], F32R, 186)
        xTh = at("xTh", [P, 4, T], F32R, 122)
        xTl = at("xTl", [P, 4, T], F32R, 130)
        pu = at("pu", [P, 3, T + 16], F32, 64)
        gate1 = at("gate1", [P, 2, D], F32, 56)

        ps = ctxs.enter_context(nc.psum_tensor("ps", [P, 8, 512], F32))
        up = [ps[:, b, :] for b in range(4)]
        dn = [ps[:, 4 + b, :] for b in range(4)]

        def sem(name):
            return ctxs.enter_context(nc.semaphore(name))

        s_small = sem("small_loaded")
        s_x = sem("x_loaded")
        s_first = [sem(f"mfirst_loaded{n}") for n in range(4)]
        s_tab = sem("rope_loaded")
        s_raw = [sem(f"raw_loaded{n}") for n in range(3)]
        s_ms = [sem(f"mstage_loaded{n}") for n in range(2)]
        s_mb = sem("mbias_loaded")
        s_gain = sem("gain_row_loaded")
        s_out = sem("out_stored")
        s_init = sem("constants_set")
        s_pc = sem("pool_chain")
        s_vc = sem("vector_chain")
        s_ac = sem("scalar_chain")
        s_hi = sem("half_high")
        s_lo = sem("half_low")
        s_used = sem("half_used")
        s_vt = sem("vectors_transposed")
        s_cols = sem("columns_ready")
        s_silu = sem("silu_c_ready")
        s_mfu = sem("mfirst_used")
        s_mr = sem("mod_rows_summed")
        s_mrb = sem("mod_rows_ready")
        s_mrt = sem("mod_rows_transposed")
        s_scl = sem("scales_ready")
        s_msu = sem("mstage_used")
        s_macc = sem("macc_ready")
        s_msum = sem("macc_summed")
        s_mfin = sem("macc_finished")
        s_sqy = sem("y_squares")
        s_rsy = sem("y_rstd")
        s_xup = sem("x_updated")
        s_sqx = sem("x_squares")
        s_rsx = sem("x_rstd")
        s_xn = sem("x_normed")
        s_tr = sem("norm_transposed")
        s_hf = sem("h_ready")
        s_hh = sem("h_high")
        s_hl = sem("h_low")
        s_row = sem("rows_multiplied")
        s_rowf = sem("rows_taken")
        s_rope = sem("roped")
        s_qt = sem("qk_transposed")
        s_qh = sem("qk_high")
        s_ql = sem("qk_low")
        s_vh = sem("v_high")
        s_vl = sem("v_low")
        s_sc = sem("scores")
        s_max = sem("maxima")
        s_exp = sem("exponentials")
        s_inv = sem("inverse_totals")
        s_pn = sem("probs_normed")
        s_pt = sem("probs_transposed")
        s_ph = sem("probs_high")
        s_pl = sem("probs_low")
        s_pv = sem("pv_used_probs")
        s_ah = sem("attn_high")
        s_al = sem("attn_low")
        s_jobf = sem("job_bank_free")
        s_cz = sem("cz_ready")
        s_cz1 = sem("centre_tap")
        s_cv = sem("sconv_done")
        s_bs = sem("sconv_gated")
        s_sh = sem("sconv_high")
        s_sl = sem("sconv_low")
        s_cw = sem("taps_ready")
        s_g1 = sem("ffn_centre_tap")
        s_gc = sem("ffn_conv_done")
        s_si = sem("ffn_silu")
        s_am = sem("ffn_gated")
        s_ahh = sem("act_high")
        s_all = sem("act_low")
        s_dp = sem("down_piece")
        s_ya = sem("y_added")
        s_xh = sem("l1_fft_high")
        s_xl = sem("l1_fft_low")
        s_u = sem("pool_in_ready")
        s_pw = sem("pool_windowed")
        s_pih = sem("pool_high")
        s_pil = sem("pool_low")
        s_ca = sem("chan_dft")
        s_cah = sem("chan_dft_high")
        s_cal = sem("chan_dft_low")
        s_pg = sem("pool_grouped")
        s_pgs = sem("pool_scaled")
        s_pgh = sem("pool_out_high")
        s_pgl = sem("pool_out_low")
        s_td = sem("time_dft")
        s_tdh = sem("time_dft_high")
        s_tdl = sem("time_dft_low")

        block = ctxs.enter_context(nc.Block())

        def W(eng, s, v):
            if not (isinstance(v, int) and v <= 0):
                eng.wait_ge(s, v)

        def last_of(eng, s, n, count, h, before=0):
            if n < count - 1:
                eng.wait_ge(s, before + n + 1)
            else:
                eng.wait_ge(s_used, h + 1)

        def half_view(t, h, kind):
            v = t[:, h % RING, :]
            if kind == "tm":
                return v.rearrange("p (k n) -> p k n", n=256)
            if kind == "fm":
                return v.rearrange("p (k n) -> p k n", n=P)
            return v

        def raw_view(slot, a, kind):
            if kind == "fm":
                return raw[slot].rearrange("p a (k n) -> p (a k) n", n=256)[:, :, a * P:(a + 1) * P]
            if kind == "chan":
                return raw[slot][:, a, 0:256]
            if kind == "grp":
                return raw[slot][:, a, 0:512]
            return raw[slot][:, a, :]

        def ring_view(t, h, kind):
            v = t[:, h % RING, :]
            if kind == "fm":
                return v.rearrange("p (k n) -> p k n", n=P)
            if kind == "chan":
                return v[:, 0:256]
            if kind == "grp":
                return v[:, 0:512]
            return v

        def split_high(act, h, slot, a, kind, loads, dh=0):
            act.wait_ge(s_raw[slot], loads)
            W(act, s_used, h - 2 + dh)
            nc.scalar.activation(ring_view(wh, h, kind), raw_view(slot, a, kind), ACT.Copy).then_inc(s_hi, 1)

        def split_low(dve, h, slot, a, kind, dh=0):
            dve.wait_ge(s_hi, h + 1 + dh)
            nc.vector.tensor_sub(ring_view(wl, h, kind), raw_view(slot, a, kind), ring_view(wh, h, kind).bitcast(F32)).then_inc(s_lo, 1)

        plan = {}
        uses = [0, 0, 0]

        def unit(u2, slot, kinds):
            uses[slot] += 1
            for a in range(2):
                plan[u2 + a] = (slot, a, kinds[a], 32 * uses[slot])

        for u in range(U_L0):
            unit(2 * u, u % 2, ("tm", "tm") if u < 3 or u >= 9 else ("fm", "fm"))
        ffn_uses = []
        ffn_uses.append(list(uses))
        uses[:] = [n + NPAIR for n in uses]
        for u in range(U_L1):
            unit(B_L1 + 2 * u, (0, 2, 1)[u % 3], ("fm", "fm") if u < 4 else (("chan", "grp") if u == 4 else ("tm", "tm")))
        ffn_uses.append(list(uses))

        half_of = {n: 6 + f for f, n in enumerate(n for n, (j, _, _) in enumerate(JOBS) if j[0] != "m")}
        ffn_jobs = {"g0": (0, 1, 2), "d": (3, 4), "v0": (5, 6, 7), "g1": (8, 9, 10), "v1": (11, 12, 13)}
        rows_before = {1: 11, 3: 23}

        GS, DS, VS = 0, 1, 2

        def ffn_half(layer, i, what):
            hb = (B_FFN0, B_FFN1)[layer]
            k = {"g0": -2, "v0": 1, "g1": 2, "v1": 3, "d0": 5, "d1": 6}[what]
            if not isinstance(i, int):
                return hb + k, i * 6
            if i == 0 and what in ("g0", "v0"):
                k += 2 if what == "g0" else 0
            if i == NPAIR - 1 and what[0] == "d":
                k -= 1
            return hb + k + 6 * i, 0

        def ffn_split(eng, fn, layer, i, what):
            slot = {"g": GS, "d": DS, "v": VS}[what[0]]
            h, dh = ffn_half(layer, i, what)
            kind = "dn" if what[0] == "d" else "fm"
            loads = (i + (ffn_uses[layer][slot] + 1)) * 32
            if fn == "high":
                split_high(eng, h, slot, int(what[1]), kind, loads, dh)
            else:
                split_low(eng, h, slot, int(what[1]), kind, dh)

        def straight_high(act, h):
            if h in plan:
                slot, a, kind, loads = plan[h]
                split_high(act, h, slot, a, kind, loads)
            else:
                layer, idx = (0, h - B_FFN0) if h < B_L1 else (1, h - B_FFN1)
                ffn_split(act, "high", layer, 0, ("g0", "v0", "g1", "v1")[idx])

        def straight_low(dve, h):
            if h in plan:
                slot, a, kind, _ = plan[h]
                split_low(dve, h, slot, a, kind)
            else:
                layer, idx = (0, h - B_FFN0) if h < B_L1 else (1, h - B_FFN1)
                ffn_split(dve, "low", layer, 0, ("g0", "v0", "g1", "v1")[idx])

        def norm_index(e, t):
            return t if e == 0 else 6 + 4 * (e - 1) + t

        def norm_cols(n):
            return (4 if 4 <= n < 6 else 0) if n < 6 else 1 + (n - 6) // 4

        def norm_src(n):
            return xs[:, n, :] if n < 4 else (xc[:, n - 4, :] if n < 6 else ys[:, (n - 6) % 4, :])

        def norm_dst(t, n):
            if 4 <= n < 6:
                return (hcTh, hcTl)[t][:, :, (n - 4) * P:(n - 3) * P]
            tt = n if n < 4 else (n - 6) % 4
            return (hTh, hTl)[t][:, :, tt * P:(tt + 1) * P]

        @block.sync
        def _(sp):
            def load_unit(slot, halves):
                for dst, src in halves:
                    sp.dma_start(dst, src).then_inc(s_raw[slot], 16)

            def cols_unit(slot, w, c0, order=(0, 1)):
                v = w[:, c0:c0 + 256].rearrange("(k p) n -> p k n", p=P)
                load_unit(slot, [(raw[slot][:, a, :].rearrange("p (k n) -> p k n", n=256), v[:, 4 * g:4 * g + 4, :])
                                 for a, g in enumerate(order)])

            w_in, w_out = att_w_in[0], att_w_out[0]

            def first(k):
                if k >= 4:
                    sp.wait_ge(s_mfu, k - 3)
                sp.dma_start(mfirst[:, k % 4, :], mod_w[0, k * P:(k + 1) * P, 0:2 * MC]).then_inc(s_first[k % 4], 16)

            first(0)
            for t in range(NT):
                sp.dma_start(xs[:, t, :], x[0, t * P:(t + 1) * P, :]).then_inc(s_x, 16)
                if t % 2:
                    first(1 + t // 2)
            for t in range(NTC):
                sp.dma_start(xc[:, t, :], ctx[0, t * P:(t + 1) * P, :]).then_inc(s_x, 16)
            for k in range(3, 8):
                first(k)
            cols_unit(0, w_in, 0)
            sp.dma_start(rcos[:, :, :], rope_cos.rearrange("(t p) n -> p t n", p=P)).then_inc(s_tab, 16)
            sp.dma_start(rsin[:, :, :], rope_sin.rearrange("(t p) n -> p t n", p=P)).then_inc(s_tab, 16)
            cols_unit(1, w_in, 256)

            nm = [0]

            def mod_tile(src, acc_wait=True):
                n = nm[0]
                if n >= 2:
                    sp.wait_ge(s_msu, n - 1)
                sp.dma_start(mstage[:, n % 2, :], src).then_inc(s_ms[n % 2], 16)
                nm[0] += 1

            def mod_chunk_tile(l, m, k):
                if k == 0:
                    c_n = {(0, 2): 0, (0, 3): 1, (0, 4): 2, (0, 5): 3}[(l, m)]
                    if c_n:
                        sp.wait_ge(s_msu, 8 * (c_n - 1) + 1)
                    sp.dma_start(mbias[0:1, :], mod_b[l:l + 1, m * MC:(m + 1) * MC]).then_inc(s_mb, 16)
                mod_tile(mod_w[l, k * P:(k + 1) * P, m * MC:(m + 1) * MC])

            s0 = QKV
            col = {"b": s0, "c": s0 + SCD, "z": s0 + 2 * SCD}
            order = [("unit", 2), ("unit", 3), ("unit", 4), ("tables",)] + attention_loads()
            for what in order:
                if what[0] == "mod":
                    mod_chunk_tile(0, what[1], what[2])
                elif what[0] == "tables":
                    sp.wait_ge(s_rope, 14)
                    sp.wait_ge(s_init, 5)
                else:
                    u = what[1]
                    sp.wait_ge(s_lo, 2 * (u - 2) + 2)
                    if u == 2:
                        cols_unit(0, w_in, 512)
                    elif u < 9:
                        jj, kind = divmod(u - 3, 3)
                        cols_unit(u % 2, w_in, col["czb"[kind]] + 256 * jj)
                    else:
                        cols_unit(u % 2, w_out, 256 * (u - 9), order=(1, 0))
            sp.wait_ge(s_pv, STEPS // 2)
            for t in range(NT):
                sp.dma_start(xs[:, t, :], x[0, t * P:(t + 1) * P, :]).then_inc(s_x, 16)

            def ffn_loads(layer):
                hb = (B_FFN0, B_FFN1)[layer]
                wu = ffn_w_up[layer].rearrange("(k p) n -> p k n", p=P)
                wd = ffn_w_down[layer].rearrange("(j p) n -> p j n", p=P)

                def g_or_v(i, slot, off):
                    for a in range(2):
                        src = wu[:, 4 * a:4 * a + 4, bass.ds(i * 256 + off, 256)]
                        sp.dma_start(raw[slot][:, a, :].rearrange("p (k n) -> p k n", n=256), src).then_inc(s_raw[slot], 16)

                def dn_(i):
                    for a in range(2):
                        src = wd[:, bass.ds(i * 2 + a, 1), :].rearrange("p j n -> p (j n)")
                        sp.dma_start(raw[DS][:, a, :], src).then_inc(s_raw[DS], 16)

                def turn(i, mod=False):
                    if isinstance(i, int) and i == 0:
                        sp.wait_ge(s_lo, hb if layer == 0 else hb - 2)
                        g_or_v(0, GS, 0)
                        sp.wait_ge(s_lo, hb)
                        g_or_v(0, VS, DFF)
                        return
                    first_turn = isinstance(i, int) and i == 1
                    sp.wait_ge(s_lo, hb + 3 if first_turn else hb + 6 * i - 2 - 1)
                    g_or_v(i, GS, 0)
                    if not first_turn:
                        sp.wait_ge(s_lo, hb + 6 * i - 5 + 0)
                    dn_(i - 1)
                    sp.wait_ge(s_lo, hb + 6 * i - 2)
                    g_or_v(i, VS, DFF)

                def mod_tiles(m, lo, hi):
                    for k in range(lo, hi):
                        sp.wait_ge(s_msu, m * KT + (4 * KT + k - 1))
                        cols = bass.ds(m * MC, MC) if not isinstance(m, int) else slice(m * MC, (m + 1) * MC)
                        sp.dma_start(mstage[:, k % 2, :], mod_w[1, k * P:(k + 1) * P, cols]).then_inc(s_ms[k % 2], 16)

                def mod_bias(m):
                    sp.wait_ge(s_msu, m * KT + (3 * KT + 1))
                    cols = bass.ds(m * MC, MC) if not isinstance(m, int) else slice(m * MC, (m + 1) * MC)
                    sp.dma_start(mbias[0:1, :], mod_b[1:2, cols]).then_inc(s_mb, 16)

                turn(0)
                turn(1)
                if layer == 0:
                    for k in range(6):
                        mod_chunk_tile(0, 5, k)
                turn(2)
                if layer == 0:
                    for k in (6, 7):
                        mod_chunk_tile(0, 5, k)
                    mod_bias(0)
                    mod_tiles(0, 0, 6)
                    with sp.Fori(3, 8) as i:
                        turn(i)
                        mod_tiles(i - 3, 6, KT)
                        mod_bias(i - 2)
                        mod_tiles(i - 2, 0, 6)
                    turn(8)
                    mod_tiles(5, 6, KT)
                    turn(9)
                    sp.wait_ge(s_xup, 4)
                    sp.dma_start(gate[:, :], norm_g[0, 3:4, :].broadcast_to([P, D])).then_inc(s_gain, 16)
                    sp.wait_ge(s_msu, 10 * KT)
                    for n, g in enumerate((1, 3)):
                        sp.dma_start(gate1[:, n, :], norm_g[1, g:g + 1, :].broadcast_to([P, D])).then_inc(s_gain, 16)
                else:
                    with sp.Fori(3, NPAIR - 1) as i:
                        turn(i)
                turn(NPAIR - 1)
                sp.wait_ge(s_lo, hb + 6 * NPAIR - 5)
                dn_(NPAIR - 1)

            ffn_loads(0)
            for u in range(U_L1):
                free = (B_L1 - 3, B_L1 - 2, B_L1)[u] if u < 3 else B_L1 + 2 * (u - 3) + 2
                sp.wait_ge(s_lo, free)
                slot = plan[B_L1 + 2 * u][0]
                if u < 4:
                    cols_unit(slot, mix_w_in[0], (SCD, SCD + 256, 0, 256)[u])
                elif u == 4:
                    load_unit(slot, [(raw[slot][:, 0, 0:256], dft_chan),
                                     (raw[slot][:, 1, 0:512].rearrange("p (g n) -> p g n", g=4),
                                      pool_w_grp[0].rearrange("g c n -> c g n"))])
                elif u < 7:
                    cols_unit(slot, dft_time, 256 * (u - 5))
                else:
                    cols_unit(slot, mix_w_out[0], 256 * (u - 7))
            ffn_loads(1)
            for t in range(NT):
                sp.wait_ge(s_xup, 4 * 3 + t + 1)
                sp.dma_start(out[0, t * P:(t + 1) * P, :], xs[:, t, :]).then_inc(s_out, 16)
            sp.wait_ge(s_out, 16 * NT)

        @block.gpsimd
        def _(pool):
            nc.gpsimd.memset(ones[:, :], 1.0).then_inc(s_init, 1)
            nc.gpsimd.memset(mbias[:, :], 0.0).then_inc(s_init, 1)
            nc.gpsimd.memset(mhalf[:, :], -0.5).then_inc(s_init, 1)
            nc.gpsimd.memset(vH[:, :, :].bitcast(F32), 0.0).then_inc(s_init, 1)
            nc.gpsimd.memset(vL[:, :, :].bitcast(F32), 0.0).then_inc(s_init, 1)
            pool.wait_ge(s_init, 5)
            ch = Chain(pool, s_pc)

            def rstd(row, q, done):
                ch.link(nc.gpsimd.tensor_scalar(stat[:, row + 1, q:q + 1], stat[:, row, q:q + 1], 1.0 / D, EPS, ALU.mult, ALU.add))
                nc.gpsimd.tensor_tensor(stat[:, row + 2, q:q + 1], stat[:, row + 1, q:q + 1], mhalf[:, :], ALU.pow).then_inc(done, 1)

            def rstd_x(n):
                pool.wait_ge(s_sqx, n + 1)
                rstd(3, n, s_rsx)

            def h_high(n, b):
                pool.wait_ge(s_hf, 2 * n + b + 1)
                nc.gpsimd.tensor_scalar(norm_dst(0, n)[:, 4 * b:4 * b + 4, :], hf[:, b, :, :], 1.0, 0.0, ALU.mult, ALU.add).then_inc(s_hh, 1)

            for n in range(6):
                rstd_x(n)
            for n in range(6):
                for b in range(2):
                    h_high(n, b)
            for s in range(STEPS):
                nk = (keys_of(step_of(s)[0])[1] + 2) * P
                pool.wait_ge(s_inv, s + 1)
                nc.gpsimd.tensor_scalar(prob[:, s % 3, 0:nk], prob[:, s % 3, 0:nk], att[:, s, 3:4], None, ALU.mult).then_inc(s_pn, 1)
            for e in range(1, 5):
                for t in range(NT + 2):
                    if t < NT:
                        pool.wait_ge(s_sqy, 4 * (e - 1) + t + 1)
                        rstd(0, 4 * (e - 1) + t, s_rsy)
                    if 1 <= t <= NT and e < 4:
                        rstd_x(norm_index(e, t - 1))
                    if t >= 2 and e < 4:
                        for b in range(2):
                            h_high(norm_index(e, t - 2), b)

        @block.scalar
        def _(act):
            small = [
                (ident[:, :], identity),
                (vecs[0:8, :], c.rearrange("b (r p) -> (b r) p", p=P)),
                (vecs[8:16, :], c_ctx.rearrange("(r p) -> r p", p=P)),
                (vecs[16:80, :], norm_g.rearrange("l g (r p) -> (l g r) p", p=P)),
                (vecs[80:92, :], sconv_w.rearrange("o w (r p) -> (o w r) p", p=P)),
                (vecs[92:96, :], pool_scale.rearrange("o (r p) -> (o r) p", p=P)),
                (vecf[0:3 * NJ, 0, :], ffn_conv[0].rearrange("w (r p) -> (w r) p", p=P)),
                (vecf[0:3 * NJ, 1, :], ffn_conv[1].rearrange("w (r p) -> (w r) p", p=P)),
                (brow[:, :], mod_b[0:1, 0:2 * MC].broadcast_to([2, 2 * MC])),
                (sink[:, :], att_sink[0:1, :].broadcast_to([P, HEADS])),
                (edge[:, :, :], pool_edge.unsqueeze(0).broadcast_to([P, 4, 16])),
                (mask[:, :], attn_mask),
                (gate[:, :], norm_g[0, 1:2, :].broadcast_to([P, D])),
            ]
            for dst, src in small:
                act.dma_start(dst, src).then_inc(s_small, 16)
            ch = Chain(act, s_ac)

            written = {"junk": None}

            def square(dst, src, done, count):
                if written["junk"]:
                    act.wait_ge(*written["junk"])
                nc.scalar.activation(junk[:, :], src, ACT.Square, accum_out=dst).then_inc(done, 1)
                written["junk"] = (done, count)

            def h_tile(n):
                e = norm_cols(n)
                for b in range(2):
                    act.wait_ge(s_tr, 2 * n + b + 1)
                    W(act, s_hl, 2 * n + b - 1)
                    bank = up[2 * (n % 2) + b].rearrange("p (k n) -> p k n", n=P)
                    for k in range(4):
                        ins = nc.scalar.activation(hf[:, b, k, :], bank[:, k, :], ACT.Identity,
                                                   scale=scl[:, e, 4 * b + k:4 * b + k + 1], bias=shf[:, e, 4 * b + k:4 * b + k + 1])
                    ins.then_inc(s_hf, 1)

            act.wait_ge(s_vt, 1)
            nc.scalar.activation(siluc[:, :], up[0][:, 0:16], ACT.Silu).then_inc(s_silu, 1)
            for n in range(6):
                act.wait_ge(s_x, 96)
                square(stat[:, 3, n:n + 1], norm_src(n), s_sqx, n + 1)
            for h in range(3):
                if h < 2:
                    straight_high(act, h)
            act.wait_ge(s_scl, 2)
            for n in range(6):
                h_tile(n)
            straight_high(act, 2)

            def qk_high(n):
                act.wait_ge(s_qt, n + 1)
                if n < 8:
                    u, t = divmod(n, 4)
                    dst = qT[:, 4 * u:4 * u + 4, t * P:(t + 1) * P]
                    src = up[n % 2].rearrange("p (h n) -> p h n", n=P)
                else:
                    dst = kH[:, :, (n - 8) * P:(n - 7) * P]
                    src = up[n % 2][:, 0:2 * P].rearrange("p (h n) -> p h n", n=P)
                nc.scalar.activation(dst, src, ACT.Copy).then_inc(s_qh, 1)

            def v_high(t):
                last_of(act, s_row, t, 6, 5, 6)
                act.wait_ge(s_init, 5)
                bank = dn[t] if t < 4 else up[t - 2]
                dst = vH[:, t, 64:320].rearrange("p (h n) -> p h n", n=P)[:, :, 0:HD]
                nc.scalar.activation(dst, bank[:, P:2 * P].rearrange("p (h n) -> p h n", n=HD), ACT.Copy).then_inc(s_vh, 1)

            straight_high(act, 3)
            straight_high(act, 4)
            for n in range(4):
                qk_high(n)
            straight_high(act, 5)
            straight_high(act, 6)
            for n in range(4, 8):
                qk_high(n)
            straight_high(act, 7)
            for t in range(6):
                v_high(t)
            straight_high(act, 8)
            for n in range(8, 14):
                qk_high(n)

            nsh = [0]
            for s in range(STEPS + 4):
                if s < STEPS:
                    b, kv, e, w = step_of(s)
                    head = 4 * kv + e + 2 * w
                    nk = (keys_of(b)[1] + 2) * P
                    act.wait_ge(s_max, s + 1)
                    nc.scalar.activation(prob[:, s % 3, 0:nk], prob[:, s % 3, 0:nk], ACT.Exp, bias=att[:, s, 1:2],
                                         scale=SCALE, accum_out=att[:, s, 2:3])
                    nc.scalar.activation(att[:, s, 3:4], sink[:, head:head + 1], ACT.Exp, bias=att[:, s, 1:2]).then_inc(s_exp, 1)
                for n, (job, _, _) in enumerate(JOBS):
                    if job_end(n) == s and job[0] != "m":
                        kind, jj, a = job
                        if kind == "c":
                            act.wait_ge(s_used, half_of[n] + 1)
                            W(act, s_cv, 2 * (jj - 1) + a + 1)
                            nc.scalar.activation(czb[:, a, 1:T + 1], up[3], ACT.Copy).then_inc(s_jobf, 1)
                        elif kind == "z":
                            act.wait_ge(s_cz, 2 * jj + a + 1)
                            W(act, s_sl, 2 * (jj - 1) + a + 1)
                            f = 80 + 4 + 2 * jj + a
                            nc.scalar.activation(cvt[:, a, :], czb[:, a, 1:T + 1], ACT.Copy, scale=cols[:, f:f + 1]).then_inc(s_cz1, 1)
                        else:
                            act.wait_ge(s_bs, 2 * jj + a + 1)
                            nc.scalar.activation(aTh[:, 4 + 2 * jj + a, :], cvt[:, a, :], ACT.Copy).then_inc(s_sh, 1)
                if 2 <= s < STEPS + 2:
                    r = s - 2
                    nb = keys_of(step_of(r)[0])[1] + 2
                    act.wait_ge(s_pt, r + 1)
                    W(act, s_pv, r // 2)
                    src = ps[:, 0:2, :].rearrange("p b n -> p (b n)")[:, 0:nb * P].rearrange("p (j n) -> p j n", n=P)
                    nc.scalar.activation(pTh[:, 0:nb, r % 2, :], src, ACT.Copy).then_inc(s_ph, 1)
                if s >= 7 and (s - 7) % 4 == 0:
                    o = (s - 7) // 4
                    act.wait_ge(s_pv, 2 * o + 2)
                    b, kv = divmod(o, 2)
                    nc.scalar.activation(aTh[:, 2 * kv:2 * kv + 2, b * P:(b + 1) * P],
                                         up[2][:, 0:2 * P].rearrange("p (w n) -> p w n", n=P), ACT.Copy).then_inc(s_ah, 1)
                for n, (job, _, _) in enumerate(JOBS):
                    if job_end(n) == s - 1 and job[0] != "m":
                        nsh[0] += 1
                        straight_high(act, 6 + nsh[0] + 2)

            def transition(e, splits):
                for t in range(NT + 2):
                    if t < NT:
                        q = 4 * (e - 1) + t
                        y_wait(act, e, t)
                        square(stat[:, 0, q:q + 1], ys[:, t, :], s_sqy, q + 1)
                    if t == NT - 1:
                        for h in splits:
                            straight_high(act, h)
                    if 1 <= t <= NT and e < 4:
                        act.wait_ge(s_xup, 4 * (e - 1) + t)
                        n = norm_index(e, t - 1)
                        square(stat[:, 3, n:n + 1], xs[:, t - 1, :], s_sqx, n + 1)
                    if t >= 2 and e < 4:
                        h_tile(norm_index(e, t - 2))

            def ffn(layer):
                hb = (B_FFN0, B_FFN1)[layer]

                def centre(i, jj):
                    h, dh = ffn_half(layer, i, ("g0", "g1")[jj])
                    act.wait_ge(s_used, h + 1 + dh)
                    act.wait_ge(s_cw, NPAIR * layer + i + 1)
                    W(act, s_si, 2 * NPAIR * layer + 2 * i + jj - 1)
                    nc.scalar.activation(conv[:, jj, :], up[jj], ACT.Copy, scale=cw[:, 3 * jj + 1:3 * jj + 2]).then_inc(s_g1, 1)

                def silu(i, jj):
                    act.wait_ge(s_gc, 2 * NPAIR * layer + 2 * i + jj + 1)
                    W(act, s_am, 2 * NPAIR * layer + 2 * i + jj - 1)
                    nc.scalar.activation(sil[:, jj, :], conv[:, jj, :], ACT.Silu).then_inc(s_si, 1)

                def act_high(i, jj):
                    act.wait_ge(s_am, 2 * NPAIR * layer + 2 * i + jj + 1)
                    if not (isinstance(i, int) and i == 0):
                        act.wait_ge(s_used, hb + 6 * i + 1)
                    nc.scalar.activation(actH[:, jj, :], actF[:, jj, :], ACT.Copy).then_inc(s_ahh, 1)

                def turn(i, last=False):
                    zero = isinstance(i, int) and i == 0
                    if not zero:
                        ffn_split(act, "high", layer, i - 1, "d1")
                        act_high(i - 1, 1)
                        ffn_split(act, "high", layer, i, "v0")
                    centre(i, 0)
                    silu(i, 0)
                    if not zero:
                        ffn_split(act, "high", layer, i, "g1")
                    ffn_split(act, "high", layer, i, "v1")
                    act_high(i, 0)
                    if not last:
                        ffn_split(act, "high", layer, i + 1, "g0")
                    centre(i, 1)
                    silu(i, 1)
                    ffn_split(act, "high", layer, i, "d0")

                turn(0)
                with act.Fori(1, NPAIR - 1) as i:
                    turn(i)
                turn(NPAIR - 1, last=True)
                ffn_split(act, "high", layer, NPAIR - 1, "d1")
                act_high(NPAIR - 1, 1)

            def y_wait(eng, e, t):
                if e in (1, 3):
                    eng.wait_ge(s_rowf, 16 * (e // 2) + 3 * NT + t + 1)
                else:
                    eng.wait_ge(s_ya, 8 * NPAIR * (e // 2) - 8 + 2 * t + 2)

            for h in range(2 * 9 + 3, B_FFN0 + 2):
                straight_high(act, h)
            transition(1, [B_FFN0 + 2])
            ffn(0)
            straight_high(act, B_L1)
            transition(2, [B_L1 + 1, B_L1 + 2])
            for n in range(4):
                act.wait_ge(s_used, B_L1 + n + 1)
                nc.scalar.activation(xTh[:, n, :], up[n], ACT.Copy).then_inc(s_xh, 1)
                straight_high(act, B_L1 + 3 + n)
            for g in range(4):
                act.wait_ge(s_used, B_L1 + 4 + g + 1)
                act.wait_ge(s_init, 7)
                W(act, s_pw, g)
                nc.scalar.activation(pu[:, 0, 8:T + 8], up[g], ACT.Copy).then_inc(s_u, 1)
                straight_high(act, B_L1 + 7 + g)
                act.wait_ge(s_pw, g + 1)
                nc.scalar.activation(bTh[:, g, :], pu[:, 2 if g % 2 == 0 else 1, 0:T], ACT.Copy).then_inc(s_pih, 1)
            for n in range(16):
                tt, g = divmod(n, 4)
                last_of(act, s_ca, n, 16, B_L1 + 8)
                dst = xcsH[:, :, g * P:(g + 1) * P].rearrange("p (s t) n -> p s t n", s=2)[:, :, tt, :]
                nc.scalar.activation(dst, dn[n % 4][:, 0:256].rearrange("p (s n) -> p s n", n=P), ACT.Copy).then_inc(s_cah, 1)
            straight_high(act, B_L1 + 11)
            for g in range(4):
                last_of(act, s_pg, g, 4, B_L1 + 9)
                W(act, s_pgl, g - 1)
                ch.link(nc.scalar.activation(hf[:, g % 2, :, :].rearrange("p k n -> p (k n)"), up[g], ACT.Copy, scale=cols[:, 92 + g:93 + g]))
                nc.scalar.activation(bTh[:, g, :], hf[:, g % 2, :, :].rearrange("p k n -> p (k n)"), ACT.Copy).then_inc(s_pgh, 1)
            straight_high(act, B_L1 + 12)
            for ck in range(2):
                straight_high(act, B_L1 + 13 + 2 * ck)
                for g in range(4):
                    last_of(act, s_td, g, 4, B_L1 + 11 + 2 * ck, 3 * ck)
                    nc.scalar.activation(bTh[:, 4 + g, ck * 256:(ck + 1) * 256], dn[g][:, 0:256], ACT.Copy).then_inc(s_tdh, 1)
                straight_high(act, B_L1 + 14 + 2 * ck)
            for h in range(B_L1 + 17, B_FFN1 + 2):
                straight_high(act, h)
            transition(3, [B_FFN1 + 2])
            ffn(1)
            transition(4, [])


        @block.vector
        def _(dve):
            ch = Chain(dve, s_vc)

            dve.wait_ge(s_small, 16 * 13)
            dve.wait_ge(s_vt, 3)
            dve.wait_ge(s_silu, 1)
            ch.link(nc.vector.tensor_copy(cols[:, :], up[0][:, 0:96]))
            for l in range(2):
                nc.vector.tensor_copy(convc[:, l, :, :].rearrange("p j w -> p w j"),
                                      up[1 + l][:, 0:3 * NJ].rearrange("p (w j) -> p w j", w=3)).then_inc(s_cols, 1)
            nc.vector.tensor_scalar(nsink[:, :], sink[:, :], -1.0, None, ALU.mult).then_inc(s_cols, 1)

            def xn(n, dst, src):
                dve.wait_ge(s_rsx, n + 1)
                nc.vector.tensor_scalar(dst, src, stat[:, 5, n:n + 1], None, ALU.mult).then_inc(s_xn, 1)

            def h_low(n):
                for b in range(2):
                    dve.wait_ge(s_hh, 2 * n + b + 1)
                    nc.vector.tensor_sub(norm_dst(1, n)[:, 4 * b:4 * b + 4, :], hf[:, b, :, :],
                                         norm_dst(0, n)[:, 4 * b:4 * b + 4, :].bitcast(F32)).then_inc(s_hl, 1)

            for n in range(6):
                xn(n, norm_src(n), norm_src(n))
            straight_low(dve, 0)
            straight_low(dve, 1)
            dve.wait_ge(s_mr, 1)
            for n in range(4):
                ins = nc.vector.tensor_tensor(mrow[:, n * 512:(n + 1) * 512], dn[n][0:2, :], brow[:, n * 512:(n + 1) * 512], ALU.add)
            ins.then_inc(s_mrb, 1)
            dve.wait_ge(s_mrt, 1)
            ch.link(nc.vector.tensor_copy(modc[:, :, :], dn[0][:, 0:32].rearrange("p (k v) -> p k v", v=2)))
            for v in range(2):
                nc.vector.tensor_copy(shf[:, 4 * v, :], modc[:, 0:KT, v])
                nc.vector.scalar_tensor_tensor(out=scl[:, 4 * v, :], in0=modc[:, KT:2 * KT, v], scalar=1.0, in1=cols[:, 16:24],
                                               op0=ALU.add, op1=ALU.mult).then_inc(s_scl, 1)
            for n in range(6):
                h_low(n)
            straight_low(dve, 2)

            rp = lambda ap: ap.rearrange("p (h r f) -> p h r f", r=2, f=16)

            def rope(n, bank, t, width):
                W(dve, s_qt, n - 3)
                W(dve, s_rope, n)
                nh = width // HD
                src = rp(bank[:, 0:width])
                cs, sn = rp(rcos[:, t, 0:width]), rp(rsin[:, t, 0:width])
                nc.vector.tensor_tensor(rt[:, 0, 0:width], bank[:, 0:width], rcos[:, t, 0:width], ALU.mult)
                for r in range(2):
                    ins = nc.vector.tensor_tensor(rp(rt[:, 1, 0:width])[:, :, r, :], src[:, :, 1 - r, :], sn[:, :, r, :], ALU.mult)
                return ins, nh

            def rope_add(n, nh):
                wide = lambda a: rt[:, a, 0:nh * HD].rearrange("p (h o d) -> p h o d", o=1, d=HD).broadcast_to([P, nh, 2, HD])
                nc.vector.tensor_tensor(qd[:, n % 4, 0:nh, :].rearrange("p h (o d) -> p h o d", o=2), wide(0), wide(1), ALU.add).then_inc(s_rope, 1)

            def rope_q(n):
                u, t = divmod(n, 4)
                last_of(dve, s_row, t, 4, 2 * u + 1, 3 * u)
                ins, nh = rope(n, dn[t], t, 256)
                ch.link(ins)
                rope_add(n, nh)

            def qk_low(n):
                dve.wait_ge(s_qh, n + 1)
                if n < 8:
                    u, t = divmod(n, 4)
                    dst = qT[64:P, 4 * u:4 * u + 4, t * P:(t + 1) * P]
                    nc.vector.tensor_sub(dst, up[n % 2][64:P, :].rearrange("p (h n) -> p h n", n=P), dst.bitcast(F32)).then_inc(s_ql, 1)
                else:
                    c0 = (n - 8) * P
                    nc.vector.tensor_sub(kL[:, :, c0:c0 + P], up[n % 2][:, 0:2 * P].rearrange("p (h n) -> p h n", n=P),
                                         kH[:, :, c0:c0 + P].bitcast(F32)).then_inc(s_ql, 1)

            dve.wait_ge(s_tab, 32)
            for n in range(4):
                rope_q(n)
            straight_low(dve, 3)
            straight_low(dve, 4)
            for n in range(4):
                qk_low(n)
            straight_low(dve, 5)
            for n in range(4, 8):
                rope_q(n)
            straight_low(dve, 6)
            for n in range(4, 8):
                qk_low(n)
            for t in range(6):
                n = 8 + t
                bank = dn[t] if t < 4 else up[t - 2]
                dve.wait_ge(s_vh, t + 1)
                if t < 4:
                    ins, nh = rope(n, bank, t, P)
                    ch.link(ins)
                    rope_add(n, nh)
                else:
                    W(dve, s_qt, n - 3)
                    nc.vector.tensor_copy(qd[:, n % 4, 0:2, :].rearrange("p h (o d) -> p h o d", o=2),
                                          bank[:, 0:P].rearrange("p (h o d) -> p h o d", o=1, d=HD).broadcast_to([P, 2, 2, HD])).then_inc(s_rope, 1)
                vv = lambda z: z[:, t, 64:320].rearrange("p (h n) -> p h n", n=P)[:, :, 0:HD]
                nc.vector.tensor_sub(vv(vL), bank[:, P:2 * P].rearrange("p (h n) -> p h n", n=HD), vv(vH).bitcast(F32)).then_inc(s_vl, 1)
                if t:
                    qk_low(n - 1)
            qk_low(13)
            straight_low(dve, 7)
            straight_low(dve, 8)
            nc.vector.memset(czb[:, :, 0:1], 0.0)
            ch.link(nc.vector.memset(czb[:, :, T + 1:T + 2], 0.0))

            nm = [0]

            def mod_step(acc, k, n, turns=0):
                dve.wait_ge(s_ms[n % 2], turns * (16 * KT // 2) + 16 * (n // 2 + 1))
                if k == 0:
                    dve.wait_ge(s_mb, turns * 16 + 16 * (n // 8 + 1))
                ins = nc.vector.scalar_tensor_tensor(out=acc, in0=mstage[:, n % 2, :], scalar=siluc[:, k:k + 1],
                                                     in1=mbias[:, :] if k == 0 else acc, op0=ALU.mult, op1=ALU.add)
                ins.then_inc(s_msu, 1)
                dve.wait_ge(s_msu, turns * KT + (n + 1))

            def fin(n, bank, dst_kind, hh, tile):
                dve.wait_ge(s_msum, n + 1)
                if dst_kind == "gate":
                    nc.vector.tensor_tensor(tile[:, hh * 512:(hh + 1) * 512], bank, tile[:, hh * 512:(hh + 1) * 512], ALU.mult).then_inc(s_mfin, 1)
                    return
                W(dve, s_mfin, n)
                for k in range(4):
                    kk = 4 * hh + k
                    dst = mcol[:, kk:kk + 1] if dst_kind == "scale" else shf[:, tile, kk:kk + 1]
                    ins = nc.vector.tensor_tensor_reduce(junkc[:, k, :], bank[:, k * P:(k + 1) * P], ident[:, :], 1.0, 0.0, ALU.mult, ALU.add, dst)
                ins.then_inc(s_mfin, 1)
                if dst_kind == "scale" and hh == 1:
                    e, g0 = tile
                    dve.wait_ge(s_mfin, n + 1)
                    ch.link(nc.vector.scalar_tensor_tensor(out=scl[:, e, :], in0=mcol[:, :], scalar=1.0, in1=cols[:, g0:g0 + KT],
                                                           op0=ALU.add, op1=ALU.mult))

            nsl = [0]
            for s in range(STEPS + 4):
                if s < STEPS:
                    b, kv, e, w = step_of(s)
                    head = 4 * kv + e + 2 * w
                    lo, nw = keys_of(b)
                    nk = (nw + 2) * P
                    dve.wait_ge(s_sc, s + 1)
                    W(dve, s_pt, s - 2)
                    m0 = {0: P, 3: 5 * P}.get(b, 0)
                    src = ps[:, 4 + 2 * (s % 2):6 + 2 * (s % 2), :].rearrange("p b n -> p (b n)")[:, 512 - nw * P:768]
                    ch.link(nc.vector.tensor_tensor_reduce(prob[:, s % 3, 0:nk], src, mask[:, m0:m0 + nk], 1.0, -3e38, ALU.add, ALU.max, att[:, s, 0:1]))
                    nc.vector.scalar_tensor_tensor(out=att[:, s, 1:2], in0=att[:, s, 0:1], scalar=-SCALE, in1=nsink[:, head:head + 1],
                                                   op0=ALU.mult, op1=ALU.min).then_inc(s_max, 1)
                for n, (job, _, _) in enumerate(JOBS):
                    if job_end(n) == s:
                        kind, jj, a = job
                        if kind == "m":
                            fin(2 * (jj - 2) + a, up[3], {2: "gate", 3: "shift", 4: "scale"}[jj], a, {2: gate, 3: 1, 4: (1, 16 + 2 * KT)}[jj])
                        elif kind == "z":
                            dve.wait_ge(s_used, half_of[n] + 1)
                            dve.wait_ge(s_jobf, 2 * jj + a + 1)
                            nc.vector.tensor_tensor(czb[:, a, 1:T + 1], up[3], czb[:, a, 1:T + 1], ALU.mult).then_inc(s_cz, 1)
                        elif kind == "b":
                            dve.wait_ge(s_used, half_of[n] + 1)
                            dve.wait_ge(s_cv, 2 * jj + a + 1)
                            nc.vector.tensor_tensor(cvt[:, a, :], up[3], cvt[:, a, :], ALU.mult).then_inc(s_bs, 1)
                if 1 <= s < STEPS + 1:
                    r = s - 1
                    dve.wait_ge(s_exp, r + 1)
                    ch.link(nc.vector.tensor_tensor(att[:, r, 0:1], att[:, r, 2:3], att[:, r, 3:4], ALU.add))
                    nc.vector.reciprocal(att[:, r, 3:4], att[:, r, 0:1]).then_inc(s_inv, 1)
                if 2 <= s < STEPS + 2:
                    r = s - 2
                    nb = keys_of(step_of(r)[0])[1] + 2
                    dve.wait_ge(s_ph, r + 1)
                    src = ps[:, 0:2, :].rearrange("p b n -> p (b n)")[:, 0:nb * P].rearrange("p (j n) -> p j n", n=P)
                    nc.vector.tensor_sub(pTl[:, 0:nb, r % 2, :], src, pTh[:, 0:nb, r % 2, :].bitcast(F32)).then_inc(s_pl, 1)
                for n, (job, _, _) in enumerate(JOBS):
                    if job_end(n) == s:
                        kind, jj, a = job
                        if kind == "z":
                            dve.wait_ge(s_cz1, 2 * jj + a + 1)
                            for tap in (0, 2):
                                f = 80 + 4 * tap + 2 * jj + a
                                ins = nc.vector.scalar_tensor_tensor(out=cvt[:, a, :], in0=czb[:, a, tap:tap + T], scalar=cols[:, f:f + 1],
                                                                     in1=cvt[:, a, :], op0=ALU.mult, op1=ALU.add)
                                if tap == 0:
                                    ch.link(ins)
                            ins.then_inc(s_cv, 1)
                        elif kind == "b":
                            dve.wait_ge(s_sh, 2 * jj + a + 1)
                            nc.vector.tensor_sub(aTl[:, 4 + 2 * jj + a, :], cvt[:, a, :], aTh[:, 4 + 2 * jj + a, :].bitcast(F32)).then_inc(s_sl, 1)
                if s >= 7 and (s - 7) % 4 == 0:
                    o = (s - 7) // 4
                    b, kv = divmod(o, 2)
                    dve.wait_ge(s_ah, o + 1)
                    d_ = lambda z: z[:, 2 * kv:2 * kv + 2, b * P:(b + 1) * P]
                    nc.vector.tensor_sub(d_(aTl), up[2][:, 0:2 * P].rearrange("p (w n) -> p w n", n=P), d_(aTh).bitcast(F32)).then_inc(s_al, 1)
                for n, (job, _, _) in enumerate(JOBS):
                    if job_end(n) == s - 1 and job[0] != "m":
                        nsl[0] += 1
                        straight_low(dve, 6 + nsl[0] + 2)
                for m in (2, 3, 4):
                    start = mod_start(m)
                    if start <= s < start + 4:
                        for k in (2 * (s - start), 2 * (s - start) + 1):
                            mod_step(macc0[:, :], k, nm[0])
                            nm[0] += 1

            def gate_of(e):
                return gate[:, :] if e < 3 else gate1[:, e - 3, :]

            def update(e, t):
                q = 4 * (e - 1) + t
                dve.wait_ge(s_rsy, q + 1)
                ch.link(nc.vector.scalar_tensor_tensor(out=ys[:, t, :], in0=ys[:, t, :], scalar=stat[:, 2, q:q + 1], in1=gate_of(e),
                                                       op0=ALU.mult, op1=ALU.mult))
                if e == 1:
                    dve.wait_ge(s_x, 16 * 10)
                nc.vector.tensor_tensor(xs[:, t, :], xs[:, t, :], ys[:, t, :], ALU.add).then_inc(s_xup, 1)

            def norm_x(e, t):
                n = norm_index(e, t)
                dve.wait_ge(s_xup, 4 * (e - 1) + t + 1)
                xn(n, ys[:, t, :], xs[:, t, :])

            def transition(e, pieces, splits):
                for t in range(NT + 3 if e < 4 else NT + 1):
                    if t < NT:
                        pieces(t)
                    if t == NT - 1:
                        for h in splits:
                            straight_low(dve, h)
                    if 1 <= t <= NT:
                        update(e, t - 1)
                    if 2 <= t <= NT + 1 and e < 4:
                        norm_x(e, t - 2)
                    if t >= 3 and e < 4:
                        h_low(norm_index(e, t - 3))

            def out_projection(e, h0):
                k = 0
                for u in range(3):
                    straight_low(dve, h0 + k)
                    k += 1
                    for t in range(NT):
                        last_of(dve, s_row, t, NT, h0 - 3 + 2 * u + 1, rows_before[e] + 3 * u)
                        nc.vector.tensor_copy(ys[:, t, 256 * u:256 * (u + 1)], dn[t][:, 0:256]).then_inc(s_rowf, 1)
                    straight_low(dve, h0 + k)
                    k += 1
                straight_low(dve, h0 + k)

                def piece(t):
                    last_of(dve, s_row, t, NT, h0 - 3 + 7, rows_before[e] + 9)
                    nc.vector.tensor_copy(ys[:, t, 768:1024], dn[t][:, 0:256]).then_inc(s_rowf, 1)
                return piece

            piece = out_projection(1, 21)
            transition(1, piece, [B_FFN0 + 2])

            def ffn(layer):
                hb = (B_FFN0, B_FFN1)[layer]
                jb = 2 * NPAIR * layer
                pb = 8 * NPAIR * layer

                def taps(i):
                    if isinstance(i, int):
                        src = convc[:, layer, 2 * i:2 * i + 2, :]
                    else:
                        src = convc[:, layer, bass.ds(i * 2, 2), :]
                    nc.vector.tensor_copy(cw[:, :].rearrange("p (j w) -> p j w", w=3), src).then_inc(s_cw, 1)

                def other_taps(i, jj):
                    dve.wait_ge(s_g1, jb + 2 * i + jj + 1)
                    ch.link(nc.vector.scalar_tensor_tensor(out=conv[:, jj, 1:T], in0=up[jj][:, 0:T - 1], scalar=cw[:, 3 * jj:3 * jj + 1],
                                                           in1=conv[:, jj, 1:T], op0=ALU.mult, op1=ALU.add))
                    nc.vector.scalar_tensor_tensor(out=conv[:, jj, 0:T - 1], in0=up[jj][:, 1:T], scalar=cw[:, 3 * jj + 2:3 * jj + 3],
                                                   in1=conv[:, jj, 0:T - 1], op0=ALU.mult, op1=ALU.add).then_inc(s_gc, 1)

                def gated(i, jj):
                    h, dh = ffn_half(layer, i, ("v0", "v1")[jj])
                    dve.wait_ge(s_used, h + 1 + dh)
                    dve.wait_ge(s_si, jb + 2 * i + jj + 1)
                    nc.vector.tensor_tensor(actF[:, jj, :], up[2 + jj], sil[:, jj, :], ALU.mult).then_inc(s_am, 1)

                def act_low(i, jj):
                    dve.wait_ge(s_ahh, jb + 2 * i + jj + 1)
                    nc.vector.tensor_sub(actL[:, jj, :], actF[:, jj, :], actH[:, jj, :].bitcast(F32)).then_inc(s_all, 1)

                def add_piece(i, p):
                    t, hh = divmod(p, 2)
                    if p < 7:
                        dve.wait_ge(s_dp, 7 * NPAIR * layer + 7 * i + p + 1)
                    else:
                        h, dh = ffn_half(layer, i, "d1")
                        dve.wait_ge(s_used, h + 1 + dh)
                    dst = ys[:, t, hh * 512:(hh + 1) * 512]
                    if isinstance(i, int) and i == 0:
                        nc.vector.tensor_copy(dst, dn[p % 3]).then_inc(s_ya, 1)
                    else:
                        nc.vector.tensor_tensor(dst, dn[p % 3], dst, ALU.add).then_inc(s_ya, 1)

                def turn(i, mod=None, jobs=None, last=False):
                    zero = isinstance(i, int) and i == 0
                    if not zero:
                        gated(i - 1, 1)
                        ffn_split(dve, "low", layer, i - 1, "d1")
                        act_low(i - 1, 1)
                        if jobs:
                            jobs("g0")
                        ffn_split(dve, "low", layer, i, "v0")
                    taps(i)
                    other_taps(i, 0)
                    if not zero:
                        for p in range(8):
                            add_piece(i - 1, p)
                            if mod and p % 2:
                                mod(i, p // 2)
                            if jobs and p in (2, 5):
                                jobs("d", p // 3)
                        ffn_split(dve, "low", layer, i, "g1")
                    ffn_split(dve, "low", layer, i, "v1")
                    if mod:
                        mod(i, 4)
                        mod(i, 5)
                    if jobs:
                        jobs("v0")
                    gated(i, 0)
                    act_low(i, 0)
                    if not last:
                        ffn_split(dve, "low", layer, i + 1, "g0")
                    if mod:
                        mod(i, 6)
                    if jobs:
                        jobs("g1")
                    other_taps(i, 1)
                    ffn_split(dve, "low", layer, i, "d0")
                    if mod:
                        mod(i, 7)
                    if jobs:
                        jobs("v1")

                if layer == 0:
                    n0 = nm[0]

                    def last_chunk(i, k):
                        mod_step(macc[:, 6, :], k, n0 + k)

                    def chunk(i, k):
                        acc = macc[:, bass.ds(i - 2, 1), :].rearrange("p a n -> p (a n)")
                        mod_step(acc, k, n0 + KT + k, turns=i - 2)

                    turn(0)
                    turn(1, mod=last_chunk)
                    ch.loop(2, 8, 2, lambda i: turn(i, mod=chunk))
                    ch.loop(8, NPAIR - 1, 2, turn)
                    kinds = {0: ("shift", 2), 1: ("scale", (2, 16 + 4 * KT)), 2: ("gate", gate1[:, 0, :]),
                             3: ("shift", 3), 4: ("scale", (3, 16 + 6 * KT)), 5: ("gate", gate1[:, 1, :]), 6: ("gate", gate)}

                    def jobs(what, only=None):
                        for n in ffn_jobs[what] if only is None else ffn_jobs[what][only:only + 1]:
                            m, hh = divmod(n, 2)
                            k, where = kinds[m]
                            if k == "gate":
                                dve.wait_ge(s_gain, 16 * 3)
                            fin(6 + n, dn[3], k, hh, where)
                    turn(NPAIR - 1, jobs=jobs, last=True)
                else:
                    turn(0)
                    turn(1)
                    ch.loop(2, NPAIR - 1, 2, turn)
                    turn(NPAIR - 1, last=True)
                i = NPAIR - 1
                gated(i, 1)
                ffn_split(dve, "low", layer, i, "d1")
                act_low(i, 1)

                def piece(t):
                    add_piece(i, 2 * t)
                    add_piece(i, 2 * t + 1)
                return piece

            piece = ffn(0)
            straight_low(dve, B_L1)
            transition(2, piece, [B_L1 + 1, B_L1 + 2])

            nc.vector.memset(pu[:, 0, 0:8], 0.0).then_inc(s_init, 1)
            nc.vector.memset(pu[:, 0, T + 8:T + 16], 0.0).then_inc(s_init, 1)
            for n in range(4):
                dve.wait_ge(s_xh, n + 1)
                nc.vector.tensor_sub(xTl[:, n, :], up[n], xTh[:, n, :].bitcast(F32)).then_inc(s_xl, 1)
                straight_low(dve, B_L1 + 3 + n)
            for g, w in enumerate(WINDOWS):
                dve.wait_ge(s_u, g + 1)
                dve.wait_ge(s_init, 7)
                W(dve, s_pil, g)
                src, length, span, n = pu[:, 0, :], T + 16, 1, 0
                while span < w:
                    length -= span
                    dst = pu[:, 1 + n % 2, :]
                    ch.link(nc.vector.tensor_tensor(dst[:, 0:length], src[:, 0:length], src[:, span:span + length], ALU.add))
                    src, span, n = dst, 2 * span, n + 1
                o = 8 - w // 2
                nc.vector.tensor_tensor(src[:, o:o + 8], src[:, o:o + 8], edge[:, g, 0:8], ALU.mult)
                ch.link(nc.vector.tensor_tensor(src[:, o + T - 8:o + T], src[:, o + T - 8:o + T], edge[:, g, 8:16], ALU.mult))
                nc.vector.scalar_tensor_tensor(out=pu[:, 1 + n % 2, 0:T], in0=src[:, o:o + T], scalar=1.0 / w, in1=pu[:, 0, 8:T + 8],
                                               op0=ALU.mult, op1=ALU.subtract).then_inc(s_pw, 1)
                dve.wait_ge(s_pih, g + 1)
                nc.vector.tensor_sub(bTl[:, g, :], pu[:, 1 + n % 2, 0:T], bTh[:, g, :].bitcast(F32)).then_inc(s_pil, 1)
                straight_low(dve, B_L1 + 7 + g)
            for n in range(16):
                tt, g = divmod(n, 4)
                dve.wait_ge(s_cah, n + 1)
                d_ = lambda z: z[:, :, g * P:(g + 1) * P].rearrange("p (s t) n -> p s t n", s=2)[:, :, tt, :]
                nc.vector.tensor_sub(d_(xcsL), dn[n % 4][:, 0:256].rearrange("p (s n) -> p s n", n=P), d_(xcsH).bitcast(F32)).then_inc(s_cal, 1)
            straight_low(dve, B_L1 + 11)
            for g in range(4):
                dve.wait_ge(s_pgh, g + 1)
                nc.vector.tensor_sub(bTl[:, g, :], hf[:, g % 2, :, :].rearrange("p k n -> p (k n)"), bTh[:, g, :].bitcast(F32)).then_inc(s_pgl, 1)
            straight_low(dve, B_L1 + 12)
            for ck in range(2):
                straight_low(dve, B_L1 + 13 + 2 * ck)
                for g in range(4):
                    dve.wait_ge(s_tdh, 4 * ck + g + 1)
                    nc.vector.tensor_sub(bTl[:, 4 + g, ck * 256:(ck + 1) * 256], dn[g][:, 0:256],
                                         bTh[:, 4 + g, ck * 256:(ck + 1) * 256].bitcast(F32)).then_inc(s_tdl, 1)
                straight_low(dve, B_L1 + 14 + 2 * ck)
            piece = out_projection(3, B_L1 + 17)
            transition(3, piece, [B_FFN1 + 2])
            piece = ffn(1)
            transition(4, piece, [])

        @block.tensor
        def _(pe):
            def three(dst, ah, al, bh, bl, start, stop):
                nc.tensor.matmul(dst, ah, bh, start=start, stop=False)
                nc.tensor.matmul(dst, ah, bl, start=False, stop=False)
                return nc.tensor.matmul(dst, al, bh, start=False, stop=stop)

            def norm_transposes(n):
                pe.wait_ge(s_xn, n + 1)
                W(pe, s_hf, 2 * (n - 2) + 2)
                for b in range(2):
                    for k in range(4):
                        ins = nc.tensor.transpose(up[2 * (n % 2) + b][:, k * P:(k + 1) * P],
                                                  norm_src(n)[:, (4 * b + k) * P:(4 * b + k + 1) * P], ident[:, :])
                    ins.then_inc(s_tr, 1)

            pe.wait_ge(s_small, 16 * 13)
            nc.tensor.transpose(up[0][:, 0:96], vecs[0:96, :], ident[0:96, 0:96]).then_inc(s_vt, 1)
            for l in range(2):
                nc.tensor.transpose(up[1 + l][:, 0:3 * NJ], vecf[0:3 * NJ, l, :], ident[0:3 * NJ, 0:3 * NJ]).then_inc(s_vt, 1)
            pe.wait_ge(s_silu, 1)
            sc = siluc[:, :].rearrange("p (v k) -> p k v", v=2)
            for k in range(KT):
                pe.wait_ge(s_first[k % 4], 16 * (k // 4 + 1))
                for n in range(4):
                    ins = nc.tensor.matmul(dn[n][0:2, :], sc[:, k, :], mfirst[:, k % 4, n * 512:(n + 1) * 512], start=(k == 0), stop=(k == KT - 1))
                ins.then_inc(s_mr if k == KT - 1 else s_mfu, 1)
                if k == 3:
                    pe.wait_ge(s_cols, 3)
                    norm_transposes(0)
                    norm_transposes(1)
            pe.wait_ge(s_mrb, 1)
            for k in range(16):
                ins = nc.tensor.transpose(dn[0][:, 2 * k:2 * k + 2], mrow[:, k * P:(k + 1) * P], ident[0:2, 0:2])
            ins.then_inc(s_mrt, 1)
            for n in range(2, 6):
                norm_transposes(n)

            def stat_qkv(which):
                def f(r, k):
                    z, zc = ((hTh, hcTh), (hTl, hcTl))[which]
                    return z[:, k, r * P:(r + 1) * P] if r < 4 else zc[:, k, (r - 4) * P:(r - 3) * P]
                return f

            def qk_transposes(n):
                pe.wait_ge(s_rope, n + 1)
                W(pe, s_ql, n - 1) if n >= 2 else pe.wait_ge(s_hf, 12)
                for h in range(4 if n < 8 else 2):
                    ins = nc.tensor.transpose(up[n % 2][:, h * P:(h + 1) * P], qd[:, n % 4, h, :], ident[:, :])
                ins.then_inc(s_qt, 1)

            banks6 = dn + up[2:4]
            for u in range(3):
                for a in range(2):
                    def before(r, u=u, a=a):
                        if a == 0:
                            if u == 0:
                                pe.wait_ge(s_hl, 2 * (r + 1))
                                if r == 0:
                                    pe.wait_ge(s_scl, 2)
                            elif r < 4:
                                pe.wait_ge(s_rope, 4 * (u - 1) + r + 1)
                            else:
                                pe.wait_ge(s_hl, 12)
                    tm_half_ins(pe, three, half_view, 2 * u + a, 4 if u < 2 else 6, a, stat_qkv(0), stat_qkv(1), banks6, before, s_row, s_used, s_lo, wh, wl)
                    if u and a == 0:
                        for n in range(4 * (u - 1), 4 * u):
                            qk_transposes(n)
            for n in range(8, 14):
                qk_transposes(n)

            atoms = [(n, i) for n, (j, lo, hi) in enumerate(JOBS) for i in range(hi - lo)]
            def atom(n, i):
                kind, jj, a = JOBS[n][0]
                total = JOBS[n][2] - JOBS[n][1]
                if i == 0:
                    if n == 0:
                        pe.wait_ge(s_vl, 6)
                        pe.wait_ge(s_rope, 14)
                    else:
                        job_free(n - 1)
                if kind == "m":
                    if i == 0:
                        pe.wait_ge(s_msu, 8 * (jj - 1))
                        nc.tensor.matmul(up[3], ones[:, :], macc0[:, a * 512:(a + 1) * 512], start=True, stop=True).then_inc(s_msum, 1)
                    return
                h = half_of[n]
                if i == 0:
                    pe.wait_ge(s_lo, h + 1)
                k, p = divmod(i, 3)
                vh, vl = half_view(wh, h, "fm"), half_view(wl, h, "fm")
                wt = (vh, vh, vl)[p][:, k, :]
                mv = (hTh, hTl, hTh)[p][:, k, :]
                ins = nc.tensor.matmul(up[3], wt, mv, start=(i == 0), stop=(i == total - 1))
                if i == total - 1:
                    ins.then_inc(s_used, 1)

            def job_free(n):
                kind, jj, a = JOBS[n][0]
                if kind == "m":
                    pe.wait_ge(s_mfin, 2 * (jj - 2) + a + 1)
                elif kind == "c":
                    pe.wait_ge(s_jobf, 2 * jj + a + 1)
                elif kind == "z":
                    pe.wait_ge(s_cz, 2 * jj + a + 1)
                else:
                    pe.wait_ge(s_bs, 2 * jj + a + 1)

            def scores(s):
                b, kv, e, w = step_of(s)
                head = 4 * kv + e + 2 * w
                lo, nw = keys_of(b)
                if s < 2:
                    pe.wait_ge(s_rope, 14)
                    pe.wait_ge(s_vl, 6)
                    pe.wait_ge(s_ql, 14)
                else:
                    pe.wait_ge(s_max, s - 1)
                a0 = ps[:, 4 + 2 * (s % 2), 512 - nw * P:512]
                a1 = ps[:, 5 + 2 * (s % 2), 0:TC]
                q = qT[:, head, b * P:(b + 1) * P]
                for z, st, sp_ in ((kH, True, False), (kL, False, True)):
                    nc.tensor.matmul(a0, q, z[:, kv, lo * P:(lo + nw) * P], start=st, stop=sp_)
                    ins = nc.tensor.matmul(a1, q, z[:, kv, T:T + TC], start=st, stop=sp_)
                ins.then_inc(s_sc, 1)

            def prob_transposes(r):
                nb = keys_of(step_of(r)[0])[1] + 2
                pe.wait_ge(s_pn, r + 1)
                W(pe, s_pl, r)
                for j in range(nb):
                    ins = nc.tensor.transpose(ps[:, j // 4, (j % 4) * P:(j % 4 + 1) * P], prob[:, r % 3, j * P:(j + 1) * P], ident[:, :])
                ins.then_inc(s_pt, 1)

            def values(g):
                b, kv, e, _ = step_of(2 * g)
                lo, nw = keys_of(b)
                pe.wait_ge(s_pl, 2 * g + 2)
                if e == 0:
                    W(pe, s_al, g // 2)
                off = 64 + 128 * kv - 64 * e
                for j in range(nw + 2):
                    tile = lo + j if j < nw else NT + j - nw
                    vh, vl = vH[:, tile, off:off + P], vL[:, tile, off:off + P]
                    mh, ml = (z[:, j, :, :].rearrange("p w n -> p (w n)") for z in (pTh, pTl))
                    nc.tensor.matmul(up[2][:, 0:256], vh, mh, start=(e == 0 and j == 0), stop=False)
                    nc.tensor.matmul(up[2][:, 0:256], vl, mh, start=False, stop=False)
                    ins = nc.tensor.matmul(up[2][:, 0:256], vh, ml, start=False, stop=(e == 1 and j == nw + 1))
                ins.then_inc(s_pv, 1)

            for s in range(STEPS + 3):
                if s < STEPS:
                    scores(s)
                mine = atoms[PER_STEP * s:PER_STEP * (s + 1)]
                cut = next((n for n, (j, i) in enumerate(mine) if i == 0), len(mine))
                for n, i in mine[:cut]:
                    atom(n, i)
                if s >= 4 and s % 2 == 0:
                    values((s - 4) // 2)
                if 2 <= s < STEPS + 2:
                    prob_transposes(s - 2)
                for n, i in mine[cut:]:
                    atom(n, i)

            def out_projection(e, h0, th, tl, order):
                for u in range(4):
                    for a in range(2):
                        def before(r, u=u, a=a):
                            if a == 0:
                                if u:
                                    pe.wait_ge(s_rowf, 16 * (e // 2) + 4 * (u - 1) + r + 1)
                        tm_half_ins(pe, three, half_view, h0 + 2 * u + a, 4, a,
                                    lambda r, k: th[:, order[k], r * P:(r + 1) * P], lambda r, k: tl[:, order[k], r * P:(r + 1) * P],
                                    dn, before, s_row, s_used, s_lo, wh, wl, first=lambda a=a, u=u: out_ready(e, u, a))

            def out_ready(e, u, a):
                if u == 0 and e == 1:
                    if a == 0:
                        pe.wait_ge(s_sl, 4)
                        pe.wait_ge(s_max, STEPS)
                    else:
                        pe.wait_ge(s_al, STEPS // 4)
                if u == 0 and e == 3 and a == 0:
                    pe.wait_ge(s_pgl, 4)
                    pe.wait_ge(s_tdl, 8)

            def transition(e):
                for t in range(NT):
                    norm_transposes(norm_index(e, t))

            out_projection(1, 18, aTh, aTl, (4, 5, 6, 7, 0, 1, 2, 3))
            transition(1)

            def ffn(layer):
                hb = (B_FFN0, B_FFN1)[layer]
                jb = 2 * NPAIR * layer
                pb = 8 * NPAIR * layer
                e = 1 + 2 * layer

                def up_half(i, what):
                    h, dh = ffn_half(layer, i, what)
                    jj = int(what[1])
                    pe.wait_ge(s_lo, h + 1 + dh)
                    if isinstance(i, int) and i == 0:
                        pe.wait_ge(s_hl, 2 * norm_index(e, NT - 1) + 2)
                    elif what[0] == "g":
                        pe.wait_ge(s_gc, jb + 2 * i + jj - 1)
                    else:
                        pe.wait_ge(s_am, jb + 2 * i + jj - 1)
                    dst = up[jj + (2 if what[0] == "v" else 0)]
                    vh, vl = half_view(wh, h, "fm"), half_view(wl, h, "fm")
                    for k in range(KT):
                        nc.tensor.matmul(dst, vh[:, k, :], hTh[:, k, :], start=(k == 0), stop=False)
                        nc.tensor.matmul(dst, vh[:, k, :], hTl[:, k, :], start=False, stop=False)
                        ins = nc.tensor.matmul(dst, vl[:, k, :], hTh[:, k, :], start=False, stop=(k == KT - 1))
                        if k == KT - 1:
                            ins.then_inc(s_used, 1)
                        if k == 2 or k == 5 or k == KT - 1:
                            yield k

                def down(i, between=None):
                    h, dh = ffn_half(layer, i, "d0")
                    pe.wait_ge(s_lo, h + 2 + dh)
                    pe.wait_ge(s_all, jb + 2 * i + 2)
                    for p in range(8):
                        t, hh = divmod(p, 2)
                        if not (isinstance(i, int) and i == 0) or p >= 3:
                            pe.wait_ge(s_ya, pb + 8 * i + (-1, 0, -2)[p] if p < 3 else pb + 8 * i + p - 2)
                        for jj in range(2):
                            wv = lambda z: z[:, (h + jj) % RING, hh * 512:(hh + 1) * 512]
                            ins = three(dn[p % 3], actH[:, jj, t * P:(t + 1) * P], actL[:, jj, t * P:(t + 1) * P], wv(wh), wv(wl),
                                        start=(jj == 0), stop=(jj == 1))
                        if p < 7:
                            ins.then_inc(s_dp, 1)
                        else:
                            ins.then_inc(s_used, 2)
                        if between and p in (2, 5):
                            between(p)

                def job(n):
                    if n:
                        pe.wait_ge(s_mfin, 6 + n)
                    m, hh = divmod(n, 2)
                    nc.tensor.matmul(dn[3], ones[:, :], macc[:, m, hh * 512:(hh + 1) * 512], start=True, stop=True).then_inc(s_msum, 1)

                def turn(i, jobs=False):
                    def half(what):
                        for n, _ in enumerate(up_half(i, what)):
                            if jobs:
                                job(ffn_jobs[what][n])
                    half("g0")
                    if not (isinstance(i, int) and i == 0):
                        down(i - 1, (lambda p: job(ffn_jobs["d"][p // 3])) if jobs else None)
                    half("v0")
                    half("g1")
                    half("v1")

                turn(0)
                turn(1)
                with pe.Fori(2, NPAIR - 1) as i:
                    turn(i)
                if layer == 0:
                    pe.wait_ge(s_msu, 10 * KT)
                turn(NPAIR - 1, jobs=(layer == 0))
                down(NPAIR - 1)

            ffn(0)
            transition(2)

            for n in range(8):
                h = B_L1 + n
                pe.wait_ge(s_lo, h + 1)
                if n == 0:
                    pe.wait_ge(s_hl, 2 * norm_index(2, NT - 1) + 2)
                elif n >= 4:
                    pe.wait_ge(s_xl, n - 3)
                vh, vl = half_view(wh, h, "fm"), half_view(wl, h, "fm")
                for k in range(KT):
                    nc.tensor.matmul(up[n % 4], vh[:, k, :], hTh[:, k, :], start=(k == 0), stop=False)
                    nc.tensor.matmul(up[n % 4], vh[:, k, :], hTl[:, k, :], start=False, stop=False)
                    ins = nc.tensor.matmul(up[n % 4], vl[:, k, :], hTh[:, k, :], start=False, stop=(k == KT - 1))
                ins.then_inc(s_used, 1)
            h = B_L1 + 8
            pe.wait_ge(s_lo, h + 1)
            pe.wait_ge(s_xl, 4)
            for n in range(16):
                tt, g = divmod(n, 4)
                if n >= 4:
                    pe.wait_ge(s_cal, n - 3)
                ins = three(dn[n % 4][:, 0:256], xTh[:, g, tt * P:(tt + 1) * P], xTl[:, g, tt * P:(tt + 1) * P],
                            wh[:, h % RING, 0:256], wl[:, h % RING, 0:256], True, True)
                ins.then_inc(s_ca if n < 15 else s_used, 1)
            h = B_L1 + 9
            pe.wait_ge(s_lo, h + 1)
            for g in range(4):
                pe.wait_ge(s_pil, g + 1)
                pe.wait_ge(s_u, g + 1)
                ins = three(up[g], wh[:, h % RING, g * P:(g + 1) * P], wl[:, h % RING, g * P:(g + 1) * P], bTh[:, g, :], bTl[:, g, :], True, True)
                ins.then_inc(s_pg if g < 3 else s_used, 1)
            for ck in range(2):
                for a in range(2):
                    def before(r, ck=ck, a=a):
                        if a == 0 and ck:
                            pe.wait_ge(s_tdl, r + 1)
                    tm_half_ins(pe, three, half_view, B_L1 + 10 + 2 * ck + a, 4, a,
                                lambda r, k: xcsH[:, k, r * P:(r + 1) * P], lambda r, k: xcsL[:, k, r * P:(r + 1) * P],
                                dn, before, s_td, s_used, s_lo, wh, wl, first=lambda: pe.wait_ge(s_cal, 16))
            out_projection(3, B_L1 + 14, bTh, bTl, tuple(range(8)))
            transition(3)
            ffn(1)


def tm_half_ins(pe, three, half_view, h, rows, a, stat_h, stat_l, banks, before, done, s_used, s_lo, wh, wl, first=None):
    pe.wait_ge(s_lo, h + 1)
    if first:
        first()
    vh, vl = half_view(wh, h, "tm"), half_view(wl, h, "tm")
    for r in range(rows):
        before(r)
        for k in range(4):
            ins = three(banks[r][:, 0:256], stat_h(r, 4 * a + k), stat_l(r, 4 * a + k), vh[:, k, :], vl[:, k, :],
                        a == 0 and k == 0, a == 1 and k == 3)
        if a == 1 and r < rows - 1:
            ins.then_inc(done, 1)
    ins.then_inc(s_used, 1)


_INS = ["x", "c", "ctx", "c_ctx", "mod_w", "mod_b", "norm_g", "att_w_in", "att_sink", "sconv_w", "att_w_out",
        "mix_w_in", "pool_w_grp", "pool_scale", "mix_w_out", "ffn_w_up", "ffn_conv", "ffn_w_down"]


def kernel(**inputs):
    import concourse.bacc as _bacc
    from concourse.bass_utils import run_bass_kernel_spmd as _run

    nc = _bacc.Bacc("TRN2", target_bir_lowering=False, num_devices=1)
    arrays, args = {}, {}
    given = {name: np.ascontiguousarray(inputs[name]) for name in _INS}
    for name, a in {**given, **constants()}.items():
        arrays[f"in_{name}"] = a
        args[name] = nc.dram_tensor(f"in_{name}", a.shape, mybir.dt.from_np(a.dtype), kind="ExternalInput").ap()
    args["out"] = nc.dram_tensor("out", (1, T, D), F32, kind="ExternalOutput").ap()
    build(nc, **args)
    return _run(nc, [arrays], core_ids=[0]).results[0]["out"]
```

```python
from contextlib import ExitStack

import numpy as np

import concourse.bass as bass
from concourse import mybir

F32 = mybir.dt.float32
F32R = mybir.dt.float32r
ALU = mybir.AluOpType
ACT = mybir.ActivationFunctionType

P = 128
D = 1024
T = 512
TC = 256
NT = T // P
NTC = TC // P
KT = D // P
DFF = 2816
NJ = DFF // P
NPAIR = NJ // 2
HEADS, KVH, HD = 8, 2, 64
QKV = (HEADS + 2 * KVH) * HD
SCD = 512
EPS = 1e-6
SCALE = HD ** -0.5
MASKED = -1e30
WINDOWS = (2, 4, 8, 16)
GRID_W = 64
RING = 3
HALF = 1024
MC = 1024
KB = 1024

U_L0 = 13
U_FFN = 3 * NPAIR
U_L1 = 11
B_FFN0 = 2 * U_L0
B_L1 = B_FFN0 + 2 * U_FFN
B_FFN1 = B_L1 + 2 * U_L1


def constants():
    t = np.arange(T)
    nf = HD // 4
    inv = (10000.0 ** (-np.arange(nf, dtype=np.float32) / nf)).astype(np.float32)
    ang = [(v.astype(np.float32)[:, None] * inv).astype(np.float32).astype(np.float64) for v in (t // GRID_W, t % GRID_W)]
    cos = np.concatenate([np.concatenate([np.cos(a)] * 2, 1) for a in ang], 1)
    sin = np.concatenate([np.concatenate([-np.sin(a), np.sin(a)], 1) for a in ang], 1)
    q, k = np.arange(P)[:, None], np.arange(P)[None, :]
    before = np.where(k >= q, 0.0, MASKED)
    after = np.where(k <= q, 0.0, MASKED)
    z = np.zeros((P, P))
    mask = np.concatenate([before, z, after, z, z, before, z, z, z], 1)
    a = 2 * np.pi * np.outer(t, t) % (2 * np.pi * T) / T
    norm = 1.0 / np.sqrt(T * P)
    c = np.arange(P)
    b = 2 * np.pi * (np.outer(c, c) % P) / P
    a = 2 * np.pi * (np.outer(t, t) % T) / T
    edge = np.zeros((4, 16))
    for g, w in enumerate(WINDOWS):
        for n, p in enumerate(list(range(8)) + list(range(T - 8, T))):
            edge[g, n] = w / (min(p + w - w // 2, T) - max(p - w // 2, 0))
    f = np.float32
    return {
        "rope_cos": np.tile(cos, (1, 4)).astype(f), "rope_sin": np.tile(sin, (1, 4)).astype(f),
        "attn_mask": mask.astype(f), "identity": np.eye(P, dtype=f),
        "dft_time": (np.concatenate([np.cos(a), -np.sin(a)], 0) * norm).astype(f),
        "dft_chan": np.concatenate([np.cos(b), np.sin(b)], 1).astype(f),
        "pool_edge": edge.astype(f),
    }


class Chain:

    def __init__(self, eng, sem):
        self.eng, self.sem, self.n, self.extra = eng, sem, 0, None

    def link(self, ins):
        ins.then_inc(self.sem, 1)
        self.n += 1
        self.eng.wait_ge(self.sem, self.n if self.extra is None else self.n + self.extra)

    def loop(self, lo, hi, per, body):
        n0 = self.n
        with self.eng.Fori(lo, hi) as i:
            self.extra = (i - lo) * per
            body(i)
            assert self.n - n0 == per, (self.n - n0, per)
        self.extra = None
        self.n = n0 + per * (hi - lo)


def attention_jobs():
    fm = [(kind, jj, a) for jj in range(2) for kind in "czb" for a in range(2)]
    jobs = []
    for n, j in enumerate(fm):
        jobs.append(j)
        if n in (4, 8, 11):
            m = {4: 2, 8: 3, 11: 4}[n]
            jobs += [("m", m, 0), ("m", m, 1)]
    at, out = 0, []
    for j in jobs:
        first = at
        at += 4 if j[0] == "m" else 3 * KT
        out.append((j, first, at))
    return out


JOBS = attention_jobs()
STEPS = 4 * HEADS
PER_STEP = -(-JOBS[-1][2] // STEPS)


def job_end(n):
    return (JOBS[n][2] - 1) // PER_STEP


def step_of(s):
    return s // 8, (s // 4) % 2, (s // 2) % 2, s % 2


def keys_of(b):
    lo, hi = max(b - 1, 0), min(b + 1, NT - 1)
    return lo, hi - lo + 1


def build(nc, x, c, ctx, c_ctx, mod_w, mod_b, norm_g, att_w_in, att_sink, sconv_w, att_w_out, mix_w_in,
          pool_w_grp, pool_scale, mix_w_out, ffn_w_up, ffn_conv, ffn_w_down, rope_cos, rope_sin,
          attn_mask, identity, dft_time, dft_chan, pool_edge, out):
    ctxs = ExitStack()
    base = -(-nc.sbuf_base // 64) * 64

    def at(name, shape, dt, kb):
        return nc.alloc_sbuf_tensor_at(name, shape, dt, offset=base + int(kb * KB))

    with ctxs:
        hTh = at("hTh", [P, KT, T], F32R, 0)
        hTl = at("hTl", [P, KT, T], F32R, 16)
        wh = at("wh", [P, RING, HALF], F32R, 32)
        wl = at("wl", [P, RING, HALF], F32R, 44)
        mstage = at("mstage", [P, 2, MC], F32, 56)
        macc0 = at("macc0", [P, MC], F32, 64)
        macc1 = at("macc1", [P, MC], F32, 203.5625)
        mbias = at("mbias", [P, MC], F32, 68)
        gate = at("gate", [P, D], F32, 72)
        ident = at("ident", [P, P], F32, 76)
        ones = at("ones", [P, P], F32, 76.5)
        junkc = at("junkc", [P, 4, P], F32, 77)
        vecs = at("vecs", [P, P], F32, 77.5)
        vecf = at("vecf", [P, 2, P], F32, 78)
        cols = at("cols", [P, 96], F32, 79)
        convc = at("convc", [P, 2, NJ, 3], F32, 79.375)
        cw = at("cw", [P, 6], F32, 80)
        siluc = at("siluc", [P, 16], F32, 80.0625)
        modc = at("modc", [P, 16, 2], F32, 80.125)
        scl = at("scl", [P, 5, KT], F32, 80.25)
        shf = at("shf", [P, 5, KT], F32, 80.4375)
        mcol = at("mcol", [P, KT], F32, 80.625)
        sink = at("sink", [P, HEADS], F32, 80.6875)
        nsink = at("nsink", [P, HEADS], F32, 80.75)
        stat = at("stat", [P, 8, 24], F32, 80.8125)
        mhalf = at("mhalf", [P, 1], F32, 81.6875)
        edge = at("edge", [P, 4, 16], F32, 81.71875)
        raw = [at("raw0", [P, 2, HALF], F32, 82), at("raw1", [P, 2, HALF], F32, 90), at("raw2", [P, 2, HALF], F32, 98)]
        xs = at("xs", [P, NT, D], F32, 106)
        ys = at("ys", [P, NT, D], F32, 122)
        hf = at("hf", [P, 2, 4, P], F32, 203.5625)
        junk = at("junk", [P, D], F32, 199.53125)
        qT = at("qT", [P, HEADS, T], F32R, 98)
        kH = at("kH", [P, KVH, T + TC], F32R, 114)
        kL = at("kL", [P, KVH, T + TC], F32R, 120)
        vH = at("vH", [P, NT + NTC, 320], F32R, 126)
        vL = at("vL", [P, NT + NTC, 320], F32R, 133.5)
        mask = at("mask", [P, 9 * P], F32, 141)
        aTh = at("aTh", [P, KT, T], F32R, 146)
        aTl = at("aTl", [P, KT, T], F32R, 162)
        prob = at("prob", [P, 3, 640], F32, 178)
        pTh = at("pTh", [P, 5, 2, P], F32R, 185.5)
        pTl = at("pTl", [P, 5, 2, P], F32R, 190.5)
        czb = at("czb", [P, 2, T + 2], F32, 195.5)
        cvt = at("cvt", [P, 2, T], F32, 199.53125)
        att = at("att", [P, STEPS, 4], F32, 145.5)
        xc = at("xc", [P, NTC, D], F32, 98)
        mfirst = at("mfirst", [P, 4, 2 * MC], F32, 146)
        hcTh = at("hcTh", [P, KT, TC], F32R, 146)
        hcTl = at("hcTl", [P, KT, TC], F32R, 154)
        mrow = at("mrow", [2, 2 * MC], F32, 178)
        brow = at("brow", [2, 2 * MC], F32, 186)
        rcos = at("rcos", [P, NT, 256], F32, 56)
        rsin = at("rsin", [P, NT, 256], F32, 60)
        rt = at("rt", [P, 2, 256], F32, 186)
        qd = at("qd", [P, 4, 4, P], F32, 188)
        actH = at("actH", [P, 2, T], F32R, 138)
        actL = at("actL", [P, 2, T], F32R, 142)
        conv = at("conv", [P, 2, T], F32, 146)
        sil = at("sil", [P, 2, T], F32, 150)
        actF = at("actF", [P, 2, T], F32, 154)
        macc = at("macc", [P, 7, MC], F32, 158)
        bTh = at("bTh", [P, KT, T], F32R, 138)
        bTl = at("bTl", [P, KT, T], F32R, 154)
        xcsH = at("xcsH", [P, 8, T], F32R, 170)
        xcsL = at("xcsL", [P, 8, T], F32R, 186)
        xTh = at("xTh", [P, 4, T], F32R, 122)
        xTl = at("xTl", [P, 4, T], F32R, 130)
        pu = at("pu", [P, 3, T + 16], F32, 64)
        gate1 = at("gate1", [P, 2, D], F32, 56)

        ps = ctxs.enter_context(nc.psum_tensor("ps", [P, 8, 512], F32))
        up = [ps[:, b, :] for b in range(4)]
        dn = [ps[:, 4 + b, :] for b in range(4)]
        job_bank = [up[3], dn[3]]
        pv_bank = [dn[2], up[2]]

        def sem(name):
            return ctxs.enter_context(nc.semaphore(name))

        s_small = sem("small_loaded")
        s_vecs = sem("vectors_loaded")
        s_vecf = sem("taps_loaded")
        s_x = sem("x_loaded")
        s_first = [sem(f"mfirst_loaded{n}") for n in range(4)]
        s_tab = sem("rope_loaded")
        s_raw = [sem(f"raw_loaded{n}") for n in range(3)]
        s_ms = [sem(f"mstage_loaded{n}") for n in range(2)]
        s_mb = sem("mbias_loaded")
        s_gain = sem("gain_row_loaded")
        s_out = sem("out_stored")
        s_init = sem("constants_set")
        s_pc = sem("pool_chain")
        s_vc = sem("vector_chain")
        s_ac = sem("scalar_chain")
        s_hi = sem("half_high")
        s_lo = sem("half_low")
        s_used = sem("half_used")
        s_vt = sem("vectors_transposed")
        s_cols = sem("columns_ready")
        s_silu = sem("silu_c_ready")
        s_mfu = sem("mfirst_used")
        s_mr = sem("mod_rows_summed")
        s_mrb = sem("mod_rows_ready")
        s_mrt = sem("mod_rows_transposed")
        s_scl = sem("scales_ready")
        s_mp = sem("mod_products")
        s_msu = sem("mstage_used")
        s_macc = sem("macc_ready")
        s_msum = sem("macc_summed")
        s_mfin = sem("macc_finished")
        s_sqy = sem("y_squares")
        s_rsy = sem("y_rstd")
        s_yg = sem("y_gated")
        s_xup = sem("x_left_updated")
        s_xur = sem("x_right_updated")
        s_sqx = sem("x_squares")
        s_rsx = sem("x_rstd")
        s_xn = sem("x_normed")
        s_tr = sem("norm_transposed")
        s_hf = sem("h_ready")
        s_hh = sem("h_high")
        s_hl = sem("h_low")
        s_row = sem("rows_multiplied")
        s_rowf = sem("rows_taken")
        s_rope = sem("roped")
        s_qt = sem("qk_transposed")
        s_qh = sem("qk_high")
        s_ql = sem("qk_low")
        s_vh = sem("v_high")
        s_vl = sem("v_low")
        s_sc = sem("scores")
        s_max = sem("maxima")
        s_exp = sem("exponentials")
        s_inv = sem("inverse_totals")
        s_pn = sem("probs_normed")
        s_pt = sem("probs_transposed")
        s_ph = sem("probs_high")
        s_pl = sem("probs_low")
        s_pv = sem("pv_used_probs")
        s_ah = sem("attn_high")
        s_al = sem("attn_low")
        s_jobf = sem("job_bank_free")
        s_cz = sem("cz_ready")
        s_cz1 = sem("centre_tap")
        s_cv = sem("sconv_done")
        s_bs = sem("sconv_gated")
        s_sh = sem("sconv_high")
        s_sl = sem("sconv_low")
        s_cw = sem("taps_ready")
        s_g1 = sem("ffn_centre_tap")
        s_gc = sem("ffn_conv_done")
        s_si = sem("ffn_silu")
        s_am = sem("ffn_gated")
        s_ahh = sem("act_high")
        s_all = sem("act_low")
        s_dp = sem("down_piece")
        s_ya = sem("y_added")
        s_xh = sem("l1_fft_high")
        s_xl = sem("l1_fft_low")
        s_u = sem("pool_in_ready")
        s_pw = sem("pool_windowed")
        s_pih = sem("pool_high")
        s_pil = sem("pool_low")
        s_ca = sem("chan_dft")
        s_cah = sem("chan_dft_high")
        s_cal = sem("chan_dft_low")
        s_pg = sem("pool_grouped")
        s_pgs = sem("pool_scaled")
        s_pgh = sem("pool_out_high")
        s_pgl = sem("pool_out_low")
        s_td = sem("time_dft")
        s_tdh = sem("time_dft_high")
        s_tdl = sem("time_dft_low")

        block = ctxs.enter_context(nc.Block())

        def W(eng, s, v):
            if not (isinstance(v, int) and v <= 0):
                eng.wait_ge(s, v)

        def last_of(eng, s, n, count, h, before=0):
            if n < count - 1:
                eng.wait_ge(s, before + n + 1)
            else:
                eng.wait_ge(s_used, h + 1)

        def half_view(t, h, kind):
            v = t[:, h % RING, :]
            if kind == "tm":
                return v.rearrange("p (k n) -> p k n", n=256)
            if kind == "fm":
                return v.rearrange("p (k n) -> p k n", n=P)
            return v

        def raw_view(slot, a, kind):
            if kind == "fm":
                return raw[slot].rearrange("p a (k n) -> p (a k) n", n=256)[:, :, a * P:(a + 1) * P]
            if kind == "chan":
                return raw[slot][:, a, 0:256]
            if kind == "grp":
                return raw[slot][:, a, 0:512]
            return raw[slot][:, a, :]

        def ring_view(t, h, kind):
            v = t[:, h % RING, :]
            if kind == "fm":
                return v.rearrange("p (k n) -> p k n", n=P)
            if kind == "chan":
                return v[:, 0:256]
            if kind == "grp":
                return v[:, 0:512]
            return v

        def split_high(act, h, slot, a, kind, loads, dh=0):
            act.wait_ge(s_raw[slot], loads)
            W(act, s_used, h - 2 + dh)
            nc.scalar.activation(ring_view(wh, h, kind), raw_view(slot, a, kind), ACT.Copy).then_inc(s_hi, 1)

        def split_low(dve, h, slot, a, kind, dh=0):
            dve.wait_ge(s_hi, h + 1 + dh)
            nc.vector.tensor_sub(ring_view(wl, h, kind), raw_view(slot, a, kind), ring_view(wh, h, kind).bitcast(F32)).then_inc(s_lo, 1)

        plan = {}
        uses = [0, 0, 0]

        def unit(u2, slot, kinds):
            uses[slot] += 1
            for a in range(2):
                plan[u2 + a] = (slot, a, kinds[a], 32 * uses[slot])

        for u in range(U_L0):
            unit(2 * u, u % 2, ("tm", "tm") if u < 3 or u >= 9 else ("fm", "fm"))
        ffn_uses = []
        ffn_uses.append(list(uses))
        uses[:] = [n + NPAIR for n in uses]
        for u in range(U_L1):
            unit(B_L1 + 2 * u, (0, 2, 1)[u % 3], ("fm", "fm") if u < 4 else (("chan", "grp") if u == 4 else ("tm", "tm")))
        ffn_uses.append(list(uses))

        half_of = {n: 6 + f for f, n in enumerate(n for n, (j, _, _) in enumerate(JOBS) if j[0] != "m")}
        ffn_jobs = {"g0": (0, 1, 2), "d": (3, 4), "v0": (5, 6, 7), "g1": (8, 9, 10), "v1": (11, 12, 13)}
        rows_before = {1: 11, 3: 23}

        GS, DS, VS = 0, 1, 2

        def ffn_half(layer, i, what):
            hb = (B_FFN0, B_FFN1)[layer]
            k = {"g0": -2, "v0": 1, "g1": 2, "v1": 3, "d0": 5, "d1": 6}[what]
            if not isinstance(i, int):
                return hb + k, i * 6
            if i == 0 and what in ("g0", "v0"):
                k += 2 if what == "g0" else 0
            if i == NPAIR - 1 and what[0] == "d":
                k -= 1
            return hb + k + 6 * i, 0

        def ffn_split(eng, fn, layer, i, what):
            slot = {"g": GS, "d": DS, "v": VS}[what[0]]
            h, dh = ffn_half(layer, i, what)
            kind = "dn" if what[0] == "d" else "fm"
            loads = (i + (ffn_uses[layer][slot] + 1)) * 32
            if fn == "high":
                split_high(eng, h, slot, int(what[1]), kind, loads, dh)
            else:
                split_low(eng, h, slot, int(what[1]), kind, dh)

        def straight_high(act, h):
            if h in plan:
                slot, a, kind, loads = plan[h]
                split_high(act, h, slot, a, kind, loads)
            else:
                layer, idx = (0, h - B_FFN0) if h < B_L1 else (1, h - B_FFN1)
                ffn_split(act, "high", layer, 0, ("g0", "v0", "g1", "v1")[idx])

        def straight_low(dve, h):
            if h in plan:
                slot, a, kind, _ = plan[h]
                split_low(dve, h, slot, a, kind)
            else:
                layer, idx = (0, h - B_FFN0) if h < B_L1 else (1, h - B_FFN1)
                ffn_split(dve, "low", layer, 0, ("g0", "v0", "g1", "v1")[idx])

        def norm_index(e, t):
            return t if e == 0 else 6 + 4 * (e - 1) + t

        def norm_cols(n):
            return (4 if 4 <= n < 6 else 0) if n < 6 else 1 + (n - 6) // 4

        def norm_bank(n, b):
            banks = dn if n >= 6 and (n - 6) % 4 >= 2 else up
            return banks[2 * (n % 2) + b]

        def norm_src(n):
            return xs[:, n, :] if n < 4 else (xc[:, n - 4, :] if n < 6 else ys[:, (n - 6) % 4, :])

        def norm_dst(t, n):
            if 4 <= n < 6:
                return (hcTh, hcTl)[t][:, :, (n - 4) * P:(n - 3) * P]
            tt = n if n < 4 else (n - 6) % 4
            return (hTh, hTl)[t][:, :, tt * P:(tt + 1) * P]

        @block.sync
        def _(sp):
            def load_unit(slot, halves):
                for dst, src in halves:
                    sp.dma_start(dst, src).then_inc(s_raw[slot], 16)

            def cols_unit(slot, w, c0, order=(0, 1)):
                v = w[:, c0:c0 + 256].rearrange("(k p) n -> p k n", p=P)
                load_unit(slot, [(raw[slot][:, a, :].rearrange("p (k n) -> p k n", n=256), v[:, 4 * g:4 * g + 4, :])
                                 for a, g in enumerate(order)])

            w_in, w_out = att_w_in[0], att_w_out[0]

            for dst, src in ((vecs[0:8, :], c.rearrange("b (r p) -> (b r) p", p=P)),
                             (vecs[8:16, :], c_ctx.rearrange("(r p) -> r p", p=P)),
                             (vecs[16:80, :], norm_g.rearrange("l g (r p) -> (l g r) p", p=P))):
                sp.dma_start(dst, src).then_inc(s_vecs, 16)

            def first(k):
                if k >= 4:
                    sp.wait_ge(s_mfu, k - 3)
                sp.dma_start(mfirst[:, k % 4, :], mod_w[0, k * P:(k + 1) * P, 0:2 * MC]).then_inc(s_first[k % 4], 16)

            first(0)
            for t in range(NT):
                sp.dma_start(xs[:, t, :], x[0, t * P:(t + 1) * P, :]).then_inc(s_x, 16)
                if t % 2:
                    first(1 + t // 2)
            for t in range(NTC):
                sp.dma_start(xc[:, t, :], ctx[0, t * P:(t + 1) * P, :]).then_inc(s_x, 16)
            for k in range(3, 8):
                first(k)
            cols_unit(0, w_in, 0)
            sp.dma_start(rcos[:, :, :], rope_cos.rearrange("(t p) n -> p t n", p=P)).then_inc(s_tab, 16)
            sp.dma_start(rsin[:, :, :], rope_sin.rearrange("(t p) n -> p t n", p=P)).then_inc(s_tab, 16)
            cols_unit(1, w_in, 256)

            s0 = QKV
            col = {"b": s0, "c": s0 + SCD, "z": s0 + 2 * SCD}
            for u in range(2, U_L0):
                sp.wait_ge(s_lo, 2 * (u - 2) + 2)
                if u == 2:
                    cols_unit(0, w_in, 512)
                elif u < 9:
                    jj, kind = divmod(u - 3, 3)
                    cols_unit(u % 2, w_in, col["czb"[kind]] + 256 * jj)
                else:
                    cols_unit(u % 2, w_out, 256 * (u - 9), order=(1, 0))
            sp.wait_ge(s_pv, STEPS // 2)
            for t in range(NT):
                sp.dma_start(xs[:, t, :], x[0, t * P:(t + 1) * P, :]).then_inc(s_x, 16)

            def ffn_loads(layer):
                hb = (B_FFN0, B_FFN1)[layer]
                wu = ffn_w_up[layer].rearrange("(k p) n -> p k n", p=P)
                wd = ffn_w_down[layer].rearrange("(j p) n -> p j n", p=P)

                def g_or_v(i, slot, off):
                    for a in range(2):
                        src = wu[:, 4 * a:4 * a + 4, bass.ds(i * 256 + off, 256)]
                        sp.dma_start(raw[slot][:, a, :].rearrange("p (k n) -> p k n", n=256), src).then_inc(s_raw[slot], 16)

                def dn_(i):
                    for a in range(2):
                        src = wd[:, bass.ds(i * 2 + a, 1), :].rearrange("p j n -> p (j n)")
                        sp.dma_start(raw[DS][:, a, :], src).then_inc(s_raw[DS], 16)

                def turn(i):
                    if isinstance(i, int) and i == 0:
                        sp.wait_ge(s_lo, hb if layer == 0 else hb - 2)
                        g_or_v(0, GS, 0)
                        sp.wait_ge(s_lo, hb)
                        g_or_v(0, VS, DFF)
                        return
                    first_turn = isinstance(i, int) and i == 1
                    sp.wait_ge(s_lo, hb + 3 if first_turn else hb + 6 * i - 2 - 1)
                    g_or_v(i, GS, 0)
                    if not first_turn:
                        sp.wait_ge(s_lo, hb + 6 * i - 5 + 0)
                    dn_(i - 1)
                    sp.wait_ge(s_lo, hb + 6 * i - 2)
                    g_or_v(i, VS, DFF)

                turn(0)
                turn(1)
                with sp.Fori(2, NPAIR - 1) as i:
                    turn(i)
                turn(NPAIR - 1)
                sp.wait_ge(s_lo, hb + 6 * NPAIR - 5)
                dn_(NPAIR - 1)

            ffn_loads(0)
            for u in range(U_L1):
                free = (B_L1 - 3, B_L1 - 2, B_L1)[u] if u < 3 else B_L1 + 2 * (u - 3) + 2
                sp.wait_ge(s_lo, free)
                slot = plan[B_L1 + 2 * u][0]
                if u < 4:
                    cols_unit(slot, mix_w_in[0], (SCD, SCD + 256, 0, 256)[u])
                elif u == 4:
                    load_unit(slot, [(raw[slot][:, 0, 0:256], dft_chan),
                                     (raw[slot][:, 1, 0:512].rearrange("p (g n) -> p g n", g=4),
                                      pool_w_grp[0].rearrange("g c n -> c g n"))])
                elif u < 7:
                    cols_unit(slot, dft_time, 256 * (u - 5))
                else:
                    cols_unit(slot, mix_w_out[0], 256 * (u - 7))
            ffn_loads(1)
            for t in range(NT):
                sp.wait_ge(s_xup, 4 * 3 + t + 1)
                sp.wait_ge(s_xur, 4 * 3 + t + 1)
                sp.dma_start(out[0, t * P:(t + 1) * P, :], xs[:, t, :]).then_inc(s_out, 16)
            sp.wait_ge(s_out, 16 * NT)

        @block.gpsimd
        def _(pool):
            nc.gpsimd.memset(ones[:, :], 1.0).then_inc(s_init, 1)
            nc.gpsimd.memset(mbias[:, :], 0.0).then_inc(s_init, 1)
            nc.gpsimd.memset(mhalf[:, :], -0.5).then_inc(s_init, 1)
            nc.gpsimd.memset(vH[:, :, :].bitcast(F32), 0.0).then_inc(s_init, 1)
            nc.gpsimd.memset(vL[:, :, :].bitcast(F32), 0.0).then_inc(s_init, 1)
            pool.wait_ge(s_init, 5)
            ch = Chain(pool, s_pc)

            def rstd(row, q, done):
                ch.link(nc.gpsimd.tensor_scalar(stat[:, row + 1, q:q + 1], stat[:, row, q:q + 1], 1.0 / D, EPS, ALU.mult, ALU.add))
                nc.gpsimd.tensor_tensor(stat[:, row + 2, q:q + 1], stat[:, row + 1, q:q + 1], mhalf[:, :], ALU.pow).then_inc(done, 1)

            def rstd_x(n):
                pool.wait_ge(s_sqx, n + 1)
                rstd(3, n, s_rsx)

            def h_high(n, b):
                pool.wait_ge(s_hf, 2 * n + b + 1)
                nc.gpsimd.tensor_scalar(norm_dst(0, n)[:, 4 * b:4 * b + 4, :], hf[:, b, :, :], 1.0, 0.0, ALU.mult, ALU.add).then_inc(s_hh, 1)

            for n in range(6):
                rstd_x(n)
            for n in range(6):
                for b in range(2):
                    h_high(n, b)

            chunks = [(0, 2, macc0), (0, 3, macc1), (0, 4, macc0), (0, 5, macc[:, 6, :])] + [(1, m, macc[:, m, :]) for m in range(6)]

            def mod_load(n):
                (l, m, _), k = chunks[n // KT], n % KT
                cols = slice(m * MC, (m + 1) * MC)
                if k == 0:
                    if n:
                        pool.wait_ge(s_msu, n - KT + 1)
                    pool.dma_start(mbias[0:1, :], mod_b[l:l + 1, cols]).then_inc(s_mb, 16)
                if n >= 2:
                    pool.wait_ge(s_msu, n - 1)
                pool.dma_start(mstage[:, n % 2, :], mod_w[l, k * P:(k + 1) * P, cols]).then_inc(s_ms[n % 2], 16)

            def mod_add(n):
                acc, k = chunks[n // KT][2], n % KT
                pool.wait_ge(s_ms[n % 2], 16 * (n // 2 + 1))
                if k == 0:
                    pool.wait_ge(s_mb, 16 * (n // KT + 1))
                if n == 2 * KT:
                    pool.wait_ge(s_msum, 2)
                nc.gpsimd.tensor_scalar(mstage[:, n % 2, :], mstage[:, n % 2, :], siluc[:, k:k + 1], 0.0, ALU.mult, ALU.add).then_inc(s_mp, 1)
                pool.wait_ge(s_mp, n + 1)
                if n:
                    pool.wait_ge(s_msu, n)
                nc.gpsimd.tensor_tensor(acc[:, :], mstage[:, n % 2, :], mbias[:, :] if k == 0 else acc[:, :], ALU.add).then_inc(s_msu, 1)

            def mod_tiles(lo, hi):
                for n in range(lo, lo + 2):
                    mod_load(n)
                for n in range(lo, hi):
                    mod_add(n)
                    if n + 2 < hi:
                        mod_load(n + 2)

            pool.wait_ge(s_rope, 14)
            mod_tiles(0, 3 * KT)

            def transition(e):
                for t in range(NT + 2):
                    if 1 <= t <= NT and e < 4:
                        rstd_x(norm_index(e, t - 1))
                    if t < NT:
                        pool.wait_ge(s_sqy, 4 * (e - 1) + t + 1)
                        rstd(0, 4 * (e - 1) + t, s_rsy)
                    if t >= 2 and e < 4:
                        h_high(norm_index(e, t - 2), 0)
                    if t < NT:
                        pool.wait_ge(s_yg, 4 * (e - 1) + t + 1)
                        nc.gpsimd.tensor_tensor(xs[:, t, D // 2:D], xs[:, t, D // 2:D], ys[:, t, D // 2:D], ALU.add).then_inc(s_xur, 1)
                    if t >= 2 and e < 4:
                        h_high(norm_index(e, t - 2), 1)

            transition(1)

            mod_tiles(3 * KT, 10 * KT)
            pool.wait_ge(s_yg, 4)
            pool.dma_start(gate[:, :], norm_g[0, 3:4, :].broadcast_to([P, D])).then_inc(s_gain, 16)
            pool.wait_ge(s_msu, 10 * KT)
            for n, g in enumerate((1, 3)):
                pool.dma_start(gate1[:, n, :], norm_g[1, g:g + 1, :].broadcast_to([P, D])).then_inc(s_gain, 16)
            for e in (2, 3, 4):
                transition(e)

        @block.scalar
        def _(act):
            for dst, src in ((ident[:, :], identity),
                             (vecs[80:92, :], sconv_w.rearrange("o w (r p) -> (o w r) p", p=P)),
                             (vecs[92:96, :], pool_scale.rearrange("o (r p) -> (o r) p", p=P))):
                act.dma_start(dst, src).then_inc(s_vecs, 16)
            for l in range(2):
                act.dma_start(vecf[0:3 * NJ, l, :], ffn_conv[l].rearrange("w (r p) -> (w r) p", p=P)).then_inc(s_vecf, 16)
            small = [
                (brow[:, :], mod_b[0:1, 0:2 * MC].broadcast_to([2, 2 * MC])),
                (sink[:, :], att_sink[0:1, :].broadcast_to([P, HEADS])),
                (edge[:, :, :], pool_edge.unsqueeze(0).broadcast_to([P, 4, 16])),
                (mask[:, :], attn_mask),
                (gate[:, :], norm_g[0, 1:2, :].broadcast_to([P, D])),
            ]
            for dst, src in small:
                act.dma_start(dst, src).then_inc(s_small, 16)
            ch = Chain(act, s_ac)

            written = {"junk": None}

            def square(dst, src, done, count):
                if written["junk"]:
                    act.wait_ge(*written["junk"])
                nc.scalar.activation(junk[:, :], src, ACT.Square, accum_out=dst).then_inc(done, 1)
                written["junk"] = (done, count)

            def h_tile(n):
                e = norm_cols(n)
                for b in range(2):
                    act.wait_ge(s_tr, 2 * n + b + 1)
                    W(act, s_hl, 2 * n + b - 1)
                    bank = norm_bank(n, b).rearrange("p (k n) -> p k n", n=P)
                    for k in range(4):
                        ins = nc.scalar.activation(hf[:, b, k, :], bank[:, k, :], ACT.Identity,
                                                   scale=scl[:, e, 4 * b + k:4 * b + k + 1], bias=shf[:, e, 4 * b + k:4 * b + k + 1])
                    ins.then_inc(s_hf, 1)

            act.wait_ge(s_vt, 1)
            nc.scalar.activation(siluc[:, :], up[0][:, 0:16], ACT.Silu).then_inc(s_silu, 1)
            for n in range(6):
                act.wait_ge(s_x, 96)
                square(stat[:, 3, n:n + 1], norm_src(n), s_sqx, n + 1)
            for h in range(3):
                if h < 2:
                    straight_high(act, h)
            act.wait_ge(s_scl, 2)
            for n in range(6):
                h_tile(n)
            straight_high(act, 2)

            def qk_high(n):
                act.wait_ge(s_qt, n + 1)
                if n < 8:
                    u, t = divmod(n, 4)
                    dst = qT[:, 4 * u:4 * u + 4, t * P:(t + 1) * P]
                    src = up[n % 2].rearrange("p (h n) -> p h n", n=P)
                else:
                    dst = kH[:, :, (n - 8) * P:(n - 7) * P]
                    src = up[n % 2][:, 0:2 * P].rearrange("p (h n) -> p h n", n=P)
                nc.scalar.activation(dst, src, ACT.Copy).then_inc(s_qh, 1)

            def v_high(t):
                last_of(act, s_row, t, 6, 5, 6)
                act.wait_ge(s_init, 5)
                bank = dn[t] if t < 4 else up[t - 2]
                dst = vH[:, t, 64:320].rearrange("p (h n) -> p h n", n=P)[:, :, 0:HD]
                nc.scalar.activation(dst, bank[:, P:2 * P].rearrange("p (h n) -> p h n", n=HD), ACT.Copy).then_inc(s_vh, 1)

            straight_high(act, 3)
            straight_high(act, 4)
            for n in range(4):
                qk_high(n)
            straight_high(act, 5)
            straight_high(act, 6)
            for n in range(4, 8):
                qk_high(n)
            straight_high(act, 7)
            for t in range(6):
                v_high(t)
            straight_high(act, 8)
            for n in range(8, 14):
                qk_high(n)

            nsh = [0]
            for s in range(STEPS + 4):
                for n, (job, _, _) in enumerate(JOBS):
                    if job_end(n) == s - 1 and job[0] != "m":
                        nsh[0] += 1
                        straight_high(act, 6 + nsh[0] + 2)
                if s < STEPS:
                    b, kv, e, w = step_of(s)
                    head = 4 * kv + e + 2 * w
                    nk = (keys_of(b)[1] + 2) * P
                    act.wait_ge(s_max, s + 1)
                    nc.scalar.activation(prob[:, s % 3, 0:nk], prob[:, s % 3, 0:nk], ACT.Exp, bias=att[:, s, 1:2],
                                         scale=SCALE, accum_out=att[:, s, 2:3])
                    nc.scalar.activation(att[:, s, 3:4], sink[:, head:head + 1], ACT.Exp, bias=att[:, s, 1:2]).then_inc(s_exp, 1)
                for n, (job, _, _) in enumerate(JOBS):
                    if job_end(n) == s and job[0] != "m":
                        kind, jj, a = job
                        if kind == "c":
                            act.wait_ge(s_used, half_of[n] + 1)
                            W(act, s_cv, 2 * (jj - 1) + a + 1)
                            nc.scalar.activation(czb[:, a, 1:T + 1], job_bank[n % 2], ACT.Copy).then_inc(s_jobf, 1)
                        elif kind == "z":
                            act.wait_ge(s_cz, 2 * jj + a + 1)
                            W(act, s_sl, 2 * (jj - 1) + a + 1)
                            f = 80 + 4 + 2 * jj + a
                            nc.scalar.activation(cvt[:, a, :], czb[:, a, 1:T + 1], ACT.Copy, scale=cols[:, f:f + 1]).then_inc(s_cz1, 1)
                        else:
                            act.wait_ge(s_bs, 2 * jj + a + 1)
                            nc.scalar.activation(aTh[:, 4 + 2 * jj + a, :], cvt[:, a, :], ACT.Copy).then_inc(s_sh, 1)
                if 2 <= s < STEPS + 2:
                    r = s - 2
                    nb = keys_of(step_of(r)[0])[1] + 2
                    act.wait_ge(s_pt, r + 1)
                    W(act, s_pv, r // 2)
                    src = ps[:, 0:2, :].rearrange("p b n -> p (b n)")[:, 0:nb * P].rearrange("p (j n) -> p j n", n=P)
                    nc.scalar.activation(pTh[:, 0:nb, r % 2, :], src, ACT.Copy).then_inc(s_ph, 1)
                if s >= 7 and (s - 7) % 4 == 0:
                    o = (s - 7) // 4
                    act.wait_ge(s_pv, 2 * o + 2)
                    b, kv = divmod(o, 2)
                    nc.scalar.activation(aTh[:, 2 * kv:2 * kv + 2, b * P:(b + 1) * P],
                                         pv_bank[o % 2][:, 0:2 * P].rearrange("p (w n) -> p w n", n=P), ACT.Copy).then_inc(s_ah, 1)
                if 1 <= s < STEPS + 1:
                    nk = (keys_of(step_of(s - 1)[0])[1] + 2) * P
                    act.wait_ge(s_inv, s)
                    nc.scalar.activation(prob[:, (s - 1) % 3, 0:nk], prob[:, (s - 1) % 3, 0:nk], ACT.Copy, scale=att[:, s - 1, 3:4]).then_inc(s_pn, 1)

            def transition(e, splits):
                for t in range(NT + 2):
                    if 1 <= t <= NT and e < 4:
                        act.wait_ge(s_xup, 4 * (e - 1) + t)
                        act.wait_ge(s_xur, 4 * (e - 1) + t)
                        n = norm_index(e, t - 1)
                        square(stat[:, 3, n:n + 1], xs[:, t - 1, :], s_sqx, n + 1)
                    if t < NT:
                        q = 4 * (e - 1) + t
                        y_wait(act, e, t)
                        square(stat[:, 0, q:q + 1], ys[:, t, :], s_sqy, q + 1)
                    for h in splits.get(t, ()):
                        straight_high(act, h)
                    if t >= 2 and e < 4:
                        h_tile(norm_index(e, t - 2))

            def ffn(layer):
                hb = (B_FFN0, B_FFN1)[layer]

                def centre(i, jj):
                    h, dh = ffn_half(layer, i, ("g0", "g1")[jj])
                    act.wait_ge(s_used, h + 1 + dh)
                    act.wait_ge(s_cw, NPAIR * layer + i + 1)
                    W(act, s_si, 2 * NPAIR * layer + 2 * i + jj - 1)
                    nc.scalar.activation(conv[:, jj, :], up[jj], ACT.Copy, scale=cw[:, 3 * jj + 1:3 * jj + 2]).then_inc(s_g1, 1)

                def silu(i, jj):
                    act.wait_ge(s_gc, 2 * NPAIR * layer + 2 * i + jj + 1)
                    W(act, s_am, 2 * NPAIR * layer + 2 * i + jj - 1)
                    nc.scalar.activation(sil[:, jj, :], conv[:, jj, :], ACT.Silu).then_inc(s_si, 1)

                def act_high(i, jj):
                    act.wait_ge(s_am, 2 * NPAIR * layer + 2 * i + jj + 1)
                    if not (isinstance(i, int) and i == 0):
                        act.wait_ge(s_used, hb + 6 * i + 1)
                    nc.scalar.activation(actH[:, jj, :], actF[:, jj, :], ACT.Copy).then_inc(s_ahh, 1)

                def turn(i, last=False):
                    zero = isinstance(i, int) and i == 0
                    if not zero:
                        ffn_split(act, "high", layer, i - 1, "d1")
                        act_high(i - 1, 1)
                    centre(i, 0)
                    if not zero:
                        ffn_split(act, "high", layer, i, "v0")
                    silu(i, 0)
                    if not zero:
                        ffn_split(act, "high", layer, i, "g1")
                    ffn_split(act, "high", layer, i, "v1")
                    act_high(i, 0)
                    centre(i, 1)
                    silu(i, 1)
                    if not last:
                        ffn_split(act, "high", layer, i + 1, "g0")
                    ffn_split(act, "high", layer, i, "d0")

                turn(0)
                with act.Fori(1, NPAIR - 1) as i:
                    turn(i)
                turn(NPAIR - 1, last=True)
                ffn_split(act, "high", layer, NPAIR - 1, "d1")
                act_high(NPAIR - 1, 1)

            def y_wait(eng, e, t):
                if e in (1, 3):
                    eng.wait_ge(s_rowf, 16 * (e // 2) + 3 * NT + t + 1)
                else:
                    eng.wait_ge(s_ya, 8 * NPAIR * (e // 2) - 8 + 2 * t + 2)

            for h in range(2 * 9 + 3, B_FFN0 + 2):
                straight_high(act, h)
            transition(1, {4: [B_FFN0 + 2]})
            ffn(0)
            straight_high(act, B_L1)
            transition(2, {3: [B_L1 + 1], 4: [B_L1 + 2]})
            for n in range(4):
                act.wait_ge(s_used, B_L1 + n + 1)
                nc.scalar.activation(xTh[:, n, :], up[n], ACT.Copy).then_inc(s_xh, 1)
                straight_high(act, B_L1 + 3 + n)
            for g in range(4):
                act.wait_ge(s_used, B_L1 + 4 + g + 1)
                act.wait_ge(s_init, 7)
                W(act, s_pw, g)
                nc.scalar.activation(pu[:, 0, 8:T + 8], up[g], ACT.Copy).then_inc(s_u, 1)
                straight_high(act, B_L1 + 7 + g)
                act.wait_ge(s_pw, g + 1)
                nc.scalar.activation(bTh[:, g, :], pu[:, 2 if g % 2 == 0 else 1, 0:T], ACT.Copy).then_inc(s_pih, 1)
            for n in range(16):
                tt, g = divmod(n, 4)
                last_of(act, s_ca, n, 16, B_L1 + 8)
                dst = xcsH[:, :, g * P:(g + 1) * P].rearrange("p (s t) n -> p s t n", s=2)[:, :, tt, :]
                nc.scalar.activation(dst, dn[n % 4][:, 0:256].rearrange("p (s n) -> p s n", n=P), ACT.Copy).then_inc(s_cah, 1)
            straight_high(act, B_L1 + 11)
            for g in range(4):
                last_of(act, s_pg, g, 4, B_L1 + 9)
                W(act, s_pgl, g - 1)
                ch.link(nc.scalar.activation(hf[:, g % 2, :, :].rearrange("p k n -> p (k n)"), up[g], ACT.Copy, scale=cols[:, 92 + g:93 + g]))
                nc.scalar.activation(bTh[:, g, :], hf[:, g % 2, :, :].rearrange("p k n -> p (k n)"), ACT.Copy).then_inc(s_pgh, 1)
            straight_high(act, B_L1 + 12)
            for ck in range(2):
                straight_high(act, B_L1 + 13 + 2 * ck)
                for g in range(4):
                    last_of(act, s_td, g, 4, B_L1 + 11 + 2 * ck, 3 * ck)
                    nc.scalar.activation(bTh[:, 4 + g, ck * 256:(ck + 1) * 256], dn[g][:, 0:256], ACT.Copy).then_inc(s_tdh, 1)
                straight_high(act, B_L1 + 14 + 2 * ck)
            for h in range(B_L1 + 17, B_FFN1 + 2):
                straight_high(act, h)
            transition(3, {4: [B_FFN1 + 2]})
            ffn(1)
            transition(4, {})


        @block.vector
        def _(dve):
            ch = Chain(dve, s_vc)

            dve.wait_ge(s_vt, 3)
            dve.wait_ge(s_silu, 1)
            ch.link(nc.vector.tensor_copy(cols[:, :], up[0][:, 0:96]))
            for l in range(2):
                nc.vector.tensor_copy(convc[:, l, :, :].rearrange("p j w -> p w j"),
                                      up[1 + l][:, 0:3 * NJ].rearrange("p (w j) -> p w j", w=3)).then_inc(s_cols, 1)

            def xn(n, dst, src):
                dve.wait_ge(s_rsx, n + 1)
                nc.vector.tensor_scalar(dst, src, stat[:, 5, n:n + 1], None, ALU.mult).then_inc(s_xn, 1)

            def h_low(n, b):
                dve.wait_ge(s_hh, 2 * n + b + 1)
                nc.vector.tensor_sub(norm_dst(1, n)[:, 4 * b:4 * b + 4, :], hf[:, b, :, :],
                                     norm_dst(0, n)[:, 4 * b:4 * b + 4, :].bitcast(F32)).then_inc(s_hl, 1)

            for n in range(6):
                xn(n, norm_src(n), norm_src(n))
            straight_low(dve, 0)
            straight_low(dve, 1)
            dve.wait_ge(s_small, 16 * 5)
            dve.wait_ge(s_mr, 1)
            for n in range(4):
                ins = nc.vector.tensor_tensor(mrow[:, n * 512:(n + 1) * 512], dn[n][0:2, :], brow[:, n * 512:(n + 1) * 512], ALU.add)
            ins.then_inc(s_mrb, 1)
            dve.wait_ge(s_mrt, 1)
            ch.link(nc.vector.tensor_copy(modc[:, :, :], dn[0][:, 0:32].rearrange("p (k v) -> p k v", v=2)))
            for v in range(2):
                nc.vector.tensor_copy(shf[:, 4 * v, :], modc[:, 0:KT, v])
                nc.vector.scalar_tensor_tensor(out=scl[:, 4 * v, :], in0=modc[:, KT:2 * KT, v], scalar=1.0, in1=cols[:, 16:24],
                                               op0=ALU.add, op1=ALU.mult).then_inc(s_scl, 1)
            for n in range(6):
                for b in range(2):
                    h_low(n, b)
            straight_low(dve, 2)

            rp = lambda ap: ap.rearrange("p (h r f) -> p h r f", r=2, f=16)

            def rope(n, bank, t, width):
                W(dve, s_qt, n - 3)
                W(dve, s_rope, n)
                nh = width // HD
                src = rp(bank[:, 0:width])
                cs, sn = rp(rcos[:, t, 0:width]), rp(rsin[:, t, 0:width])
                nc.vector.tensor_tensor(rt[:, 0, 0:width], bank[:, 0:width], rcos[:, t, 0:width], ALU.mult)
                for r in range(2):
                    ins = nc.vector.tensor_tensor(rp(rt[:, 1, 0:width])[:, :, r, :], src[:, :, 1 - r, :], sn[:, :, r, :], ALU.mult)
                return ins, nh

            def rope_add(n, nh):
                wide = lambda a: rt[:, a, 0:nh * HD].rearrange("p (h o d) -> p h o d", o=1, d=HD).broadcast_to([P, nh, 2, HD])
                nc.vector.tensor_tensor(qd[:, n % 4, 0:nh, :].rearrange("p h (o d) -> p h o d", o=2), wide(0), wide(1), ALU.add).then_inc(s_rope, 1)

            def rope_q(n):
                u, t = divmod(n, 4)
                last_of(dve, s_row, t, 4, 2 * u + 1, 3 * u)
                ins, nh = rope(n, dn[t], t, 256)
                ch.link(ins)
                rope_add(n, nh)

            def qk_low(n):
                dve.wait_ge(s_qh, n + 1)
                if n < 8:
                    u, t = divmod(n, 4)
                    dst = qT[64:P, 4 * u:4 * u + 4, t * P:(t + 1) * P]
                    nc.vector.tensor_sub(dst, up[n % 2][64:P, :].rearrange("p (h n) -> p h n", n=P), dst.bitcast(F32)).then_inc(s_ql, 1)
                else:
                    c0 = (n - 8) * P
                    nc.vector.tensor_sub(kL[:, :, c0:c0 + P], up[n % 2][:, 0:2 * P].rearrange("p (h n) -> p h n", n=P),
                                         kH[:, :, c0:c0 + P].bitcast(F32)).then_inc(s_ql, 1)

            ch.link(nc.vector.tensor_scalar(nsink[:, :], sink[:, :], -1.0, None, ALU.mult))
            dve.wait_ge(s_tab, 32)
            for n in range(4):
                rope_q(n)
            straight_low(dve, 3)
            straight_low(dve, 4)
            for n in range(4):
                qk_low(n)
            straight_low(dve, 5)
            for n in range(4, 8):
                rope_q(n)
            straight_low(dve, 6)
            for n in range(4, 8):
                qk_low(n)
            for t in range(6):
                n = 8 + t
                bank = dn[t] if t < 4 else up[t - 2]
                dve.wait_ge(s_vh, t + 1)
                if t < 4:
                    ins, nh = rope(n, bank, t, P)
                    ch.link(ins)
                    rope_add(n, nh)
                else:
                    W(dve, s_qt, n - 3)
                    nc.vector.tensor_copy(qd[:, n % 4, 0:2, :].rearrange("p h (o d) -> p h o d", o=2),
                                          bank[:, 0:P].rearrange("p (h o d) -> p h o d", o=1, d=HD).broadcast_to([P, 2, 2, HD])).then_inc(s_rope, 1)
                vv = lambda z: z[:, t, 64:320].rearrange("p (h n) -> p h n", n=P)[:, :, 0:HD]
                nc.vector.tensor_sub(vv(vL), bank[:, P:2 * P].rearrange("p (h n) -> p h n", n=HD), vv(vH).bitcast(F32)).then_inc(s_vl, 1)
                if t:
                    qk_low(n - 1)
            qk_low(13)
            straight_low(dve, 7)
            straight_low(dve, 8)
            nc.vector.memset(czb[:, :, 0:1], 0.0)
            ch.link(nc.vector.memset(czb[:, :, T + 1:T + 2], 0.0))

            def fin(n, bank, dst_kind, hh, tile):
                dve.wait_ge(s_msum, n + 1)
                if dst_kind == "gate":
                    nc.vector.tensor_tensor(tile[:, hh * 512:(hh + 1) * 512], bank, tile[:, hh * 512:(hh + 1) * 512], ALU.mult).then_inc(s_mfin, 1)
                    return
                W(dve, s_mfin, n)
                for k in range(4):
                    kk = 4 * hh + k
                    dst = mcol[:, kk:kk + 1] if dst_kind == "scale" else shf[:, tile, kk:kk + 1]
                    ins = nc.vector.tensor_tensor_reduce(junkc[:, k, :], bank[:, k * P:(k + 1) * P], ident[:, :], 1.0, 0.0, ALU.mult, ALU.add, dst)
                ins.then_inc(s_mfin, 1)
                if dst_kind == "scale" and hh == 1:
                    e, g0 = tile
                    dve.wait_ge(s_mfin, n + 1)
                    ch.link(nc.vector.scalar_tensor_tensor(out=scl[:, e, :], in0=mcol[:, :], scalar=1.0, in1=cols[:, g0:g0 + KT],
                                                           op0=ALU.add, op1=ALU.mult))

            nsl = [0]
            for s in range(STEPS + 4):
                if s < STEPS:
                    b, kv, e, w = step_of(s)
                    head = 4 * kv + e + 2 * w
                    lo, nw = keys_of(b)
                    nk = (nw + 2) * P
                    dve.wait_ge(s_sc, s + 1)
                    W(dve, s_pt, s - 2)
                    m0 = {0: P, NT - 1: 5 * P}.get(b, 0)
                    src = ps[:, 4:6, :].rearrange("p b n -> p (b n)")[:, 512 - nw * P:768]
                    ch.link(nc.vector.tensor_tensor_reduce(prob[:, s % 3, 0:nk], src, mask[:, m0:m0 + nk], 1.0, -3e38, ALU.add, ALU.max, att[:, s, 0:1]))
                    nc.vector.scalar_tensor_tensor(out=att[:, s, 1:2], in0=att[:, s, 0:1], scalar=-SCALE, in1=nsink[:, head:head + 1],
                                                   op0=ALU.mult, op1=ALU.min).then_inc(s_max, 1)
                if 1 <= s < STEPS + 1:
                    r = s - 1
                    dve.wait_ge(s_exp, r + 1)
                    ch.link(nc.vector.tensor_tensor(att[:, r, 0:1], att[:, r, 2:3], att[:, r, 3:4], ALU.add))
                    nc.vector.reciprocal(att[:, r, 3:4], att[:, r, 0:1]).then_inc(s_inv, 1)
                for n, (job, _, _) in enumerate(JOBS):
                    if job_end(n) == s - 1 and job[0] != "m":
                        nsl[0] += 1
                        straight_low(dve, 6 + nsl[0] + 2)
                for n, (job, _, _) in enumerate(JOBS):
                    if job_end(n) == s:
                        kind, jj, a = job
                        if kind == "m":
                            fin(2 * (jj - 2) + a, job_bank[n % 2], {2: "gate", 3: "shift", 4: "scale"}[jj], a, {2: gate, 3: 1, 4: (1, 16 + 2 * KT)}[jj])
                        elif kind == "z":
                            dve.wait_ge(s_used, half_of[n] + 1)
                            dve.wait_ge(s_jobf, 2 * jj + a + 1)
                            nc.vector.tensor_tensor(czb[:, a, 1:T + 1], job_bank[n % 2], czb[:, a, 1:T + 1], ALU.mult).then_inc(s_cz, 1)
                        elif kind == "b":
                            dve.wait_ge(s_used, half_of[n] + 1)
                            dve.wait_ge(s_cv, 2 * jj + a + 1)
                            nc.vector.tensor_tensor(cvt[:, a, :], job_bank[n % 2], cvt[:, a, :], ALU.mult).then_inc(s_bs, 1)
                if 2 <= s < STEPS + 2:
                    r = s - 2
                    nb = keys_of(step_of(r)[0])[1] + 2
                    dve.wait_ge(s_ph, r + 1)
                    src = ps[:, 0:2, :].rearrange("p b n -> p (b n)")[:, 0:nb * P].rearrange("p (j n) -> p j n", n=P)
                    nc.vector.tensor_sub(pTl[:, 0:nb, r % 2, :], src, pTh[:, 0:nb, r % 2, :].bitcast(F32)).then_inc(s_pl, 1)
                for n, (job, _, _) in enumerate(JOBS):
                    if job_end(n) == s:
                        kind, jj, a = job
                        if kind == "z":
                            dve.wait_ge(s_cz1, 2 * jj + a + 1)
                            for tap in (0, 2):
                                f = 80 + 4 * tap + 2 * jj + a
                                ins = nc.vector.scalar_tensor_tensor(out=cvt[:, a, :], in0=czb[:, a, tap:tap + T], scalar=cols[:, f:f + 1],
                                                                     in1=cvt[:, a, :], op0=ALU.mult, op1=ALU.add)
                                if tap == 0:
                                    ch.link(ins)
                            ins.then_inc(s_cv, 1)
                        elif kind == "b":
                            dve.wait_ge(s_sh, 2 * jj + a + 1)
                            nc.vector.tensor_sub(aTl[:, 4 + 2 * jj + a, :], cvt[:, a, :], aTh[:, 4 + 2 * jj + a, :].bitcast(F32)).then_inc(s_sl, 1)
                if s >= 7 and (s - 7) % 4 == 0:
                    o = (s - 7) // 4
                    b, kv = divmod(o, 2)
                    dve.wait_ge(s_ah, o + 1)
                    d_ = lambda z: z[:, 2 * kv:2 * kv + 2, b * P:(b + 1) * P]
                    nc.vector.tensor_sub(d_(aTl), pv_bank[o % 2][:, 0:2 * P].rearrange("p (w n) -> p w n", n=P), d_(aTh).bitcast(F32)).then_inc(s_al, 1)

            def gate_of(e):
                return gate[:, :] if e < 3 else gate1[:, e - 3, :]

            def update(e, t):
                q = 4 * (e - 1) + t
                dve.wait_ge(s_rsy, q + 1)
                nc.vector.scalar_tensor_tensor(out=ys[:, t, :], in0=ys[:, t, :], scalar=stat[:, 2, q:q + 1], in1=gate_of(e),
                                               op0=ALU.mult, op1=ALU.mult).then_inc(s_yg, 1)
                if e == 1:
                    dve.wait_ge(s_x, 16 * 10)
                dve.wait_ge(s_yg, q + 1)
                nc.vector.tensor_tensor(xs[:, t, 0:D // 2], xs[:, t, 0:D // 2], ys[:, t, 0:D // 2], ALU.add).then_inc(s_xup, 1)

            def norm_x(e, t):
                dve.wait_ge(s_xup, 4 * (e - 1) + t + 1)
                xn(norm_index(e, t), ys[:, t, :], xs[:, t, :])

            def transition(e, pieces, splits):
                for t in range(NT + 3):
                    if t >= 3 and e < 4:
                        h_low(norm_index(e, t - 3), 1)
                    if t < NT:
                        pieces(t)
                    for h in splits.get(t, ()):
                        straight_low(dve, h)
                    if 1 <= t <= NT and e < 4:
                        norm_x(e, t - 1)
                    if t < NT and e < 4:
                        update(e, t)
                    if 1 <= t <= NT and e == 4:
                        update(e, t - 1)
                    if 2 <= t < NT + 2 and e < 4:
                        h_low(norm_index(e, t - 2), 0)

            def out_projection(e, h0):
                k = 0
                for u in range(3):
                    straight_low(dve, h0 + k)
                    k += 1
                    for t in range(NT):
                        last_of(dve, s_row, t, NT, h0 - 3 + 2 * u + 1, rows_before[e] + 3 * u)
                        nc.vector.tensor_copy(ys[:, t, 256 * u:256 * (u + 1)], dn[t][:, 0:256]).then_inc(s_rowf, 1)
                    straight_low(dve, h0 + k)
                    k += 1
                straight_low(dve, h0 + k)

                def piece(t):
                    last_of(dve, s_row, t, NT, h0 - 3 + 7, rows_before[e] + 9)
                    nc.vector.tensor_copy(ys[:, t, 768:1024], dn[t][:, 0:256]).then_inc(s_rowf, 1)
                return piece

            piece = out_projection(1, 21)
            transition(1, piece, {4: [B_FFN0 + 2]})

            def ffn(layer):
                hb = (B_FFN0, B_FFN1)[layer]
                jb = 2 * NPAIR * layer
                pb = 8 * NPAIR * layer

                def taps(i):
                    if isinstance(i, int):
                        src = convc[:, layer, 2 * i:2 * i + 2, :]
                    else:
                        src = convc[:, layer, bass.ds(i * 2, 2), :]
                    nc.vector.tensor_copy(cw[:, :].rearrange("p (j w) -> p j w", w=3), src).then_inc(s_cw, 1)

                def other_taps(i, jj):
                    dve.wait_ge(s_g1, jb + 2 * i + jj + 1)
                    ch.link(nc.vector.scalar_tensor_tensor(out=conv[:, jj, 1:T], in0=up[jj][:, 0:T - 1], scalar=cw[:, 3 * jj:3 * jj + 1],
                                                           in1=conv[:, jj, 1:T], op0=ALU.mult, op1=ALU.add))
                    nc.vector.scalar_tensor_tensor(out=conv[:, jj, 0:T - 1], in0=up[jj][:, 1:T], scalar=cw[:, 3 * jj + 2:3 * jj + 3],
                                                   in1=conv[:, jj, 0:T - 1], op0=ALU.mult, op1=ALU.add).then_inc(s_gc, 1)

                def gated(i, jj):
                    h, dh = ffn_half(layer, i, ("v0", "v1")[jj])
                    dve.wait_ge(s_used, h + 1 + dh)
                    dve.wait_ge(s_si, jb + 2 * i + jj + 1)
                    nc.vector.tensor_tensor(actF[:, jj, :], up[2 + jj], sil[:, jj, :], ALU.mult).then_inc(s_am, 1)

                def act_low(i, jj):
                    dve.wait_ge(s_ahh, jb + 2 * i + jj + 1)
                    nc.vector.tensor_sub(actL[:, jj, :], actF[:, jj, :], actH[:, jj, :].bitcast(F32)).then_inc(s_all, 1)

                def add_piece(i, p):
                    t, hh = divmod(p, 2)
                    if p < 7:
                        dve.wait_ge(s_dp, 7 * NPAIR * layer + 7 * i + p + 1)
                    else:
                        h, dh = ffn_half(layer, i, "d1")
                        dve.wait_ge(s_used, h + 1 + dh)
                    dst = ys[:, t, hh * 512:(hh + 1) * 512]
                    if isinstance(i, int) and i == 0:
                        nc.vector.tensor_copy(dst, dn[p % 3]).then_inc(s_ya, 1)
                    else:
                        nc.vector.tensor_tensor(dst, dn[p % 3], dst, ALU.add).then_inc(s_ya, 1)

                def turn(i, jobs=None, last=False):
                    zero = isinstance(i, int) and i == 0
                    if not zero:
                        gated(i - 1, 1)
                        ffn_split(dve, "low", layer, i - 1, "d1")
                        act_low(i - 1, 1)
                        if jobs:
                            jobs("g0")
                    taps(i)
                    other_taps(i, 0)
                    if not zero:
                        for p in range(8):
                            add_piece(i - 1, p)
                            if jobs and p in (2, 5):
                                jobs("d", p // 3)
                            if p == 3:
                                ffn_split(dve, "low", layer, i, "v0")
                        ffn_split(dve, "low", layer, i, "g1")
                    ffn_split(dve, "low", layer, i, "v1")
                    if jobs:
                        jobs("v0")
                    gated(i, 0)
                    act_low(i, 0)
                    if jobs:
                        jobs("g1")
                    other_taps(i, 1)
                    if not last:
                        ffn_split(dve, "low", layer, i + 1, "g0")
                    ffn_split(dve, "low", layer, i, "d0")
                    if jobs:
                        jobs("v1")

                turn(0)
                turn(1)
                ch.loop(2, NPAIR - 1, 2, turn)
                if layer == 0:
                    kinds = {0: ("shift", 2), 1: ("scale", (2, 16 + 4 * KT)), 2: ("gate", gate1[:, 0, :]),
                             3: ("shift", 3), 4: ("scale", (3, 16 + 6 * KT)), 5: ("gate", gate1[:, 1, :]), 6: ("gate", gate)}

                    def jobs(what, only=None):
                        for n in ffn_jobs[what] if only is None else ffn_jobs[what][only:only + 1]:
                            m, hh = divmod(n, 2)
                            k, where = kinds[m]
                            if k == "gate":
                                dve.wait_ge(s_gain, 16 * 3)
                            fin(6 + n, dn[3], k, hh, where)
                    turn(NPAIR - 1, jobs=jobs, last=True)
                else:
                    turn(NPAIR - 1, last=True)
                i = NPAIR - 1
                gated(i, 1)
                ffn_split(dve, "low", layer, i, "d1")
                act_low(i, 1)

                def piece(t):
                    add_piece(i, 2 * t)
                    add_piece(i, 2 * t + 1)
                return piece

            piece = ffn(0)
            straight_low(dve, B_L1)
            transition(2, piece, {4: [B_L1 + 1, B_L1 + 2]})

            nc.vector.memset(pu[:, 0, 0:8], 0.0).then_inc(s_init, 1)
            nc.vector.memset(pu[:, 0, T + 8:T + 16], 0.0).then_inc(s_init, 1)
            for n in range(4):
                dve.wait_ge(s_xh, n + 1)
                nc.vector.tensor_sub(xTl[:, n, :], up[n], xTh[:, n, :].bitcast(F32)).then_inc(s_xl, 1)
                straight_low(dve, B_L1 + 3 + n)
            for g, w in enumerate(WINDOWS):
                dve.wait_ge(s_u, g + 1)
                dve.wait_ge(s_init, 7)
                W(dve, s_pil, g)
                src, length, span, n = pu[:, 0, :], T + 16, 1, 0
                while span < w:
                    length -= span
                    dst = pu[:, 1 + n % 2, :]
                    ch.link(nc.vector.tensor_tensor(dst[:, 0:length], src[:, 0:length], src[:, span:span + length], ALU.add))
                    src, span, n = dst, 2 * span, n + 1
                o = 8 - w // 2
                nc.vector.tensor_tensor(src[:, o:o + 8], src[:, o:o + 8], edge[:, g, 0:8], ALU.mult)
                ch.link(nc.vector.tensor_tensor(src[:, o + T - 8:o + T], src[:, o + T - 8:o + T], edge[:, g, 8:16], ALU.mult))
                nc.vector.scalar_tensor_tensor(out=pu[:, 1 + n % 2, 0:T], in0=src[:, o:o + T], scalar=1.0 / w, in1=pu[:, 0, 8:T + 8],
                                               op0=ALU.mult, op1=ALU.subtract).then_inc(s_pw, 1)
                dve.wait_ge(s_pih, g + 1)
                nc.vector.tensor_sub(bTl[:, g, :], pu[:, 1 + n % 2, 0:T], bTh[:, g, :].bitcast(F32)).then_inc(s_pil, 1)
                straight_low(dve, B_L1 + 7 + g)
            for n in range(16):
                tt, g = divmod(n, 4)
                dve.wait_ge(s_cah, n + 1)
                d_ = lambda z: z[:, :, g * P:(g + 1) * P].rearrange("p (s t) n -> p s t n", s=2)[:, :, tt, :]
                nc.vector.tensor_sub(d_(xcsL), dn[n % 4][:, 0:256].rearrange("p (s n) -> p s n", n=P), d_(xcsH).bitcast(F32)).then_inc(s_cal, 1)
            straight_low(dve, B_L1 + 11)
            for g in range(4):
                dve.wait_ge(s_pgh, g + 1)
                nc.vector.tensor_sub(bTl[:, g, :], hf[:, g % 2, :, :].rearrange("p k n -> p (k n)"), bTh[:, g, :].bitcast(F32)).then_inc(s_pgl, 1)
            straight_low(dve, B_L1 + 12)
            for ck in range(2):
                straight_low(dve, B_L1 + 13 + 2 * ck)
                for g in range(4):
                    dve.wait_ge(s_tdh, 4 * ck + g + 1)
                    nc.vector.tensor_sub(bTl[:, 4 + g, ck * 256:(ck + 1) * 256], dn[g][:, 0:256],
                                         bTh[:, 4 + g, ck * 256:(ck + 1) * 256].bitcast(F32)).then_inc(s_tdl, 1)
                straight_low(dve, B_L1 + 14 + 2 * ck)
            piece = out_projection(3, B_L1 + 17)
            transition(3, piece, {4: [B_FFN1 + 2]})
            piece = ffn(1)
            transition(4, piece, {})

        @block.tensor
        def _(pe):
            def three(dst, ah, al, bh, bl, start, stop):
                nc.tensor.matmul(dst, ah, bh, start=start, stop=False)
                nc.tensor.matmul(dst, ah, bl, start=False, stop=False)
                return nc.tensor.matmul(dst, al, bh, start=False, stop=stop)

            def norm_transposes(n):
                pe.wait_ge(s_xn, n + 1)
                W(pe, s_hf, 2 * (n - 2) + 2)
                for b in range(2):
                    for k in range(4):
                        ins = nc.tensor.transpose(norm_bank(n, b)[:, k * P:(k + 1) * P],
                                                  norm_src(n)[:, (4 * b + k) * P:(4 * b + k + 1) * P], ident[:, :])
                    ins.then_inc(s_tr, 1)

            pe.wait_ge(s_vecs, 16 * 6)
            nc.tensor.transpose(up[0][:, 0:96], vecs[0:96, :], ident[0:96, 0:96]).then_inc(s_vt, 1)
            pe.wait_ge(s_vecf, 16 * 2)
            for l in range(2):
                nc.tensor.transpose(up[1 + l][:, 0:3 * NJ], vecf[0:3 * NJ, l, :], ident[0:3 * NJ, 0:3 * NJ]).then_inc(s_vt, 1)
            pe.wait_ge(s_silu, 1)
            sc = siluc[:, :].rearrange("p (v k) -> p k v", v=2)
            for k in range(KT):
                pe.wait_ge(s_first[k % 4], 16 * (k // 4 + 1))
                for n in range(4):
                    ins = nc.tensor.matmul(dn[n][0:2, :], sc[:, k, :], mfirst[:, k % 4, n * 512:(n + 1) * 512], start=(k == 0), stop=(k == KT - 1))
                ins.then_inc(s_mr if k == KT - 1 else s_mfu, 1)
                if k == 3:
                    pe.wait_ge(s_cols, 2)
                    norm_transposes(0)
                    norm_transposes(1)
            pe.wait_ge(s_mrb, 1)
            for k in range(16):
                ins = nc.tensor.transpose(dn[0][:, 2 * k:2 * k + 2], mrow[:, k * P:(k + 1) * P], ident[0:2, 0:2])
            ins.then_inc(s_mrt, 1)
            for n in range(2, 6):
                norm_transposes(n)

            def stat_qkv(which):
                def f(r, k):
                    z, zc = ((hTh, hcTh), (hTl, hcTl))[which]
                    return z[:, k, r * P:(r + 1) * P] if r < 4 else zc[:, k, (r - 4) * P:(r - 3) * P]
                return f

            def qk_transposes(n):
                pe.wait_ge(s_rope, n + 1)
                W(pe, s_ql, n - 1) if n >= 2 else pe.wait_ge(s_hf, 12)
                for h in range(4 if n < 8 else 2):
                    ins = nc.tensor.transpose(up[n % 2][:, h * P:(h + 1) * P], qd[:, n % 4, h, :], ident[:, :])
                ins.then_inc(s_qt, 1)

            banks6 = dn + up[2:4]
            for u in range(3):
                for a in range(2):
                    def before(r, u=u, a=a):
                        if a == 0:
                            if u == 0:
                                pe.wait_ge(s_hl, 2 * (r + 1))
                                if r == 0:
                                    pe.wait_ge(s_scl, 2)
                            elif r < 4:
                                pe.wait_ge(s_rope, 4 * (u - 1) + r + 1)
                            else:
                                pe.wait_ge(s_hl, 12)
                    tm_half_ins(pe, three, half_view, 2 * u + a, 4 if u < 2 else 6, a, stat_qkv(0), stat_qkv(1), banks6, before, s_row, s_used, s_lo, wh, wl)
                    if u and a == 0:
                        for n in range(4 * (u - 1), 4 * u):
                            qk_transposes(n)
            for n in range(8, 14):
                qk_transposes(n)

            atoms = [(n, i) for n, (j, lo, hi) in enumerate(JOBS) for i in range(hi - lo)]
            def atom(n, i):
                kind, jj, a = JOBS[n][0]
                total = JOBS[n][2] - JOBS[n][1]
                if i == 0:
                    if n < 2:
                        pe.wait_ge(s_vl, 6)
                        pe.wait_ge(s_rope, 14)
                    else:
                        job_free(n - 2)
                if kind == "m":
                    if i == 0:
                        pe.wait_ge(s_msu, 8 * (jj - 1))
                        nc.tensor.matmul(job_bank[n % 2], ones[:, :], (macc1 if jj == 3 else macc0)[:, a * 512:(a + 1) * 512], start=True, stop=True).then_inc(s_msum, 1)
                    return
                h = half_of[n]
                if i == 0:
                    pe.wait_ge(s_lo, h + 1)
                k, p = divmod(i, 3)
                vh, vl = half_view(wh, h, "fm"), half_view(wl, h, "fm")
                wt = (vh, vh, vl)[p][:, k, :]
                mv = (hTh, hTl, hTh)[p][:, k, :]
                ins = nc.tensor.matmul(job_bank[n % 2], wt, mv, start=(i == 0), stop=(i == total - 1))
                if i == total - 1:
                    ins.then_inc(s_used, 1)

            def job_free(n):
                kind, jj, a = JOBS[n][0]
                if kind == "m":
                    pe.wait_ge(s_mfin, 2 * (jj - 2) + a + 1)
                elif kind == "c":
                    pe.wait_ge(s_jobf, 2 * jj + a + 1)
                elif kind == "z":
                    pe.wait_ge(s_cz, 2 * jj + a + 1)
                else:
                    pe.wait_ge(s_bs, 2 * jj + a + 1)

            def scores(s):
                b, kv, e, w = step_of(s)
                head = 4 * kv + e + 2 * w
                lo, nw = keys_of(b)
                if s == 0:
                    pe.wait_ge(s_rope, 14)
                    pe.wait_ge(s_vl, 6)
                    pe.wait_ge(s_ql, 14)
                else:
                    pe.wait_ge(s_max, s)
                a0, a1 = dn[0][:, 512 - nw * P:512], dn[1][:, 0:TC]
                q = qT[:, head, b * P:(b + 1) * P]
                for dst, k0, k1 in ((a0, lo * P, (lo + nw) * P), (a1, T, T + TC)):
                    nc.tensor.matmul(dst, q, kH[:, kv, k0:k1], start=True, stop=False)
                    ins = nc.tensor.matmul(dst, q, kL[:, kv, k0:k1], start=False, stop=True)
                ins.then_inc(s_sc, 1)

            def prob_transposes(r):
                nb = keys_of(step_of(r)[0])[1] + 2
                pe.wait_ge(s_pn, r + 1)
                W(pe, s_pl, r)
                for j in range(nb):
                    ins = nc.tensor.transpose(ps[:, j // 4, (j % 4) * P:(j % 4 + 1) * P], prob[:, r % 3, j * P:(j + 1) * P], ident[:, :])
                ins.then_inc(s_pt, 1)

            def values(g):
                b, kv, e, _ = step_of(2 * g)
                lo, nw = keys_of(b)
                pe.wait_ge(s_pl, 2 * g + 2)
                if e == 0:
                    W(pe, s_al, g // 2 - 1)
                bank = pv_bank[g // 2 % 2]
                off = 64 + 128 * kv - 64 * e
                for j in range(nw + 2):
                    tile = lo + j if j < nw else NT + j - nw
                    vh, vl = vH[:, tile, off:off + P], vL[:, tile, off:off + P]
                    mh, ml = (z[:, j, :, :].rearrange("p w n -> p (w n)") for z in (pTh, pTl))
                    nc.tensor.matmul(bank[:, 0:256], vh, mh, start=(e == 0 and j == 0), stop=False)
                    nc.tensor.matmul(bank[:, 0:256], vl, mh, start=False, stop=False)
                    ins = nc.tensor.matmul(bank[:, 0:256], vh, ml, start=False, stop=(e == 1 and j == nw + 1))
                ins.then_inc(s_pv, 1)

            for s in range(STEPS + 3):
                if s < STEPS:
                    scores(s)
                mine = atoms[PER_STEP * s:PER_STEP * (s + 1)]
                cut = next((n for n, (j, i) in enumerate(mine) if i == 0), len(mine))
                for n, i in mine[:cut]:
                    atom(n, i)
                if s >= 4 and s % 2 == 0:
                    values((s - 4) // 2)
                if 2 <= s < STEPS + 2:
                    prob_transposes(s - 2)
                for n, i in mine[cut:]:
                    atom(n, i)

            def out_projection(e, h0, th, tl, order):
                for u in range(4):
                    for a in range(2):
                        def before(r, u=u, a=a):
                            if a == 0:
                                if u:
                                    pe.wait_ge(s_rowf, 16 * (e // 2) + 4 * (u - 1) + r + 1)
                        tm_half_ins(pe, three, half_view, h0 + 2 * u + a, 4, a,
                                    lambda r, k: th[:, order[k], r * P:(r + 1) * P], lambda r, k: tl[:, order[k], r * P:(r + 1) * P],
                                    dn, before, s_row, s_used, s_lo, wh, wl, first=lambda a=a, u=u: out_ready(e, u, a))

            def out_ready(e, u, a):
                if u == 0 and e == 1:
                    if a == 0:
                        pe.wait_ge(s_sl, 4)
                        pe.wait_ge(s_max, STEPS)
                        pe.wait_ge(s_mfin, 6)
                        pe.wait_ge(s_al, STEPS // 4 - 1)
                    else:
                        pe.wait_ge(s_al, STEPS // 4)
                if u == 0 and e == 3 and a == 0:
                    pe.wait_ge(s_pgl, 4)
                    pe.wait_ge(s_tdl, 8)

            def transition(e, h0):
                for t in range(3):
                    norm_transposes(norm_index(e, t))
                for part in range(2):
                    cols = slice(256 * part, 256 * part + 256)
                    pe.wait_ge(s_hl, 2 * norm_index(e, 2 * part + 1) + 2)
                    for n in range(3):
                        h, bank = h0 + n, up[start_bank(e, n)]
                        pe.wait_ge(s_lo, h + 1)
                        vh, vl = half_view(wh, h, "fm"), half_view(wl, h, "fm")
                        for k in range(KT):
                            ins = three(bank[:, cols], vh[:, k, :], vl[:, k, :], hTh[:, k, cols], hTl[:, k, cols], k == 0, k == KT - 1)
                        if part == 0 and n == 0:
                            norm_transposes(norm_index(e, 3))
                        if part == 1:
                            ins.then_inc(s_used, 1)

            def start_bank(e, n):
                return n if e == 2 else (0, 2, 1)[n]

            out_projection(1, 18, aTh, aTl, (4, 5, 6, 7, 0, 1, 2, 3))
            transition(1, B_FFN0)

            def ffn(layer):
                hb = (B_FFN0, B_FFN1)[layer]
                jb = 2 * NPAIR * layer
                pb = 8 * NPAIR * layer
                e = 1 + 2 * layer

                def up_half(i, what):
                    h, dh = ffn_half(layer, i, what)
                    jj = int(what[1])
                    pe.wait_ge(s_lo, h + 1 + dh)
                    if isinstance(i, int) and i == 0:
                        pe.wait_ge(s_hl, 2 * norm_index(e, NT - 1) + 2)
                    elif what[0] == "g":
                        pe.wait_ge(s_gc, jb + 2 * i + jj - 1)
                    else:
                        pe.wait_ge(s_am, jb + 2 * i + jj - 1)
                    dst = up[jj + (2 if what[0] == "v" else 0)]
                    vh, vl = half_view(wh, h, "fm"), half_view(wl, h, "fm")
                    for k in range(KT):
                        nc.tensor.matmul(dst, vh[:, k, :], hTh[:, k, :], start=(k == 0), stop=False)
                        nc.tensor.matmul(dst, vh[:, k, :], hTl[:, k, :], start=False, stop=False)
                        ins = nc.tensor.matmul(dst, vl[:, k, :], hTh[:, k, :], start=False, stop=(k == KT - 1))
                        if k == KT - 1:
                            ins.then_inc(s_used, 1)
                        if k == 2 or k == 5 or k == KT - 1:
                            yield k

                def down(i, between=None):
                    h, dh = ffn_half(layer, i, "d0")
                    pe.wait_ge(s_lo, h + 2 + dh)
                    pe.wait_ge(s_all, jb + 2 * i + 2)
                    for p in range(8):
                        t, hh = divmod(p, 2)
                        if not (isinstance(i, int) and i == 0) or p >= 3:
                            pe.wait_ge(s_ya, pb + 8 * i + (-1, 0, -2)[p] if p < 3 else pb + 8 * i + p - 2)
                        for jj in range(2):
                            wv = lambda z: z[:, (h + jj) % RING, hh * 512:(hh + 1) * 512]
                            ins = three(dn[p % 3], actH[:, jj, t * P:(t + 1) * P], actL[:, jj, t * P:(t + 1) * P], wv(wh), wv(wl),
                                        start=(jj == 0), stop=(jj == 1))
                        if p < 7:
                            ins.then_inc(s_dp, 1)
                        else:
                            ins.then_inc(s_used, 2)
                        if between and p in (2, 5):
                            between(p)

                def job(n):
                    if n:
                        pe.wait_ge(s_mfin, 6 + n)
                    m, hh = divmod(n, 2)
                    nc.tensor.matmul(dn[3], ones[:, :], macc[:, m, hh * 512:(hh + 1) * 512], start=True, stop=True).then_inc(s_msum, 1)

                def turn(i, jobs=False):
                    def half(what):
                        for n, _ in enumerate(up_half(i, what)):
                            if jobs:
                                job(ffn_jobs[what][n])
                    if isinstance(i, int) and i == 0:
                        half("v1")
                        return
                    half("g0")
                    down(i - 1, (lambda p: job(ffn_jobs["d"][p // 3])) if jobs else None)
                    half("v0")
                    half("g1")
                    half("v1")

                turn(0)
                turn(1)
                with pe.Fori(2, NPAIR - 1) as i:
                    turn(i)
                if layer == 0:
                    pe.wait_ge(s_msu, 10 * KT)
                turn(NPAIR - 1, jobs=(layer == 0))
                down(NPAIR - 1)

            ffn(0)
            transition(2, B_L1)

            for n in range(3, 8):
                h = B_L1 + n
                pe.wait_ge(s_lo, h + 1)
                if n >= 4:
                    pe.wait_ge(s_xl, n - 3)
                vh, vl = half_view(wh, h, "fm"), half_view(wl, h, "fm")
                for k in range(KT):
                    nc.tensor.matmul(up[n % 4], vh[:, k, :], hTh[:, k, :], start=(k == 0), stop=False)
                    nc.tensor.matmul(up[n % 4], vh[:, k, :], hTl[:, k, :], start=False, stop=False)
                    ins = nc.tensor.matmul(up[n % 4], vl[:, k, :], hTh[:, k, :], start=False, stop=(k == KT - 1))
                ins.then_inc(s_used, 1)
            h = B_L1 + 8
            pe.wait_ge(s_lo, h + 1)
            pe.wait_ge(s_xl, 4)
            for n in range(16):
                tt, g = divmod(n, 4)
                if n >= 4:
                    pe.wait_ge(s_cal, n - 3)
                ins = three(dn[n % 4][:, 0:256], xTh[:, g, tt * P:(tt + 1) * P], xTl[:, g, tt * P:(tt + 1) * P],
                            wh[:, h % RING, 0:256], wl[:, h % RING, 0:256], True, True)
                ins.then_inc(s_ca if n < 15 else s_used, 1)
            h = B_L1 + 9
            pe.wait_ge(s_lo, h + 1)
            for g in range(4):
                pe.wait_ge(s_pil, g + 1)
                pe.wait_ge(s_u, g + 1)
                ins = three(up[g], wh[:, h % RING, g * P:(g + 1) * P], wl[:, h % RING, g * P:(g + 1) * P], bTh[:, g, :], bTl[:, g, :], True, True)
                ins.then_inc(s_pg if g < 3 else s_used, 1)
            for ck in range(2):
                for a in range(2):
                    def before(r, ck=ck, a=a):
                        if a == 0 and ck:
                            pe.wait_ge(s_tdl, r + 1)
                    tm_half_ins(pe, three, half_view, B_L1 + 10 + 2 * ck + a, 4, a,
                                lambda r, k: xcsH[:, k, r * P:(r + 1) * P], lambda r, k: xcsL[:, k, r * P:(r + 1) * P],
                                dn, before, s_td, s_used, s_lo, wh, wl, first=lambda: pe.wait_ge(s_cal, 16))
            out_projection(3, B_L1 + 14, bTh, bTl, tuple(range(8)))
            transition(3, B_FFN1)
            ffn(1)


def tm_half_ins(pe, three, half_view, h, rows, a, stat_h, stat_l, banks, before, done, s_used, s_lo, wh, wl, first=None):
    pe.wait_ge(s_lo, h + 1)
    if first:
        first()
    vh, vl = half_view(wh, h, "tm"), half_view(wl, h, "tm")
    for r in range(rows):
        before(r)
        for k in range(4):
            ins = three(banks[r][:, 0:256], stat_h(r, 4 * a + k), stat_l(r, 4 * a + k), vh[:, k, :], vl[:, k, :],
                        a == 0 and k == 0, a == 1 and k == 3)
        if a == 1 and r < rows - 1:
            ins.then_inc(done, 1)
    ins.then_inc(s_used, 1)


_INS = ["x", "c", "ctx", "c_ctx", "mod_w", "mod_b", "norm_g", "att_w_in", "att_sink", "sconv_w", "att_w_out",
        "mix_w_in", "pool_w_grp", "pool_scale", "mix_w_out", "ffn_w_up", "ffn_conv", "ffn_w_down"]


def kernel(**inputs):
    import concourse.bacc as _bacc
    from concourse.bass_utils import run_bass_kernel_spmd as _run

    nc = _bacc.Bacc("TRN2", target_bir_lowering=False, num_devices=1)
    arrays, args = {}, {}
    given = {name: np.ascontiguousarray(inputs[name]) for name in _INS}
    for name, a in {**given, **constants()}.items():
        arrays[f"in_{name}"] = a
        args[name] = nc.dram_tensor(f"in_{name}", a.shape, mybir.dt.from_np(a.dtype), kind="ExternalInput").ap()
    args["out"] = nc.dram_tensor("out", (1, T, D), F32, kind="ExternalOutput").ap()
    build(nc, **args)
    return _run(nc, [arrays], core_ids=[0]).results[0]["out"]
```

```python
from contextlib import ExitStack

import numpy as np

import concourse.bass as bass
from concourse import mybir

F32 = mybir.dt.float32
F32R = mybir.dt.float32r
ALU = mybir.AluOpType
ACT = mybir.ActivationFunctionType

P = 128
D = 1024
T = 512
TC = 256
NT = T // P
NTC = TC // P
KT = D // P
DFF = 2816
NJ = DFF // P
NPAIR = NJ // 2
HEADS, KVH, HD = 8, 2, 64
QKV = (HEADS + 2 * KVH) * HD
SCD = 512
EPS = 1e-6
SCALE = HD ** -0.5
MASKED = -1e30
WINDOWS = (2, 4, 8, 16)
GROUPS = (2, 3, 0, 1)
GRID_W = 64
RING = 3
HALF = 1024
MC = 1024
COL_CONV = 64
COL_POOL = COL_CONV + 12
COL_BIAS = COL_POOL + 4
KB = 1024

U_L0 = 13
U_FFN = 3 * NPAIR
U_L1 = 11
B_FFN0 = 2 * U_L0
B_L1 = B_FFN0 + 2 * U_FFN
B_FFN1 = B_L1 + 2 * U_L1


def constants():
    t = np.arange(T)
    nf = HD // 4
    inv = (10000.0 ** (-np.arange(nf, dtype=np.float32) / nf)).astype(np.float32)
    ang = [(v.astype(np.float32)[:, None] * inv).astype(np.float32).astype(np.float64) for v in (t // GRID_W, t % GRID_W)]
    cos = np.concatenate([np.concatenate([np.cos(a)] * 2, 1) for a in ang], 1)
    sin = np.concatenate([np.concatenate([-np.sin(a), np.sin(a)], 1) for a in ang], 1)
    q, k = np.arange(P)[:, None], np.arange(P)[None, :]
    before = np.where(k >= q, 0.0, MASKED)
    after = np.where(k <= q, 0.0, MASKED)
    z = np.zeros((P, P))
    mask = np.concatenate([before, z, after, z, z, before, z, z, z], 1)
    a = 2 * np.pi * np.outer(t, t) % (2 * np.pi * T) / T
    norm = 1.0 / np.sqrt(T * P)
    c = np.arange(P)
    b = 2 * np.pi * (np.outer(c, c) % P) / P
    a = 2 * np.pi * (np.outer(t, t) % T) / T
    edge = np.zeros((4, 16))
    for g, w in enumerate(WINDOWS):
        for n, p in enumerate(list(range(8)) + list(range(T - 8, T))):
            edge[g, n] = w / (min(p + w - w // 2, T) - max(p - w // 2, 0))
    f = np.float32
    return {
        "rope_cos": np.tile(cos, (1, 4)).astype(f), "rope_sin": np.tile(sin, (1, 4)).astype(f),
        "attn_mask": mask.astype(f), "identity": np.eye(P, dtype=f),
        "dft_time": (np.concatenate([np.cos(a), -np.sin(a)], 0) * norm).astype(f),
        "dft_chan": np.concatenate([np.cos(b), np.sin(b)], 1).astype(f),
        "pool_edge": edge.astype(f),
    }


class Chain:

    def __init__(self, eng, sem):
        self.eng, self.sem, self.n, self.extra = eng, sem, 0, None

    def link(self, ins):
        ins.then_inc(self.sem, 1)
        self.n += 1
        self.eng.wait_ge(self.sem, self.n if self.extra is None else self.n + self.extra)

    def loop(self, lo, hi, per, body):
        n0 = self.n
        with self.eng.Fori(lo, hi) as i:
            self.extra = (i - lo) * per
            body(i)
            assert self.n - n0 == per, (self.n - n0, per)
        self.extra = None
        self.n = n0 + per * (hi - lo)


def attention_jobs():
    fm = [(kind, jj, a) for jj in range(2) for kind in "czb" for a in range(2)]
    jobs = []
    for n, j in enumerate(fm):
        jobs.append(j)
        if n in (4, 8):
            m = {4: 2, 8: 3}[n]
            jobs += [("m", m, 0), ("m", m, 1)]
    at, out = 0, []
    for j in jobs:
        first = at
        at += 4 if j[0] == "m" else 3 * KT
        out.append((j, first, at))
    return out


JOBS = attention_jobs()
STEPS = 4 * HEADS
PER_STEP = -(-JOBS[-1][2] // STEPS)


def job_end(n):
    return (JOBS[n][2] - 1) // PER_STEP


def step_of(s):
    return s // 8, (s // 4) % 2, (s // 2) % 2, s % 2


def keys_of(b):
    lo, hi = max(b - 1, 0), min(b + 1, NT - 1)
    return lo, hi - lo + 1


def build(nc, x, c, ctx, c_ctx, mod_w, mod_b, norm_g, att_w_in, att_sink, sconv_w, att_w_out, mix_w_in,
          pool_w_grp, pool_scale, mix_w_out, ffn_w_up, ffn_conv, ffn_w_down, rope_cos, rope_sin,
          attn_mask, identity, dft_time, dft_chan, pool_edge, out):
    ctxs = ExitStack()
    base = -(-nc.sbuf_base // 64) * 64

    def at(name, shape, dt, kb):
        return nc.alloc_sbuf_tensor_at(name, shape, dt, offset=base + int(kb * KB))

    with ctxs:
        hTh = at("hTh", [P, KT, T], F32R, 0)
        hTl = at("hTl", [P, KT, T], F32R, 16)
        wh = at("wh", [P, RING, HALF], F32R, 32)
        wl = at("wl", [P, RING, HALF], F32R, 44)
        mstage = at("mstage", [P, 2, MC], F32, 56)
        macc0 = at("macc0", [P, MC], F32, 64)
        macc1 = at("macc1", [P, MC], F32, 203.5625)
        mbias = at("mbias", [P, MC], F32, 68)
        gate = at("gate", [P, D], F32, 72)
        ident = at("ident", [P, P], F32, 76)
        ones = at("ones", [P, P], F32, 76.5)
        junkc = at("junkc", [P, 4, P], F32, 77)
        vecs = at("vecs", [P, P], F32, 77.5)
        vecf = at("vecf", [P, 2, P], F32, 78)
        cols = at("cols", [P, 96], F32, 79)
        convc = at("convc", [P, 2, NJ, 3], F32, 79.375)
        cw = at("cw", [P, 6], F32, 80)
        siluc = at("siluc", [P, 16], F32, 80.0625)
        modc = at("modc", [P, 16, 2], F32, 80.125)
        scl = at("scl", [P, 5, KT], F32, 80.25)
        shf = at("shf", [P, 5, KT], F32, 80.4375)
        mcol = at("mcol", [P, KT], F32, 80.625)
        sink = at("sink", [P, HEADS], F32, 80.6875)
        nsink = at("nsink", [P, HEADS], F32, 80.75)
        stat = at("stat", [P, 8, 24], F32, 80.8125)
        mhalf = at("mhalf", [P, 1], F32, 81.6875)
        edge = at("edge", [P, 4, 16], F32, 81.71875)
        raw = [at("raw0", [P, 2, HALF], F32, 82), at("raw1", [P, 2, HALF], F32, 90), at("raw2", [P, 2, HALF], F32, 98)]
        xs = at("xs", [P, NT, D], F32, 106)
        ys = at("ys", [P, NT, D], F32, 122)
        hf = at("hf", [P, 2, 4, P], F32, 203.5625)
        junk = at("junk", [P, D], F32, 199.53125)
        qT = at("qT", [P, HEADS, T], F32R, 98)
        kH = at("kH", [P, KVH, T + TC], F32R, 114)
        kL = at("kL", [P, KVH, T + TC], F32R, 120)
        vH = at("vH", [P, NT + NTC, 320], F32R, 126)
        vL = at("vL", [P, NT + NTC, 320], F32R, 133.5)
        mask = at("mask", [P, 9 * P], F32, 141)
        aTh = at("aTh", [P, KT, T], F32R, 146)
        aTl = at("aTl", [P, KT, T], F32R, 162)
        prob = at("prob", [P, 3, 640], F32, 178)
        pTh = at("pTh", [P, 5, 2, P], F32R, 185.5)
        pTl = at("pTl", [P, 5, 2, P], F32R, 190.5)
        czb = at("czb", [P, 2, T + 2], F32, 195.5)
        cvt = at("cvt", [P, 2, T], F32, 199.53125)
        att = at("att", [P, STEPS, 4], F32, 145.5)
        xc = at("xc", [P, NTC, D], F32, 98)
        mfirst = at("mfirst", [P, 4, 2 * MC], F32, 146)
        hcTh = at("hcTh", [P, KT, TC], F32R, 146)
        hcTl = at("hcTl", [P, KT, TC], F32R, 154)
        mrow = at("mrow", [2, 2 * MC], F32, 178)
        cvec = at("cvec", [16, P], F32, 187)
        bcol = at("bcol", [P, 16], F32, 186)
        rcos = at("rcos", [P, NT, 256], F32, 56)
        rsin = at("rsin", [P, NT, 256], F32, 60)
        rt = at("rt", [P, 2, 256], F32, 186)
        qd = at("qd", [P, 4, 4, P], F32, 188)
        actH = at("actH", [P, 2, T], F32R, 138)
        actL = at("actL", [P, 2, T], F32R, 142)
        conv = at("conv", [P, 2, T], F32, 146)
        sil = at("sil", [P, 2, T], F32, 150)
        actF = at("actF", [P, 2, T], F32, 154)
        macc = at("macc", [P, 7, MC], F32, 158)
        bTh = at("bTh", [P, KT, T], F32R, 138)
        bTl = at("bTl", [P, KT, T], F32R, 154)
        xcsH = at("xcsH", [P, 8, T], F32R, 170)
        xcsL = at("xcsL", [P, 8, T], F32R, 186)
        xTh = at("xTh", [P, 4, T], F32R, 122)
        xTl = at("xTl", [P, 4, T], F32R, 130)
        pu = at("pu", [P, 3, T + 16], F32, 64)
        gate1 = at("gate1", [P, 2, D], F32, 56)

        ps = ctxs.enter_context(nc.psum_tensor("ps", [P, 8, 512], F32))
        up = [ps[:, b, :] for b in range(4)]
        dn = [ps[:, 4 + b, :] for b in range(4)]
        job_bank = [up[3], dn[3]]
        pv_bank = [dn[2], up[2]]

        def sem(name):
            return ctxs.enter_context(nc.semaphore(name))

        s_small = sem("small_loaded")
        s_cvec = sem("c_loaded")
        s_vecs = sem("vectors_loaded")
        s_vecf = sem("taps_loaded")
        s_mask = sem("mask_and_gain_loaded")
        s_xt = [sem(f"x_tile_loaded{n}") for n in range(NT + NTC)]
        s_x = sem("x_loaded_again")
        s_first = [sem(f"mfirst_loaded{n}") for n in range(4)]
        s_tab = sem("rope_loaded")
        s_raw = [sem(f"raw_loaded{n}") for n in range(3)]
        s_ms = [sem(f"mstage_loaded{n}") for n in range(2)]
        s_mb = sem("mbias_loaded")
        s_gain = sem("gain_row_loaded")
        s_out = sem("out_stored")
        s_init = sem("constants_set")
        s_pc = sem("pool_chain")
        s_vc = sem("vector_chain")
        s_ac = sem("scalar_chain")
        s_hi = sem("half_high")
        s_lo = sem("half_low")
        s_used = sem("half_used")
        s_vt = sem("vectors_transposed")
        s_cols = sem("columns_ready")
        s_silu = sem("silu_c_ready")
        s_mfu = sem("mfirst_used")
        s_mr = sem("mod_rows_summed")
        s_mrb = sem("mod_shift_rows_copied")
        s_mra = sem("mod_scale_rows_copied")
        s_mrt = sem("mod_rows_transposed")
        s_scl = sem("scales_ready")
        s_mp = sem("mod_products")
        s_msu = sem("mstage_used")
        s_macc = sem("macc_ready")
        s_msum = sem("macc_summed")
        s_mfin = sem("macc_finished")
        s_sqy = sem("y_squares")
        s_rsy = sem("y_rstd")
        s_yg = sem("y_gated")
        s_xup = sem("x_left_updated")
        s_xur = sem("x_right_updated")
        s_sqx = sem("x_squares")
        s_rsx = sem("x_rstd")
        s_xn = sem("x_normed")
        s_tr = sem("norm_transposed")
        s_hf = sem("h_ready")
        s_hf1 = sem("h_right_ready")
        s_hh = sem("h_high")
        s_hl = sem("h_low")
        s_row = sem("rows_multiplied")
        s_rowf = sem("rows_taken")
        s_rope = sem("roped")
        s_qt = sem("qk_transposed")
        s_qh = sem("qk_high")
        s_ql = sem("qk_low")
        s_vh = sem("v_high")
        s_vl = sem("v_low")
        s_sc = sem("scores")
        s_max = sem("maxima")
        s_exp = sem("exponentials")
        s_inv = sem("inverse_totals")
        s_pn = sem("probs_normed")
        s_pt = sem("probs_transposed")
        s_ph = sem("probs_high")
        s_pl = sem("probs_low")
        s_pv = sem("pv_used_probs")
        s_ah = sem("attn_high")
        s_al = sem("attn_low")
        s_jobf = sem("job_bank_free")
        s_cz = sem("cz_ready")
        s_cz1 = sem("centre_tap")
        s_cv = sem("sconv_done")
        s_bs = sem("sconv_gated")
        s_sh = sem("sconv_high")
        s_sl = sem("sconv_low")
        s_cw = sem("taps_ready")
        s_g1 = sem("ffn_centre_tap")
        s_gc = sem("ffn_conv_done")
        s_si = sem("ffn_silu")
        s_am = sem("ffn_gated")
        s_ahh = sem("act_high")
        s_all = sem("act_low")
        s_dp = sem("down_piece")
        s_ya = sem("y_added")
        s_xh = sem("l1_fft_high")
        s_xl = sem("l1_fft_low")
        s_u = sem("pool_in_ready")
        s_pw = sem("pool_windowed")
        s_pih = sem("pool_high")
        s_pil = sem("pool_low")
        s_ca = sem("chan_dft")
        s_cah = sem("chan_dft_high")
        s_cal = sem("chan_dft_low")
        s_pg = sem("pool_grouped")
        s_pgs = sem("pool_scaled")
        s_pgh = sem("pool_out_high")
        s_pgl = sem("pool_out_low")
        s_td = sem("time_dft")
        s_tdh = sem("time_dft_high")
        s_tdl = sem("time_dft_low")

        block = ctxs.enter_context(nc.Block())

        def W(eng, s, v):
            if not (isinstance(v, int) and v <= 0):
                eng.wait_ge(s, v)

        def last_of(eng, s, n, count, h, before=0):
            if n < count - 1:
                eng.wait_ge(s, before + n + 1)
            else:
                eng.wait_ge(s_used, h + 1)

        def half_view(t, h, kind):
            v = t[:, h % RING, :]
            if kind == "tm":
                return v.rearrange("p (k n) -> p k n", n=256)
            if kind == "fm":
                return v.rearrange("p (k n) -> p k n", n=P)
            return v

        def raw_view(slot, a, kind):
            if kind == "fm":
                return raw[slot].rearrange("p a (k n) -> p (a k) n", n=256)[:, :, a * P:(a + 1) * P]
            if kind == "chan":
                return raw[slot][:, a, 0:256]
            if kind == "grp":
                return raw[slot][:, a, 0:512]
            return raw[slot][:, a, :]

        def ring_view(t, h, kind):
            v = t[:, h % RING, :]
            if kind == "fm":
                return v.rearrange("p (k n) -> p k n", n=P)
            if kind == "chan":
                return v[:, 0:256]
            if kind == "grp":
                return v[:, 0:512]
            return v

        def split_high(act, h, slot, a, kind, loads, dh=0):
            act.wait_ge(s_raw[slot], loads)
            W(act, s_used, h - 2 + dh)
            nc.scalar.activation(ring_view(wh, h, kind), raw_view(slot, a, kind), ACT.Copy).then_inc(s_hi, 1)

        def split_low(dve, h, slot, a, kind, dh=0):
            dve.wait_ge(s_hi, h + 1 + dh)
            nc.vector.tensor_sub(ring_view(wl, h, kind), raw_view(slot, a, kind), ring_view(wh, h, kind).bitcast(F32)).then_inc(s_lo, 1)

        plan = {}
        uses = [0, 0, 0]

        def unit(u2, slot, kinds):
            uses[slot] += 1
            for a in range(2):
                plan[u2 + a] = (slot, a, kinds[a], 32 * uses[slot])

        for u in range(U_L0):
            unit(2 * u, u % 2, ("tm", "tm") if u < 3 or u >= 9 else ("fm", "fm"))
        ffn_uses = []
        ffn_uses.append(list(uses))
        uses[:] = [n + NPAIR for n in uses]
        for u in range(U_L1):
            unit(B_L1 + 2 * u, (0, 2, 1)[u % 3], ("fm", "fm") if u < 4 else (("chan", "grp") if u == 4 else ("tm", "tm")))
        ffn_uses.append(list(uses))

        def next_splits(h, with_first):
            splits = {(NT, 0): h + 1, (NT, 1): h + 2}
            if with_first:
                splits[2, 1] = h
            return splits

        half_of = {n: 6 + f for f, n in enumerate(n for n, (j, _, _) in enumerate(JOBS) if j[0] != "m")}
        ffn_jobs = {"g0": (0, 1, 2), "d": (3, 4), "v0": (5, 6, 7), "g1": (8, 9, 10), "v1": (11, 12, 13)}
        rows_before = {1: 11, 3: 20}

        GS, DS, VS = 0, 1, 2

        def ffn_half(layer, i, what):
            hb = (B_FFN0, B_FFN1)[layer]
            k = {"g0": -2, "v0": 1, "g1": 2, "v1": 3, "d0": 5, "d1": 6}[what]
            if not isinstance(i, int):
                return hb + k, i * 6
            if i == 0 and what in ("g0", "v0"):
                k += 2 if what == "g0" else 0
            if i == NPAIR - 1 and what[0] == "d":
                k -= 1
            return hb + k + 6 * i, 0

        def ffn_split(eng, fn, layer, i, what):
            slot = {"g": GS, "d": DS, "v": VS}[what[0]]
            h, dh = ffn_half(layer, i, what)
            kind = "dn" if what[0] == "d" else "fm"
            loads = (i + (ffn_uses[layer][slot] + 1)) * 32
            if fn == "high":
                split_high(eng, h, slot, int(what[1]), kind, loads, dh)
            else:
                split_low(eng, h, slot, int(what[1]), kind, dh)

        def straight_high(act, h):
            if h in plan:
                slot, a, kind, loads = plan[h]
                split_high(act, h, slot, a, kind, loads)
            else:
                layer, idx = (0, h - B_FFN0) if h < B_L1 else (1, h - B_FFN1)
                ffn_split(act, "high", layer, 0, ("g0", "v0", "g1", "v1")[idx])

        def straight_low(dve, h):
            if h in plan:
                slot, a, kind, _ = plan[h]
                split_low(dve, h, slot, a, kind)
            else:
                layer, idx = (0, h - B_FFN0) if h < B_L1 else (1, h - B_FFN1)
                ffn_split(dve, "low", layer, 0, ("g0", "v0", "g1", "v1")[idx])

        def norm_index(e, t):
            return t if e == 0 else 6 + 4 * (e - 1) + t

        def norm_cols(n):
            return (4 if 4 <= n < 6 else 0) if n < 6 else 1 + (n - 6) // 4

        def norm_bank(n, b):
            banks = dn if n >= 6 and (n - 6) % 4 >= 2 else up
            return banks[2 * (n % 2) + b]

        def norm_src(n):
            return xs[:, n, :] if n < 4 else (xc[:, n - 4, :] if n < 6 else ys[:, (n - 6) % 4, :])

        def norm_dst(t, n):
            if 4 <= n < 6:
                return (hcTh, hcTl)[t][:, :, (n - 4) * P:(n - 3) * P]
            tt = n if n < 4 else (n - 6) % 4
            return (hTh, hTl)[t][:, :, tt * P:(tt + 1) * P]

        def h_done(eng, n, b):
            if n < NT:
                eng.wait_ge(s_hf1 if b else s_hf, n + 1)
            else:
                eng.wait_ge(s_hf, NT + 2 * (n - NT) + b + 1)

        @block.sync
        def _(sp):
            def load_unit(slot, halves):
                for dst, src in halves:
                    sp.dma_start(dst, src).then_inc(s_raw[slot], 16)

            def cols_unit(slot, w, c0, order=(0, 1)):
                v = w[:, c0:c0 + 256].rearrange("(k p) n -> p k n", p=P)
                load_unit(slot, [(raw[slot][:, a, :].rearrange("p (k n) -> p k n", n=256), v[:, 4 * g:4 * g + 4, :])
                                 for a, g in enumerate(order)])

            w_in, w_out = att_w_in[0], att_w_out[0]

            def first(k):
                if k >= 4:
                    sp.wait_ge(s_mfu, k - 3)
                sp.dma_start(mfirst[:, k % 4, :], mod_w[0, k * P:(k + 1) * P, 0:2 * MC]).then_inc(s_first[k % 4], 16)

            first(0)
            for dst, src in ((ident[:, :], identity),
                             (cvec[0:8, :], c.rearrange("b (r p) -> (b r) p", p=P)),
                             (cvec[8:16, :], c_ctx.rearrange("(r p) -> r p", p=P))):
                sp.dma_start(dst, src).then_inc(s_cvec, 16)
            for dst, src in ((vecs[0:COL_CONV, :], norm_g.rearrange("l g (r p) -> (l g r) p", p=P)),
                             (vecs[COL_CONV:COL_POOL, :], sconv_w.rearrange("o w (r p) -> (o w r) p", p=P)),
                             (vecs[COL_POOL:COL_BIAS, :], pool_scale.rearrange("o (r p) -> (o r) p", p=P)),
                             (vecs[COL_BIAS:COL_BIAS + 16, :], mod_b[0:1, 0:2 * MC].rearrange("o (r p) -> (o r) p", p=P))):
                sp.dma_start(dst, src).then_inc(s_vecs, 16)
            for k in range(1, KT):
                first(k)
                for t in {1: (0,), 2: (1,), KT - 1: range(2, NT)}.get(k, ()):
                    sp.dma_start(xs[:, t, :], x[0, t * P:(t + 1) * P, :]).then_inc(s_xt[t], 16)
            cols_unit(0, w_in, 0)
            for t in range(NTC):
                sp.dma_start(xc[:, t, :], ctx[0, t * P:(t + 1) * P, :]).then_inc(s_xt[NT + t], 16)
            sp.dma_start(rcos[:, :, :], rope_cos.rearrange("(t p) n -> p t n", p=P)).then_inc(s_tab, 16)
            sp.dma_start(rsin[:, :, :], rope_sin.rearrange("(t p) n -> p t n", p=P)).then_inc(s_tab, 16)
            cols_unit(1, w_in, 256)
            sp.dma_start(mask[:, :], attn_mask).then_inc(s_mask, 16)
            sp.dma_start(gate[:, :], norm_g[0, 1:2, :].broadcast_to([P, D])).then_inc(s_mask, 16)

            s0 = QKV
            col = {"b": s0, "c": s0 + SCD, "z": s0 + 2 * SCD}
            for u in range(2, U_L0):
                if u == U_L0 - 1:
                    sp.wait_ge(s_pv, STEPS // 2)
                    for t in range(NT):
                        sp.dma_start(xs[:, t, :], x[0, t * P:(t + 1) * P, :]).then_inc(s_x, 16)
                sp.wait_ge(s_lo, 2 * (u - 2) + 2)
                if u == 2:
                    cols_unit(0, w_in, 512)
                elif u < 9:
                    jj, kind = divmod(u - 3, 3)
                    cols_unit(u % 2, w_in, col["czb"[kind]] + 256 * jj)
                else:
                    cols_unit(u % 2, w_out, 256 * (u - 9), order=(1, 0))

            def ffn_loads(layer):
                hb = (B_FFN0, B_FFN1)[layer]
                wu = ffn_w_up[layer].rearrange("(k p) n -> p k n", p=P)
                wd = ffn_w_down[layer].rearrange("(j p) n -> p j n", p=P)

                def g_or_v(i, slot, off):
                    for a in range(2):
                        src = wu[:, 4 * a:4 * a + 4, bass.ds(i * 256 + off, 256)]
                        sp.dma_start(raw[slot][:, a, :].rearrange("p (k n) -> p k n", n=256), src).then_inc(s_raw[slot], 16)

                def dn_(i):
                    for a in range(2):
                        src = wd[:, bass.ds(i * 2 + a, 1), :].rearrange("p j n -> p (j n)")
                        sp.dma_start(raw[DS][:, a, :], src).then_inc(s_raw[DS], 16)

                def turn(i):
                    if isinstance(i, int) and i == 0:
                        sp.wait_ge(s_lo, hb if layer == 0 else hb - 2)
                        g_or_v(0, GS, 0)
                        sp.wait_ge(s_lo, hb)
                        g_or_v(0, VS, DFF)
                        return
                    first_turn = isinstance(i, int) and i == 1
                    sp.wait_ge(s_lo, hb + 3 if first_turn else hb + 6 * i - 2 - 1)
                    g_or_v(i, GS, 0)
                    if not first_turn:
                        sp.wait_ge(s_lo, hb + 6 * i - 5 + 0)
                    dn_(i - 1)
                    sp.wait_ge(s_lo, hb + 6 * i - 2)
                    g_or_v(i, VS, DFF)

                turn(0)
                turn(1)
                with sp.Fori(2, NPAIR - 1) as i:
                    turn(i)
                turn(NPAIR - 1)
                sp.wait_ge(s_lo, hb + 6 * NPAIR - 5)
                dn_(NPAIR - 1)

            ffn_loads(0)
            for u in range(U_L1):
                free = (B_L1 - 3, B_L1 - 2, B_L1)[u] if u < 3 else B_L1 + 2 * (u - 3) + 2
                sp.wait_ge(s_lo, free)
                slot = plan[B_L1 + 2 * u][0]
                if u < 4:
                    cols_unit(slot, mix_w_in[0], (SCD, SCD + 256, 256, 0)[u])
                elif u == 4:
                    load_unit(slot, [(raw[slot][:, 0, 0:256], dft_chan),
                                     (raw[slot][:, 1, 0:512].rearrange("p (g n) -> p g n", g=4),
                                      pool_w_grp[0].rearrange("g c n -> c g n"))])
                elif u < 7:
                    cols_unit(slot, dft_time, 256 * (u - 5))
                else:
                    cols_unit(slot, mix_w_out[0], 256 * (u - 7))
            ffn_loads(1)
            for t in range(NT):
                sp.wait_ge(s_xup, 4 * 3 + t + 1)
                sp.wait_ge(s_xur, 4 * 3 + t + 1)
                sp.dma_start(out[0, t * P:(t + 1) * P, :], xs[:, t, :]).then_inc(s_out, 16)
            sp.wait_ge(s_out, 16 * NT)

        @block.gpsimd
        def _(pool):
            nc.gpsimd.memset(ones[:, :], 1.0).then_inc(s_init, 1)
            nc.gpsimd.memset(mbias[:, :], 0.0).then_inc(s_init, 1)
            nc.gpsimd.memset(mhalf[:, :], -0.5).then_inc(s_init, 1)
            nc.gpsimd.memset(vH[:, :, :].bitcast(F32), 0.0).then_inc(s_init, 1)
            nc.gpsimd.memset(vL[:, :, :].bitcast(F32), 0.0).then_inc(s_init, 1)
            pool.wait_ge(s_init, 5)
            ch = Chain(pool, s_pc)

            def rstd(row, q, done):
                ch.link(nc.gpsimd.tensor_scalar(stat[:, row + 1, q:q + 1], stat[:, row, q:q + 1], 1.0 / D, EPS, ALU.mult, ALU.add))
                nc.gpsimd.tensor_tensor(stat[:, row + 2, q:q + 1], stat[:, row + 1, q:q + 1], mhalf[:, :], ALU.pow).then_inc(done, 1)

            def rstd_x(n):
                pool.wait_ge(s_sqx, n + 1)
                rstd(3, n, s_rsx)

            def h_high(n, b):
                h_done(pool, n, b)
                nc.gpsimd.tensor_scalar(norm_dst(0, n)[:, 4 * b:4 * b + 4, :], hf[:, b, :, :], 1.0, 0.0, ALU.mult, ALU.add).then_inc(s_hh, 1)

            for tiles in (range(NT), range(NT, NT + NTC)):
                for n in tiles:
                    rstd_x(n)
                for n in tiles:
                    for b in range(2):
                        h_high(n, b)

            chunks = [(0, 2, macc0), (0, 3, macc1), (0, 4, macc0), (0, 5, macc[:, 6, :])] + [(1, m, macc[:, m, :]) for m in range(6)]

            def mod_load(n):
                (l, m, _), k = chunks[n // KT], n % KT
                cols = slice(m * MC, (m + 1) * MC)
                if k == 0:
                    if n:
                        pool.wait_ge(s_msu, n - KT + 1)
                    pool.dma_start(mbias[0:1, :], mod_b[l:l + 1, cols]).then_inc(s_mb, 16)
                if n >= 2:
                    pool.wait_ge(s_msu, n - 1)
                pool.dma_start(mstage[:, n % 2, :], mod_w[l, k * P:(k + 1) * P, cols]).then_inc(s_ms[n % 2], 16)

            def mod_add(n):
                acc, k = chunks[n // KT][2], n % KT
                pool.wait_ge(s_ms[n % 2], 16 * (n // 2 + 1))
                if k == 0:
                    pool.wait_ge(s_mb, 16 * (n // KT + 1))
                if n == 2 * KT:
                    pool.wait_ge(s_msum, 2)
                nc.gpsimd.tensor_scalar(mstage[:, n % 2, :], mstage[:, n % 2, :], siluc[:, k:k + 1], 0.0, ALU.mult, ALU.add).then_inc(s_mp, 1)
                pool.wait_ge(s_mp, n + 1)
                if n:
                    pool.wait_ge(s_msu, n)
                nc.gpsimd.tensor_tensor(acc[:, :], mstage[:, n % 2, :], mbias[:, :] if k == 0 else acc[:, :], ALU.add).then_inc(s_msu, 1)

            def mod_tiles(lo, hi):
                for n in range(lo, lo + 2):
                    mod_load(n)
                for n in range(lo, hi):
                    mod_add(n)
                    if n + 2 < hi:
                        mod_load(n + 2)

            pool.wait_ge(s_rope, 14)
            mod_tiles(0, 3 * KT)

            def rstd_y(e, t):
                pool.wait_ge(s_sqy, 4 * (e - 1) + t + 1)
                rstd(0, 4 * (e - 1) + t, s_rsy)

            def transition(e):
                rstd_y(e, 0)
                for t in range(NT + 2):
                    if 1 <= t <= NT and e < 4:
                        rstd_x(norm_index(e, t - 1))
                    if t + 1 < NT:
                        rstd_y(e, t + 1)
                    if t < NT:
                        pool.wait_ge(s_yg, 4 * (e - 1) + t + 1)
                        if e == 1:
                            pool.wait_ge(s_x, 16 * NT)
                        nc.gpsimd.tensor_tensor(xs[:, t, D // 2:D], xs[:, t, D // 2:D], ys[:, t, D // 2:D], ALU.add).then_inc(s_xur, 1)
                    if t >= 2 and e < 4:
                        for b in range(2):
                            h_high(norm_index(e, t - 2), b)

            transition(1)

            mod_tiles(3 * KT, 10 * KT)
            pool.wait_ge(s_yg, 4)
            pool.dma_start(gate[:, :], norm_g[0, 3:4, :].broadcast_to([P, D])).then_inc(s_gain, 16)
            pool.wait_ge(s_msu, 10 * KT)
            for n, g in enumerate((1, 3)):
                pool.dma_start(gate1[:, n, :], norm_g[1, g:g + 1, :].broadcast_to([P, D])).then_inc(s_gain, 16)
            for e in (2, 3, 4):
                transition(e)

        @block.scalar
        def _(act):
            for l in range(2):
                act.dma_start(vecf[0:3 * NJ, l, :], ffn_conv[l].rearrange("w (r p) -> (w r) p", p=P)).then_inc(s_vecf, 16)
            small = [
                (sink[:, :], att_sink[0:1, :].broadcast_to([P, HEADS])),
                (edge[:, :, :], pool_edge.unsqueeze(0).broadcast_to([P, 4, 16])),
            ]
            for dst, src in small:
                act.dma_start(dst, src).then_inc(s_small, 16)
            ch = Chain(act, s_ac)

            written = {"junk": None}

            def square(dst, src, done, count):
                if written["junk"]:
                    act.wait_ge(*written["junk"])
                nc.scalar.activation(junk[:, :], src, ACT.Square, accum_out=dst).then_inc(done, 1)
                written["junk"] = (done, count)

            def h_tile(n):
                e = norm_cols(n)
                for b in range(1 if n < NT else 2):
                    act.wait_ge(s_tr, 2 * n + b + 1)
                    W(act, s_hl, 2 * n + b - 1)
                    bank = norm_bank(n, b).rearrange("p (k n) -> p k n", n=P)
                    for k in range(4):
                        ins = nc.scalar.activation(hf[:, b, k, :], bank[:, k, :], ACT.Identity,
                                                   scale=scl[:, e, 4 * b + k:4 * b + k + 1], bias=shf[:, e, 4 * b + k:4 * b + k + 1])
                    ins.then_inc(s_hf, 1)

            act.wait_ge(s_vt, 1)
            nc.scalar.activation(siluc[:, :], up[3][:, 0:16], ACT.Silu).then_inc(s_silu, 1)
            def square_x(n):
                act.wait_ge(s_xt[n], 16)
                square(stat[:, 3, n:n + 1], norm_src(n), s_sqx, n + 1)

            for n in range(NT):
                square_x(n)
            act.wait_ge(s_mr, 1)
            nc.scalar.activation(mrow[:, 2 * 512:4 * 512], ps[0:2, 6:8, :].rearrange("p b n -> p (b n)"), ACT.Copy).then_inc(s_mra, 1)
            straight_high(act, 0)
            act.wait_ge(s_scl, 2)
            h_tile(0)
            h_tile(1)
            straight_high(act, 1)
            h_tile(2)
            h_tile(3)
            for n in range(NT, NT + NTC):
                square_x(n)
            straight_high(act, 2)
            for n in range(NT, NT + NTC):
                h_tile(n)

            def qk_high(n):
                act.wait_ge(s_qt, n + 1)
                if n < 8:
                    u, t = divmod(n, 4)
                    dst = qT[:, 4 * u:4 * u + 4, t * P:(t + 1) * P]
                    src = up[n % 2].rearrange("p (h n) -> p h n", n=P)
                else:
                    dst = kH[:, :, (n - 8) * P:(n - 7) * P]
                    src = up[n % 2][:, 0:2 * P].rearrange("p (h n) -> p h n", n=P)
                nc.scalar.activation(dst, src, ACT.Copy).then_inc(s_qh, 1)

            def v_high(t):
                last_of(act, s_row, t, 6, 5, 6)
                act.wait_ge(s_init, 5)
                bank = dn[t] if t < 4 else up[t - 2]
                dst = vH[:, t, 64:320].rearrange("p (h n) -> p h n", n=P)[:, :, 0:HD]
                nc.scalar.activation(dst, bank[:, P:2 * P].rearrange("p (h n) -> p h n", n=HD), ACT.Copy).then_inc(s_vh, 1)

            straight_high(act, 3)
            straight_high(act, 4)
            for n in range(4):
                qk_high(n)
            straight_high(act, 5)
            straight_high(act, 6)
            for n in range(4, 8):
                qk_high(n)
            straight_high(act, 7)
            for t in range(6):
                v_high(t)
                if t:
                    qk_high(8 + t - 1)
            qk_high(13)
            straight_high(act, 8)

            nsh = [0]
            for s in range(STEPS + 4):
                for n, (job, _, _) in enumerate(JOBS):
                    if job_end(n) == s - 1 and job[0] != "m":
                        nsh[0] += 1
                        straight_high(act, 6 + nsh[0] + 2)
                if s < STEPS:
                    b, kv, e, w = step_of(s)
                    head = 4 * kv + e + 2 * w
                    nk = (keys_of(b)[1] + 2) * P
                    act.wait_ge(s_max, s + 1)
                    nc.scalar.activation(prob[:, s % 3, 0:nk], prob[:, s % 3, 0:nk], ACT.Exp, bias=att[:, s, 1:2],
                                         scale=SCALE, accum_out=att[:, s, 2:3])
                    nc.scalar.activation(att[:, s, 3:4], sink[:, head:head + 1], ACT.Exp, bias=att[:, s, 1:2]).then_inc(s_exp, 1)
                if 2 <= s < STEPS + 2:
                    r = s - 2
                    nb = keys_of(step_of(r)[0])[1] + 2
                    act.wait_ge(s_pt, r + 1)
                    W(act, s_pv, r // 2)
                    src = ps[:, 0:2, :].rearrange("p b n -> p (b n)")[:, 0:nb * P].rearrange("p (j n) -> p j n", n=P)
                    nc.scalar.activation(pTh[:, 0:nb, r % 2, :], src, ACT.Copy).then_inc(s_ph, 1)
                for n, (job, _, _) in enumerate(JOBS):
                    if job_end(n) == s and job[0] != "m":
                        kind, jj, a = job
                        if kind == "c":
                            act.wait_ge(s_used, half_of[n] + 1)
                            W(act, s_cv, 2 * (jj - 1) + a + 1)
                            nc.scalar.activation(czb[:, a, 1:T + 1], job_bank[n % 2], ACT.Copy).then_inc(s_jobf, 1)
                        elif kind == "z":
                            act.wait_ge(s_cz, 2 * jj + a + 1)
                            W(act, s_sl, 2 * (jj - 1) + a + 1)
                            f = COL_CONV + 4 + 2 * jj + a
                            nc.scalar.activation(cvt[:, a, :], czb[:, a, 1:T + 1], ACT.Copy, scale=cols[:, f:f + 1]).then_inc(s_cz1, 1)
                        else:
                            act.wait_ge(s_bs, 2 * jj + a + 1)
                            nc.scalar.activation(aTh[:, 4 + 2 * jj + a, :], cvt[:, a, :], ACT.Copy).then_inc(s_sh, 1)
                if s >= 7 and (s - 7) % 4 == 0:
                    o = (s - 7) // 4
                    act.wait_ge(s_pv, 2 * o + 2)
                    b, kv = divmod(o, 2)
                    nc.scalar.activation(aTh[:, 2 * kv:2 * kv + 2, b * P:(b + 1) * P],
                                         pv_bank[o % 2][:, 0:2 * P].rearrange("p (w n) -> p w n", n=P), ACT.Copy).then_inc(s_ah, 1)
                if 1 <= s < STEPS + 1:
                    nk = (keys_of(step_of(s - 1)[0])[1] + 2) * P
                    act.wait_ge(s_inv, s)
                    nc.scalar.activation(prob[:, (s - 1) % 3, 0:nk], prob[:, (s - 1) % 3, 0:nk], ACT.Copy, scale=att[:, s - 1, 3:4]).then_inc(s_pn, 1)

            def square_y(e, t):
                y_wait(act, e, t)
                q = 4 * (e - 1) + t
                square(stat[:, 0, q:q + 1], ys[:, t, :], s_sqy, q + 1)

            def transition(e, splits):
                square_y(e, 0)
                for t in range(NT + 2):
                    if t + 1 < NT:
                        square_y(e, t + 1)
                    if (t, 0) in splits:
                        straight_high(act, splits[t, 0])
                    if t >= 2 and e < 4:
                        h_tile(norm_index(e, t - 2))
                    if (t, 1) in splits:
                        straight_high(act, splits[t, 1])
                    if t < NT and e < 4:
                        act.wait_ge(s_xup, 4 * (e - 1) + t + 1)
                        act.wait_ge(s_xur, 4 * (e - 1) + t + 1)
                        n = norm_index(e, t)
                        square(stat[:, 3, n:n + 1], xs[:, t, :], s_sqx, n + 1)

            def ffn(layer):
                hb = (B_FFN0, B_FFN1)[layer]

                def centre(i, jj):
                    h, dh = ffn_half(layer, i, ("g0", "g1")[jj])
                    act.wait_ge(s_used, h + 1 + dh)
                    act.wait_ge(s_cw, NPAIR * layer + i + 1)
                    W(act, s_si, 2 * NPAIR * layer + 2 * i + jj - 1)
                    nc.scalar.activation(conv[:, jj, :], up[jj], ACT.Copy, scale=cw[:, 3 * jj + 1:3 * jj + 2]).then_inc(s_g1, 1)

                def silu(i, jj):
                    act.wait_ge(s_gc, 2 * NPAIR * layer + 2 * i + jj + 1)
                    W(act, s_am, 2 * NPAIR * layer + 2 * i + jj - 1)
                    nc.scalar.activation(sil[:, jj, :], conv[:, jj, :], ACT.Silu).then_inc(s_si, 1)

                def act_high(i, jj):
                    act.wait_ge(s_am, 2 * NPAIR * layer + 2 * i + jj + 1)
                    if not (isinstance(i, int) and i == 0):
                        act.wait_ge(s_used, hb + 6 * i + 1)
                    nc.scalar.activation(actH[:, jj, :], actF[:, jj, :], ACT.Copy).then_inc(s_ahh, 1)

                def turn(i, last=False):
                    zero = isinstance(i, int) and i == 0
                    if not zero:
                        ffn_split(act, "high", layer, i - 1, "d1")
                        act_high(i - 1, 1)
                    centre(i, 0)
                    if not zero:
                        ffn_split(act, "high", layer, i, "v0")
                    silu(i, 0)
                    if not zero:
                        ffn_split(act, "high", layer, i, "g1")
                    ffn_split(act, "high", layer, i, "v1")
                    act_high(i, 0)
                    centre(i, 1)
                    silu(i, 1)
                    if not last:
                        ffn_split(act, "high", layer, i + 1, "g0")
                    ffn_split(act, "high", layer, i, "d0")

                turn(0)
                with act.Fori(1, NPAIR - 1) as i:
                    turn(i)
                turn(NPAIR - 1, last=True)
                ffn_split(act, "high", layer, NPAIR - 1, "d1")
                act_high(NPAIR - 1, 1)

            def y_wait(eng, e, t):
                if e in (1, 3):
                    eng.wait_ge(s_rowf, 3 * NT * (e // 2) + 2 * NT + t + 1)
                else:
                    eng.wait_ge(s_ya, 8 * NPAIR * (e // 2) - 8 + 2 * t + 2)

            for h in range(2 * 9 + 3, B_FFN0):
                straight_high(act, h)
            transition(1, next_splits(B_FFN0, True))
            ffn(0)
            straight_high(act, B_L1)
            transition(2, next_splits(B_L1, False))
            for n in range(4):
                act.wait_ge(s_used, B_L1 + n + 1)
                nc.scalar.activation(xTh[:, n, :], up[n], ACT.Copy).then_inc(s_xh, 1)
                straight_high(act, B_L1 + 3 + n)
            def pool_high(i, g):
                act.wait_ge(s_pw, i + 1)
                nc.scalar.activation(bTh[:, g, :], pu[:, 2 if g % 2 == 0 else 1, 0:T], ACT.Copy).then_inc(s_pih, 1)

            for i, g in enumerate(GROUPS):
                act.wait_ge(s_used, B_L1 + 4 + i + 1)
                act.wait_ge(s_init, 7)
                W(act, s_pw, i)
                nc.scalar.activation(pu[:, 0, 8:T + 8], up[i], ACT.Copy).then_inc(s_u, 1)
                if i < 3:
                    straight_high(act, B_L1 + 7 + i)
                    pool_high(i, g)
            for n in range(16):
                tt, g = divmod(n, 4)
                last_of(act, s_ca, n, 16, B_L1 + 8)
                dst = xcsH[:, :, g * P:(g + 1) * P].rearrange("p (s t) n -> p s t n", s=2)[:, :, tt, :]
                nc.scalar.activation(dst, dn[n % 4][:, 0:256].rearrange("p (s n) -> p s n", n=P), ACT.Copy).then_inc(s_cah, 1)
            straight_high(act, B_L1 + 10)
            pool_high(3, GROUPS[3])
            straight_high(act, B_L1 + 11)
            for i, g in enumerate(GROUPS):
                last_of(act, s_pg, i, 4, B_L1 + 9)
                W(act, s_pgl, i - 1)
                ch.link(nc.scalar.activation(hf[:, g % 2, :, :].rearrange("p k n -> p (k n)"), up[i], ACT.Copy, scale=cols[:, COL_POOL + g:COL_POOL + g + 1]))
                nc.scalar.activation(bTh[:, g, :], hf[:, g % 2, :, :].rearrange("p k n -> p (k n)"), ACT.Copy).then_inc(s_pgh, 1)
            straight_high(act, B_L1 + 12)
            for ck in range(2):
                straight_high(act, B_L1 + 13 + 2 * ck)
                for g in range(4):
                    last_of(act, s_td, g, 4, B_L1 + 11 + 2 * ck, 3 * ck)
                    nc.scalar.activation(bTh[:, 4 + g, ck * 256:(ck + 1) * 256], dn[g][:, 0:256], ACT.Copy).then_inc(s_tdh, 1)
                straight_high(act, B_L1 + 14 + 2 * ck)
            for h in range(B_L1 + 17, B_FFN1):
                straight_high(act, h)
            transition(3, next_splits(B_FFN1, True))
            ffn(1)
            transition(4, {})


        @block.vector
        def _(dve):
            ch = Chain(dve, s_vc)

            dve.wait_ge(s_vt, 4)
            nc.vector.tensor_copy(bcol[:, :], up[0][:, COL_BIAS:COL_BIAS + 16])
            ch.link(nc.vector.tensor_copy(cols[:, :], up[0][:, 0:96]))
            for l in range(2):
                nc.vector.tensor_copy(convc[:, l, :, :].rearrange("p j w -> p w j"),
                                      up[1 + l][:, 0:3 * NJ].rearrange("p (w j) -> p w j", w=3)).then_inc(s_cols, 1)

            def xn(n, dst, src):
                dve.wait_ge(s_rsx, n + 1)
                nc.vector.tensor_scalar(dst, src, stat[:, 5, n:n + 1], None, ALU.mult).then_inc(s_xn, 1)

            def h_low(n, b):
                dve.wait_ge(s_hh, 2 * n + b + 1)
                nc.vector.tensor_sub(norm_dst(1, n)[:, 4 * b:4 * b + 4, :], hf[:, b, :, :],
                                     norm_dst(0, n)[:, 4 * b:4 * b + 4, :].bitcast(F32)).then_inc(s_hl, 1)

            for n in range(NT):
                xn(n, norm_src(n), norm_src(n))
            dve.wait_ge(s_mr, 1)
            nc.vector.tensor_copy(mrow[:, 0:2 * 512], ps[0:2, 4:6, :].rearrange("p b n -> p (b n)")).then_inc(s_mrb, 1)
            dve.wait_ge(s_mrt, 1)
            ch.link(nc.vector.tensor_copy(modc[:, :, :], dn[0][:, 0:32].rearrange("p (k v) -> p k v", v=2)))
            for v in range(2):
                nc.vector.tensor_tensor(shf[:, 4 * v, :], modc[:, 0:KT, v], bcol[:, 0:KT], ALU.add)
                ch.link(nc.vector.tensor_tensor(scl[:, 4 * v, :], modc[:, KT:2 * KT, v], bcol[:, KT:2 * KT], ALU.add))
                nc.vector.scalar_tensor_tensor(out=scl[:, 4 * v, :], in0=scl[:, 4 * v, :], scalar=1.0, in1=cols[:, 0:KT],
                                               op0=ALU.add, op1=ALU.mult).then_inc(s_scl, 1)
            straight_low(dve, 0)
            def h_right(n):
                dve.wait_ge(s_tr, 2 * n + 2)
                W(dve, s_hl, 2 * n)
                for k in range(4):
                    ins = nc.vector.tensor_scalar(hf[:, 1, k, :], norm_bank(n, 1)[:, k * P:(k + 1) * P],
                                                  scl[:, 0, 4 + k:5 + k], shf[:, 0, 4 + k:5 + k], ALU.mult, ALU.add)
                ins.then_inc(s_hf1, 1)

            dve.wait_ge(s_scl, 2)
            for n in range(NT):
                h_right(n)
                for b in range(2):
                    h_low(n, b)
                if n == 1:
                    straight_low(dve, 1)
            for n in range(NT, NT + NTC):
                xn(n, norm_src(n), norm_src(n))
            straight_low(dve, 2)

            rp = lambda ap: ap.rearrange("p (h r f) -> p h r f", r=2, f=16)

            def rope(n, bank, t, width):
                W(dve, s_qt, n - 3)
                W(dve, s_rope, n)
                nh = width // HD
                src = rp(bank[:, 0:width])
                cs, sn = rp(rcos[:, t, 0:width]), rp(rsin[:, t, 0:width])
                nc.vector.tensor_tensor(rt[:, 0, 0:width], bank[:, 0:width], rcos[:, t, 0:width], ALU.mult)
                for r in range(2):
                    ins = nc.vector.tensor_tensor(rp(rt[:, 1, 0:width])[:, :, r, :], src[:, :, 1 - r, :], sn[:, :, r, :], ALU.mult)
                return ins, nh

            def rope_add(n, nh):
                wide = lambda a: rt[:, a, 0:nh * HD].rearrange("p (h o d) -> p h o d", o=1, d=HD).broadcast_to([P, nh, 2, HD])
                nc.vector.tensor_tensor(qd[:, n % 4, 0:nh, :].rearrange("p h (o d) -> p h o d", o=2), wide(0), wide(1), ALU.add).then_inc(s_rope, 1)

            def rope_q(n):
                u, t = divmod(n, 4)
                last_of(dve, s_row, t, 4, 2 * u + 1, 3 * u)
                ins, nh = rope(n, dn[t], t, 256)
                ch.link(ins)
                rope_add(n, nh)

            def qk_low(n):
                dve.wait_ge(s_qh, n + 1)
                if n < 8:
                    u, t = divmod(n, 4)
                    dst = qT[64:P, 4 * u:4 * u + 4, t * P:(t + 1) * P]
                    nc.vector.tensor_sub(dst, up[n % 2][64:P, :].rearrange("p (h n) -> p h n", n=P), dst.bitcast(F32)).then_inc(s_ql, 1)
                else:
                    c0 = (n - 8) * P
                    nc.vector.tensor_sub(kL[:, :, c0:c0 + P], up[n % 2][:, 0:2 * P].rearrange("p (h n) -> p h n", n=P),
                                         kH[:, :, c0:c0 + P].bitcast(F32)).then_inc(s_ql, 1)

            dve.wait_ge(s_small, 16 * 2)
            ch.link(nc.vector.tensor_scalar(nsink[:, :], sink[:, :], -1.0, None, ALU.mult))
            dve.wait_ge(s_tab, 32)
            for n in range(4):
                rope_q(n)
                if n < NTC:
                    for b in range(2):
                        h_low(NT + n, b)
            straight_low(dve, 3)
            straight_low(dve, 4)
            for n in range(4):
                qk_low(n)
            straight_low(dve, 5)
            for n in range(4, 8):
                rope_q(n)
            straight_low(dve, 6)
            for n in range(4, 8):
                qk_low(n)
            for t in range(6):
                n = 8 + t
                bank = dn[t] if t < 4 else up[t - 2]
                dve.wait_ge(s_vh, t + 1)
                if t < 4:
                    ins, nh = rope(n, bank, t, P)
                    ch.link(ins)
                    rope_add(n, nh)
                else:
                    W(dve, s_qt, n - 3)
                    nc.vector.tensor_copy(qd[:, n % 4, 0:2, :].rearrange("p h (o d) -> p h o d", o=2),
                                          bank[:, 0:P].rearrange("p (h o d) -> p h o d", o=1, d=HD).broadcast_to([P, 2, 2, HD])).then_inc(s_rope, 1)
                vv = lambda z: z[:, t, 64:320].rearrange("p (h n) -> p h n", n=P)[:, :, 0:HD]
                nc.vector.tensor_sub(vv(vL), bank[:, P:2 * P].rearrange("p (h n) -> p h n", n=HD), vv(vH).bitcast(F32)).then_inc(s_vl, 1)
                if t:
                    qk_low(n - 1)
            qk_low(13)
            straight_low(dve, 7)
            straight_low(dve, 8)
            nc.vector.memset(czb[:, :, 0:1], 0.0)
            ch.link(nc.vector.memset(czb[:, :, T + 1:T + 2], 0.0))

            def fin(n, bank, dst_kind, hh, tile):
                dve.wait_ge(s_msum, n + 1)
                if dst_kind == "gate":
                    nc.vector.tensor_tensor(tile[:, hh * 512:(hh + 1) * 512], bank, tile[:, hh * 512:(hh + 1) * 512], ALU.mult).then_inc(s_mfin, 1)
                    return
                W(dve, s_mfin, n)
                for k in range(4):
                    kk = 4 * hh + k
                    dst = mcol[:, kk:kk + 1] if dst_kind == "scale" else shf[:, tile, kk:kk + 1]
                    ins = nc.vector.tensor_tensor_reduce(junkc[:, k, :], bank[:, k * P:(k + 1) * P], ident[:, :], 1.0, 0.0, ALU.mult, ALU.add, dst)
                ins.then_inc(s_mfin, 1)
                if dst_kind == "scale" and hh == 1:
                    e, g0 = tile
                    dve.wait_ge(s_mfin, n + 1)
                    ch.link(nc.vector.scalar_tensor_tensor(out=scl[:, e, :], in0=mcol[:, :], scalar=1.0, in1=cols[:, g0:g0 + KT],
                                                           op0=ALU.add, op1=ALU.mult))

            dve.wait_ge(s_mask, 32)
            nsl = [0]
            for s in range(STEPS + 4):
                if s < STEPS:
                    b, kv, e, w = step_of(s)
                    head = 4 * kv + e + 2 * w
                    lo, nw = keys_of(b)
                    nk = (nw + 2) * P
                    dve.wait_ge(s_sc, s + 1)
                    W(dve, s_pt, s - 2)
                    m0 = {0: P, NT - 1: 5 * P}.get(b, 0)
                    src = ps[:, 4:6, :].rearrange("p b n -> p (b n)")[:, 512 - nw * P:768]
                    ch.link(nc.vector.tensor_tensor_reduce(prob[:, s % 3, 0:nk], src, mask[:, m0:m0 + nk], 1.0, -3e38, ALU.add, ALU.max, att[:, s, 0:1]))
                    nc.vector.scalar_tensor_tensor(out=att[:, s, 1:2], in0=att[:, s, 0:1], scalar=-SCALE, in1=nsink[:, head:head + 1],
                                                   op0=ALU.mult, op1=ALU.min).then_inc(s_max, 1)
                if 1 <= s < STEPS + 1:
                    r = s - 1
                    dve.wait_ge(s_exp, r + 1)
                    ch.link(nc.vector.tensor_tensor(att[:, r, 0:1], att[:, r, 2:3], att[:, r, 3:4], ALU.add))
                    nc.vector.reciprocal(att[:, r, 3:4], att[:, r, 0:1]).then_inc(s_inv, 1)
                for n, (job, _, _) in enumerate(JOBS):
                    if job_end(n) == s - 1 and job[0] != "m":
                        nsl[0] += 1
                        straight_low(dve, 6 + nsl[0] + 2)
                for n, (job, _, _) in enumerate(JOBS):
                    if job_end(n) == s:
                        kind, jj, a = job
                        if kind == "m":
                            fin(2 * (jj - 2) + a, job_bank[n % 2], {2: "gate", 3: "shift"}[jj], a, {2: gate, 3: 1}[jj])
                        elif kind == "z":
                            dve.wait_ge(s_used, half_of[n] + 1)
                            dve.wait_ge(s_jobf, 2 * jj + a + 1)
                            nc.vector.tensor_tensor(czb[:, a, 1:T + 1], job_bank[n % 2], czb[:, a, 1:T + 1], ALU.mult).then_inc(s_cz, 1)
                        elif kind == "b":
                            dve.wait_ge(s_used, half_of[n] + 1)
                            dve.wait_ge(s_cv, 2 * jj + a + 1)
                            nc.vector.tensor_tensor(cvt[:, a, :], job_bank[n % 2], cvt[:, a, :], ALU.mult).then_inc(s_bs, 1)
                if 2 <= s < STEPS + 2:
                    r = s - 2
                    nb = keys_of(step_of(r)[0])[1] + 2
                    dve.wait_ge(s_ph, r + 1)
                    src = ps[:, 0:2, :].rearrange("p b n -> p (b n)")[:, 0:nb * P].rearrange("p (j n) -> p j n", n=P)
                    nc.vector.tensor_sub(pTl[:, 0:nb, r % 2, :], src, pTh[:, 0:nb, r % 2, :].bitcast(F32)).then_inc(s_pl, 1)
                for n, (job, _, _) in enumerate(JOBS):
                    if job_end(n) == s:
                        kind, jj, a = job
                        if kind == "z":
                            dve.wait_ge(s_cz1, 2 * jj + a + 1)
                            for tap in (0, 2):
                                f = COL_CONV + 4 * tap + 2 * jj + a
                                ins = nc.vector.scalar_tensor_tensor(out=cvt[:, a, :], in0=czb[:, a, tap:tap + T], scalar=cols[:, f:f + 1],
                                                                     in1=cvt[:, a, :], op0=ALU.mult, op1=ALU.add)
                                if tap == 0:
                                    ch.link(ins)
                            ins.then_inc(s_cv, 1)
                        elif kind == "b":
                            dve.wait_ge(s_sh, 2 * jj + a + 1)
                            nc.vector.tensor_sub(aTl[:, 4 + 2 * jj + a, :], cvt[:, a, :], aTh[:, 4 + 2 * jj + a, :].bitcast(F32)).then_inc(s_sl, 1)
                if s >= 7 and (s - 7) % 4 == 0:
                    o = (s - 7) // 4
                    b, kv = divmod(o, 2)
                    dve.wait_ge(s_ah, o + 1)
                    d_ = lambda z: z[:, 2 * kv:2 * kv + 2, b * P:(b + 1) * P]
                    nc.vector.tensor_sub(d_(aTl), pv_bank[o % 2][:, 0:2 * P].rearrange("p (w n) -> p w n", n=P), d_(aTh).bitcast(F32)).then_inc(s_al, 1)

            def gate_of(e):
                return gate[:, :] if e < 3 else gate1[:, e - 3, :]

            def update(e, t):
                q = 4 * (e - 1) + t
                dve.wait_ge(s_rsy, q + 1)
                nc.vector.scalar_tensor_tensor(out=ys[:, t, :], in0=ys[:, t, :], scalar=stat[:, 2, q:q + 1], in1=gate_of(e),
                                               op0=ALU.mult, op1=ALU.mult).then_inc(s_yg, 1)
                if e == 1:
                    dve.wait_ge(s_x, 16 * NT)
                dve.wait_ge(s_yg, q + 1)
                nc.vector.tensor_tensor(xs[:, t, 0:D // 2], xs[:, t, 0:D // 2], ys[:, t, 0:D // 2], ALU.add).then_inc(s_xup, 1)

            def norm_x(e, t):
                dve.wait_ge(s_xup, 4 * (e - 1) + t + 1)
                xn(norm_index(e, t), ys[:, t, :], xs[:, t, :])

            def transition(e, pieces, splits):
                pieces(0)
                for t in range(NT + 3):
                    if t >= 3 and e < 4:
                        h_low(norm_index(e, t - 3), 1)
                    if t + 1 < NT:
                        pieces(t + 1)
                    if t < NT:
                        update(e, t)
                    if (t, 0) in splits:
                        straight_low(dve, splits[t, 0])
                    if 1 <= t <= NT and e < 4:
                        norm_x(e, t - 1)
                    if 2 <= t < NT + 2 and e < 4:
                        h_low(norm_index(e, t - 2), 0)
                    if (t, 1) in splits:
                        straight_low(dve, splits[t, 1])

            def out_projection(e, h0):
                for u in range(2):
                    straight_low(dve, h0 + 3 + 2 * u)
                    for t in range(NT):
                        last_of(dve, s_row, t, NT, h0 + 2 * u + 1, rows_before[e] + 3 * u)
                        nc.vector.tensor_copy(ys[:, t, 256 * u:256 * (u + 1)], dn[t][:, 0:256]).then_inc(s_rowf, 1)
                    if (e, u) == (1, 0):
                        for a in range(2):
                            fin(4 + a, up[3 - a], "scale", a, (1, 2 * KT))
                    straight_low(dve, h0 + 4 + 2 * u)
                straight_low(dve, h0 + 7)

                def piece(t):
                    last_of(dve, s_row, t, NT, h0 + 7, rows_before[e] + 6)
                    nc.vector.tensor_copy(ys[:, t, 512:768], up[t][:, 0:256])
                    nc.vector.tensor_copy(ys[:, t, 768:1024], dn[t][:, 0:256]).then_inc(s_rowf, 1)
                return piece

            piece = out_projection(1, 2 * 9)
            transition(1, piece, next_splits(B_FFN0, True))

            def ffn(layer):
                hb = (B_FFN0, B_FFN1)[layer]
                jb = 2 * NPAIR * layer
                pb = 8 * NPAIR * layer

                def taps(i):
                    if isinstance(i, int):
                        src = convc[:, layer, 2 * i:2 * i + 2, :]
                    else:
                        src = convc[:, layer, bass.ds(i * 2, 2), :]
                    nc.vector.tensor_copy(cw[:, :].rearrange("p (j w) -> p j w", w=3), src).then_inc(s_cw, 1)

                def other_taps(i, jj):
                    dve.wait_ge(s_g1, jb + 2 * i + jj + 1)
                    ch.link(nc.vector.scalar_tensor_tensor(out=conv[:, jj, 1:T], in0=up[jj][:, 0:T - 1], scalar=cw[:, 3 * jj:3 * jj + 1],
                                                           in1=conv[:, jj, 1:T], op0=ALU.mult, op1=ALU.add))
                    nc.vector.scalar_tensor_tensor(out=conv[:, jj, 0:T - 1], in0=up[jj][:, 1:T], scalar=cw[:, 3 * jj + 2:3 * jj + 3],
                                                   in1=conv[:, jj, 0:T - 1], op0=ALU.mult, op1=ALU.add).then_inc(s_gc, 1)

                def gated(i, jj):
                    h, dh = ffn_half(layer, i, ("v0", "v1")[jj])
                    dve.wait_ge(s_used, h + 1 + dh)
                    dve.wait_ge(s_si, jb + 2 * i + jj + 1)
                    nc.vector.tensor_tensor(actF[:, jj, :], up[2 + jj], sil[:, jj, :], ALU.mult).then_inc(s_am, 1)

                def act_low(i, jj):
                    dve.wait_ge(s_ahh, jb + 2 * i + jj + 1)
                    nc.vector.tensor_sub(actL[:, jj, :], actF[:, jj, :], actH[:, jj, :].bitcast(F32)).then_inc(s_all, 1)

                def add_piece(i, p):
                    t, hh = divmod(p, 2)
                    if p < 7:
                        dve.wait_ge(s_dp, 7 * NPAIR * layer + 7 * i + p + 1)
                    else:
                        h, dh = ffn_half(layer, i, "d1")
                        dve.wait_ge(s_used, h + 1 + dh)
                    dst = ys[:, t, hh * 512:(hh + 1) * 512]
                    if isinstance(i, int) and i == 0:
                        nc.vector.tensor_copy(dst, dn[p % 3]).then_inc(s_ya, 1)
                    else:
                        nc.vector.tensor_tensor(dst, dn[p % 3], dst, ALU.add).then_inc(s_ya, 1)

                def turn(i, jobs=None, last=False):
                    zero = isinstance(i, int) and i == 0
                    if not zero:
                        gated(i - 1, 1)
                        ffn_split(dve, "low", layer, i - 1, "d1")
                        act_low(i - 1, 1)
                        if jobs:
                            jobs("g0")
                    taps(i)
                    other_taps(i, 0)
                    if not zero:
                        for p in range(8):
                            add_piece(i - 1, p)
                            if jobs and p in (2, 5):
                                jobs("d", p // 3)
                            if p == 3:
                                ffn_split(dve, "low", layer, i, "v0")
                        ffn_split(dve, "low", layer, i, "g1")
                    ffn_split(dve, "low", layer, i, "v1")
                    if jobs:
                        jobs("v0")
                    gated(i, 0)
                    act_low(i, 0)
                    if jobs:
                        jobs("g1")
                    other_taps(i, 1)
                    if not last:
                        ffn_split(dve, "low", layer, i + 1, "g0")
                    ffn_split(dve, "low", layer, i, "d0")
                    if jobs:
                        jobs("v1")

                turn(0)
                turn(1)
                ch.loop(2, NPAIR - 1, 2, turn)
                if layer == 0:
                    kinds = {0: ("shift", 2), 1: ("scale", (2, 4 * KT)), 2: ("gate", gate1[:, 0, :]),
                             3: ("shift", 3), 4: ("scale", (3, 6 * KT)), 5: ("gate", gate1[:, 1, :]), 6: ("gate", gate)}

                    def jobs(what, only=None):
                        for n in ffn_jobs[what] if only is None else ffn_jobs[what][only:only + 1]:
                            m, hh = divmod(n, 2)
                            k, where = kinds[m]
                            if k == "gate":
                                dve.wait_ge(s_gain, 16 * 3)
                            fin(6 + n, dn[3], k, hh, where)
                    turn(NPAIR - 1, jobs=jobs, last=True)
                else:
                    turn(NPAIR - 1, last=True)
                i = NPAIR - 1
                ffn_split(dve, "low", layer, i, "d1")
                gated(i, 1)
                act_low(i, 1)

                def piece(t):
                    add_piece(i, 2 * t)
                    add_piece(i, 2 * t + 1)
                return piece

            piece = ffn(0)
            straight_low(dve, B_L1)
            transition(2, piece, next_splits(B_L1, False))

            nc.vector.memset(pu[:, 0, 0:8], 0.0).then_inc(s_init, 1)
            nc.vector.memset(pu[:, 0, T + 8:T + 16], 0.0).then_inc(s_init, 1)
            for n in range(4):
                dve.wait_ge(s_xh, n + 1)
                nc.vector.tensor_sub(xTl[:, n, :], up[n], xTh[:, n, :].bitcast(F32)).then_inc(s_xl, 1)
                straight_low(dve, B_L1 + 3 + n)
            def windows(i, g):
                w = WINDOWS[g]
                dve.wait_ge(s_u, i + 1)
                dve.wait_ge(s_init, 7)
                W(dve, s_pil, i)
                src, length, span, n = pu[:, 0, :], T + 16, 1, 0
                while span < w:
                    length -= span
                    dst = pu[:, 1 + n % 2, :]
                    ch.link(nc.vector.tensor_tensor(dst[:, 0:length], src[:, 0:length], src[:, span:span + length], ALU.add))
                    src, span, n = dst, 2 * span, n + 1
                o = 8 - w // 2
                nc.vector.tensor_tensor(src[:, o:o + 8], src[:, o:o + 8], edge[:, g, 0:8], ALU.mult)
                ch.link(nc.vector.tensor_tensor(src[:, o + T - 8:o + T], src[:, o + T - 8:o + T], edge[:, g, 8:16], ALU.mult))
                nc.vector.scalar_tensor_tensor(out=pu[:, 1 + n % 2, 0:T], in0=src[:, o:o + T], scalar=1.0 / w, in1=pu[:, 0, 8:T + 8],
                                               op0=ALU.mult, op1=ALU.subtract).then_inc(s_pw, 1)
                dve.wait_ge(s_pih, i + 1)
                nc.vector.tensor_sub(bTl[:, g, :], pu[:, 1 + n % 2, 0:T], bTh[:, g, :].bitcast(F32)).then_inc(s_pil, 1)

            for i in range(3):
                windows(i, GROUPS[i])
                straight_low(dve, B_L1 + 7 + i)
            for n in range(16):
                tt, g = divmod(n, 4)
                dve.wait_ge(s_cah, n + 1)
                d_ = lambda z: z[:, :, g * P:(g + 1) * P].rearrange("p (s t) n -> p s t n", s=2)[:, :, tt, :]
                nc.vector.tensor_sub(d_(xcsL), dn[n % 4][:, 0:256].rearrange("p (s n) -> p s n", n=P), d_(xcsH).bitcast(F32)).then_inc(s_cal, 1)
            windows(3, GROUPS[3])
            straight_low(dve, B_L1 + 10)
            straight_low(dve, B_L1 + 11)
            for i, g in enumerate(GROUPS):
                dve.wait_ge(s_pgh, i + 1)
                nc.vector.tensor_sub(bTl[:, g, :], hf[:, g % 2, :, :].rearrange("p k n -> p (k n)"), bTh[:, g, :].bitcast(F32)).then_inc(s_pgl, 1)
            straight_low(dve, B_L1 + 12)
            for ck in range(2):
                straight_low(dve, B_L1 + 13 + 2 * ck)
                for g in range(4):
                    dve.wait_ge(s_tdh, 4 * ck + g + 1)
                    nc.vector.tensor_sub(bTl[:, 4 + g, ck * 256:(ck + 1) * 256], dn[g][:, 0:256],
                                         bTh[:, 4 + g, ck * 256:(ck + 1) * 256].bitcast(F32)).then_inc(s_tdl, 1)
                straight_low(dve, B_L1 + 14 + 2 * ck)
            piece = out_projection(3, B_L1 + 14)
            transition(3, piece, next_splits(B_FFN1, True))
            piece = ffn(1)
            transition(4, piece, {})

        @block.tensor
        def _(pe):
            def three(dst, ah, al, bh, bl, start, stop):
                nc.tensor.matmul(dst, ah, bh, start=start, stop=False)
                nc.tensor.matmul(dst, ah, bl, start=False, stop=False)
                return nc.tensor.matmul(dst, al, bh, start=False, stop=stop)

            def norm_transposes(n):
                pe.wait_ge(s_xn, n + 1)
                if n >= 2:
                    for b in range(2):
                        h_done(pe, n - 2, b)
                for b in range(2):
                    for k in range(4):
                        ins = nc.tensor.transpose(norm_bank(n, b)[:, k * P:(k + 1) * P],
                                                  norm_src(n)[:, (4 * b + k) * P:(4 * b + k + 1) * P], ident[:, :])
                    ins.then_inc(s_tr, 1)

            pe.wait_ge(s_cvec, 16 * 3)
            nc.tensor.transpose(up[3][:, 0:16], cvec[:, :], ident[0:16, 0:16]).then_inc(s_vt, 1)
            pe.wait_ge(s_silu, 1)
            sc = siluc[:, :].rearrange("p (v k) -> p k v", v=2)
            for k in range(KT):
                pe.wait_ge(s_first[k % 4], 16 * (k // 4 + 1))
                for n in range(4):
                    ins = nc.tensor.matmul(dn[n][0:2, :], sc[:, k, :], mfirst[:, k % 4, n * 512:(n + 1) * 512], start=(k == 0), stop=(k == KT - 1))
                ins.then_inc(s_mr if k == KT - 1 else s_mfu, 1)
                if k == 0:
                    pe.wait_ge(s_vecs, 16 * 4)
                    nc.tensor.transpose(up[0][:, 0:96], vecs[0:96, :], ident[0:96, 0:96]).then_inc(s_vt, 1)
                    pe.wait_ge(s_vecf, 16 * 2)
                    for l in range(2):
                        nc.tensor.transpose(up[1 + l][:, 0:3 * NJ], vecf[0:3 * NJ, l, :], ident[0:3 * NJ, 0:3 * NJ]).then_inc(s_vt, 1)
                if k == 4:
                    pe.wait_ge(s_cols, 2)
                    norm_transposes(0)
                if k == 5:
                    norm_transposes(1)
            pe.wait_ge(s_mrb, 1)
            pe.wait_ge(s_mra, 1)
            for k in range(16):
                ins = nc.tensor.transpose(dn[0][:, 2 * k:2 * k + 2], mrow[:, k * P:(k + 1) * P], ident[0:2, 0:2])
            ins.then_inc(s_mrt, 1)
            for n in range(2, NT):
                norm_transposes(n)

            def stat_qkv(which):
                def f(r, k):
                    z, zc = ((hTh, hcTh), (hTl, hcTl))[which]
                    return z[:, k, r * P:(r + 1) * P] if r < 4 else zc[:, k, (r - 4) * P:(r - 3) * P]
                return f

            def qk_transposes(n):
                pe.wait_ge(s_rope, n + 1)
                W(pe, s_ql, n - 1) if n >= 2 else h_done(pe, NT + NTC - 1, 1)
                for h in range(4 if n < 8 else 2):
                    ins = nc.tensor.transpose(up[n % 2][:, h * P:(h + 1) * P], qd[:, n % 4, h, :], ident[:, :])
                ins.then_inc(s_qt, 1)

            banks6 = dn + up[2:4]
            for u in range(3):
                for a in range(2):
                    def before(r, u=u, a=a):
                        if a == 0:
                            if u == 0:
                                pe.wait_ge(s_hl, 2 * (r + 1))
                                if r == 0:
                                    pe.wait_ge(s_scl, 2)
                            elif r < 4:
                                pe.wait_ge(s_rope, 4 * (u - 1) + r + 1)
                            else:
                                pe.wait_ge(s_hl, 12)
                        elif u == 2 and r >= 2:
                            qk_transposes(8 + r - 2)
                    tm_half_ins(pe, three, half_view, 2 * u + a, 4 if u < 2 else 6, a, stat_qkv(0), stat_qkv(1), banks6, before, s_row, s_used, s_lo, wh, wl)
                    if (u, a) == (0, 0):
                        for n in range(NT, NT + NTC):
                            norm_transposes(n)
                    if u and a == 0:
                        for n in range(4 * (u - 1), 4 * u):
                            qk_transposes(n)
            for n in range(12, 14):
                qk_transposes(n)

            atoms = [(n, i) for n, (j, lo, hi) in enumerate(JOBS) for i in range(hi - lo)]
            def atom(n, i):
                kind, jj, a = JOBS[n][0]
                total = JOBS[n][2] - JOBS[n][1]
                if i == 0:
                    if n < 2:
                        pe.wait_ge(s_vl, 6)
                        pe.wait_ge(s_rope, 14)
                    else:
                        job_free(n - 2)
                if kind == "m":
                    if i == 0:
                        pe.wait_ge(s_msu, 8 * (jj - 1))
                        nc.tensor.matmul(job_bank[n % 2], ones[:, :], (macc1 if jj == 3 else macc0)[:, a * 512:(a + 1) * 512], start=True, stop=True).then_inc(s_msum, 1)
                    return
                h = half_of[n]
                if i == 0:
                    pe.wait_ge(s_lo, h + 1)
                k, p = divmod(i, 3)
                vh, vl = half_view(wh, h, "fm"), half_view(wl, h, "fm")
                wt = (vh, vh, vl)[p][:, k, :]
                mv = (hTh, hTl, hTh)[p][:, k, :]
                ins = nc.tensor.matmul(job_bank[n % 2], wt, mv, start=(i == 0), stop=(i == total - 1))
                if i == total - 1:
                    ins.then_inc(s_used, 1)

            def job_free(n):
                kind, jj, a = JOBS[n][0]
                if kind == "m":
                    pe.wait_ge(s_mfin, 2 * (jj - 2) + a + 1)
                elif kind == "c":
                    pe.wait_ge(s_jobf, 2 * jj + a + 1)
                elif kind == "z":
                    pe.wait_ge(s_cz, 2 * jj + a + 1)
                else:
                    pe.wait_ge(s_bs, 2 * jj + a + 1)

            def scores(s):
                b, kv, e, w = step_of(s)
                head = 4 * kv + e + 2 * w
                lo, nw = keys_of(b)
                if s == 0:
                    pe.wait_ge(s_rope, 14)
                    pe.wait_ge(s_vl, 6)
                    pe.wait_ge(s_ql, 14)
                else:
                    pe.wait_ge(s_max, s)
                a0, a1 = dn[0][:, 512 - nw * P:512], dn[1][:, 0:TC]
                q = qT[:, head, b * P:(b + 1) * P]
                for dst, k0, k1 in ((a0, lo * P, (lo + nw) * P), (a1, T, T + TC)):
                    nc.tensor.matmul(dst, q, kH[:, kv, k0:k1], start=True, stop=False)
                    ins = nc.tensor.matmul(dst, q, kL[:, kv, k0:k1], start=False, stop=True)
                ins.then_inc(s_sc, 1)

            def prob_transposes(r):
                nb = keys_of(step_of(r)[0])[1] + 2
                pe.wait_ge(s_pn, r + 1)
                W(pe, s_pl, r)
                for j in range(nb):
                    ins = nc.tensor.transpose(ps[:, j // 4, (j % 4) * P:(j % 4 + 1) * P], prob[:, r % 3, j * P:(j + 1) * P], ident[:, :])
                ins.then_inc(s_pt, 1)

            def values(g):
                b, kv, e, _ = step_of(2 * g)
                lo, nw = keys_of(b)
                pe.wait_ge(s_pl, 2 * g + 2)
                if e == 0:
                    W(pe, s_al, g // 2 - 1)
                bank = pv_bank[g // 2 % 2]
                off = 64 + 128 * kv - 64 * e
                for j in range(nw + 2):
                    tile = lo + j if j < nw else NT + j - nw
                    vh, vl = vH[:, tile, off:off + P], vL[:, tile, off:off + P]
                    mh, ml = (z[:, j, :, :].rearrange("p w n -> p (w n)") for z in (pTh, pTl))
                    nc.tensor.matmul(bank[:, 0:256], vh, mh, start=(e == 0 and j == 0), stop=False)
                    nc.tensor.matmul(bank[:, 0:256], vl, mh, start=False, stop=False)
                    ins = nc.tensor.matmul(bank[:, 0:256], vh, ml, start=False, stop=(e == 1 and j == nw + 1))
                ins.then_inc(s_pv, 1)

            def first_rows(r0):
                h = 2 * 9
                if r0 == 0:
                    pe.wait_ge(s_lo, h + 1)
                    pe.wait_ge(s_sl, 4)
                    pe.wait_ge(s_max, STEPS)
                    pe.wait_ge(s_al, STEPS // 4 - 1)
                for r in (r0, r0 + 1):
                    ins = tm_row(three, dn[r], 0, r, lambda r, k: aTh[:, 4 + k, r * P:(r + 1) * P], lambda r, k: aTl[:, 4 + k, r * P:(r + 1) * P],
                                 half_view(wh, h, "tm"), half_view(wl, h, "tm"))
                if r0:
                    ins.then_inc(s_used, 1)

            for s in range(STEPS + 3):
                if s < STEPS:
                    scores(s)
                mine = atoms[PER_STEP * s:PER_STEP * (s + 1)]
                cut = next((n for n, (j, i) in enumerate(mine) if i == 0), len(mine))
                for n, i in mine[:cut]:
                    atom(n, i)
                if s >= 4 and s % 2 == 0:
                    values((s - 4) // 2)
                if 2 <= s < STEPS + 2:
                    prob_transposes(s - 2)
                for n, i in mine[cut:]:
                    atom(n, i)
                if s in (STEPS, STEPS + 1):
                    first_rows(2 * (s - STEPS))

            def out_projection(e, h0, th, tl, order):
                stat_h = lambda r, k: th[:, order[k], r * P:(r + 1) * P]
                stat_l = lambda r, k: tl[:, order[k], r * P:(r + 1) * P]
                for u in range(3):
                    for a in range(2):
                        if (e, u, a) == (1, 0, 0) or (u, a) == (2, 1):
                            continue

                        if (e, u, a) == (1, 1, 0):
                            pe.wait_ge(s_msu, 3 * KT)
                            for n in range(2):
                                nc.tensor.matmul(up[3 - n], ones[:, :], macc0[:, n * 512:(n + 1) * 512], start=True, stop=True).then_inc(s_msum, 1)
                        if (e, u, a) == (1, 2, 0):
                            pe.wait_ge(s_mfin, 6)

                        def before(r, u=u, a=a):
                            if (u, a) == (1, 0):
                                pe.wait_ge(s_rowf, 3 * NT * (e // 2) + r + 1)
                        tm_half_ins(pe, three, half_view, h0 + 2 * u + a, 4, a, stat_h, stat_l,
                                    up if u == 2 else dn, before, s_row, s_used, s_lo, wh, wl, first=lambda a=a, u=u: out_ready(e, u, a))
                for r in range(NT):
                    for h, a, bank in ((h0 + 5, 1, up[r]), (h0 + 6, 0, dn[r]), (h0 + 7, 1, dn[r])):
                        pe.wait_ge(s_lo, h + 1)
                        if h == h0 + 6:
                            pe.wait_ge(s_rowf, 3 * NT * (e // 2) + NT + r + 1)
                        ins = tm_row(three, bank, a, r, stat_h, stat_l, half_view(wh, h, "tm"), half_view(wl, h, "tm"))
                        if r == NT - 1:
                            ins.then_inc(s_used, 1)
                        elif h == h0 + 7:
                            ins.then_inc(s_row, 1)

            def out_ready(e, u, a):
                if u == 0 and e == 1:
                    pe.wait_ge(s_al, STEPS // 4)
                if u == 0 and e == 3 and a == 0:
                    pe.wait_ge(s_pgl, 4)
                    pe.wait_ge(s_tdl, 8)

            def transition(e, h0):
                for t in range(3):
                    norm_transposes(norm_index(e, t))
                for part in range(2):
                    cols = slice(256 * part, 256 * part + 256)
                    pe.wait_ge(s_hl, 2 * norm_index(e, 2 * part + 1) + 2)
                    for n in range(3):
                        h, bank = h0 + n, up[start_bank(e, n)]
                        pe.wait_ge(s_lo, h + 1)
                        vh, vl = half_view(wh, h, "fm"), half_view(wl, h, "fm")
                        for k in range(KT):
                            ins = three(bank[:, cols], vh[:, k, :], vl[:, k, :], hTh[:, k, cols], hTl[:, k, cols], k == 0, k == KT - 1)
                        if part == 0 and n == 0:
                            norm_transposes(norm_index(e, 3))
                        if part == 1:
                            ins.then_inc(s_used, 1)

            def start_bank(e, n):
                return n if e == 2 else (0, 2, 1)[n]

            out_projection(1, 18, aTh, aTl, (4, 5, 6, 7, 0, 1, 2, 3))
            transition(1, B_FFN0)

            def ffn(layer):
                hb = (B_FFN0, B_FFN1)[layer]
                jb = 2 * NPAIR * layer
                pb = 8 * NPAIR * layer
                e = 1 + 2 * layer

                def up_half(i, what):
                    h, dh = ffn_half(layer, i, what)
                    jj = int(what[1])
                    pe.wait_ge(s_lo, h + 1 + dh)
                    if isinstance(i, int) and i == 0:
                        pe.wait_ge(s_hl, 2 * norm_index(e, NT - 1) + 2)
                    elif what[0] == "g":
                        pe.wait_ge(s_gc, jb + 2 * i + jj - 1)
                    else:
                        pe.wait_ge(s_am, jb + 2 * i + jj - 1)
                    dst = up[jj + (2 if what[0] == "v" else 0)]
                    vh, vl = half_view(wh, h, "fm"), half_view(wl, h, "fm")
                    for k in range(KT):
                        nc.tensor.matmul(dst, vh[:, k, :], hTh[:, k, :], start=(k == 0), stop=False)
                        nc.tensor.matmul(dst, vh[:, k, :], hTl[:, k, :], start=False, stop=False)
                        ins = nc.tensor.matmul(dst, vl[:, k, :], hTh[:, k, :], start=False, stop=(k == KT - 1))
                        if k == KT - 1:
                            ins.then_inc(s_used, 1)
                        if k == 2 or k == 5 or k == KT - 1:
                            yield k

                def down(i, between=None):
                    h, dh = ffn_half(layer, i, "d0")
                    wv = lambda z, hh, jj: z[:, (h + jj) % RING, hh * 512:(hh + 1) * 512]
                    act_ = lambda z, t, jj: z[:, jj, t * P:(t + 1) * P]
                    pe.wait_ge(s_lo, h + 2 + dh)
                    ahead = 0
                    if isinstance(i, int) and i == NPAIR - 1:
                        pe.wait_ge(s_all, jb + 2 * i + 1)
                        ahead = 3
                        for p in range(ahead):
                            t, hh = divmod(p, 2)
                            pe.wait_ge(s_ya, pb + 8 * i + (-1, 0, -2)[p])
                            three(dn[p], act_(actH, t, 0), act_(actL, t, 0), wv(wh, hh, 0), wv(wl, hh, 0), start=True, stop=False)
                    pe.wait_ge(s_all, jb + 2 * i + 2)
                    for p in range(8):
                        t, hh = divmod(p, 2)
                        if not (isinstance(i, int) and i == 0) or p >= 3:
                            pe.wait_ge(s_ya, pb + 8 * i + (-1, 0, -2)[p] if p < 3 else pb + 8 * i + p - 2)
                        for jj in range(1 if p < ahead else 0, 2):
                            ins = three(dn[p % 3], act_(actH, t, jj), act_(actL, t, jj), wv(wh, hh, jj), wv(wl, hh, jj),
                                        start=(jj == 0), stop=(jj == 1))
                        if p < 7:
                            ins.then_inc(s_dp, 1)
                        else:
                            ins.then_inc(s_used, 2)
                        if between and p in (2, 5):
                            between(p)

                def job(n):
                    if n:
                        pe.wait_ge(s_mfin, 6 + n)
                    m, hh = divmod(n, 2)
                    nc.tensor.matmul(dn[3], ones[:, :], macc[:, m, hh * 512:(hh + 1) * 512], start=True, stop=True).then_inc(s_msum, 1)

                def turn(i, jobs=False):
                    def half(what):
                        for n, _ in enumerate(up_half(i, what)):
                            if jobs:
                                job(ffn_jobs[what][n])
                    if isinstance(i, int) and i == 0:
                        half("v1")
                        return
                    half("g0")
                    down(i - 1, (lambda p: job(ffn_jobs["d"][p // 3])) if jobs else None)
                    half("v0")
                    half("g1")
                    half("v1")

                turn(0)
                turn(1)
                with pe.Fori(2, NPAIR - 1) as i:
                    turn(i)
                if layer == 0:
                    pe.wait_ge(s_msu, 10 * KT)
                turn(NPAIR - 1, jobs=(layer == 0))
                down(NPAIR - 1)

            ffn(0)
            transition(2, B_L1)

            for n in range(3, 8):
                h = B_L1 + n
                pe.wait_ge(s_lo, h + 1)
                if n >= 4:
                    pe.wait_ge(s_xl, n - 3)
                vh, vl = half_view(wh, h, "fm"), half_view(wl, h, "fm")
                for k in range(KT):
                    nc.tensor.matmul(up[n % 4], vh[:, k, :], hTh[:, k, :], start=(k == 0), stop=False)
                    nc.tensor.matmul(up[n % 4], vh[:, k, :], hTl[:, k, :], start=False, stop=False)
                    ins = nc.tensor.matmul(up[n % 4], vl[:, k, :], hTh[:, k, :], start=False, stop=(k == KT - 1))
                ins.then_inc(s_used, 1)
            h = B_L1 + 8
            pe.wait_ge(s_lo, h + 1)
            pe.wait_ge(s_xl, 4)
            for n in range(16):
                tt, g = divmod(n, 4)
                if n >= 4:
                    pe.wait_ge(s_cal, n - 3)
                ins = three(dn[n % 4][:, 0:256], xTh[:, g, tt * P:(tt + 1) * P], xTl[:, g, tt * P:(tt + 1) * P],
                            wh[:, h % RING, 0:256], wl[:, h % RING, 0:256], True, True)
                ins.then_inc(s_ca if n < 15 else s_used, 1)
            h = B_L1 + 9
            pe.wait_ge(s_lo, h + 1)
            for i, g in enumerate(GROUPS):
                pe.wait_ge(s_pil, i + 1)
                pe.wait_ge(s_u, i + 1)
                ins = three(up[i], wh[:, h % RING, g * P:(g + 1) * P], wl[:, h % RING, g * P:(g + 1) * P], bTh[:, g, :], bTl[:, g, :], True, True)
                ins.then_inc(s_pg if i < 3 else s_used, 1)
            for ck in range(2):
                for a in range(2):
                    def before(r, ck=ck, a=a):
                        if a == 0 and ck:
                            pe.wait_ge(s_tdl, r + 1)
                    tm_half_ins(pe, three, half_view, B_L1 + 10 + 2 * ck + a, 4, a,
                                lambda r, k: xcsH[:, k, r * P:(r + 1) * P], lambda r, k: xcsL[:, k, r * P:(r + 1) * P],
                                dn, before, s_td, s_used, s_lo, wh, wl, first=lambda: pe.wait_ge(s_cal, 16))
            out_projection(3, B_L1 + 14, bTh, bTl, tuple(range(8)))
            transition(3, B_FFN1)
            ffn(1)


def tm_row(three, bank, a, r, stat_h, stat_l, vh, vl):
    for k in range(4):
        ins = three(bank[:, 0:256], stat_h(r, 4 * a + k), stat_l(r, 4 * a + k), vh[:, k, :], vl[:, k, :],
                    a == 0 and k == 0, a == 1 and k == 3)
    return ins


def tm_half_ins(pe, three, half_view, h, rows, a, stat_h, stat_l, banks, before, done, s_used, s_lo, wh, wl, first=None):
    pe.wait_ge(s_lo, h + 1)
    if first:
        first()
    vh, vl = half_view(wh, h, "tm"), half_view(wl, h, "tm")
    for r in range(rows):
        before(r)
        ins = tm_row(three, banks[r], a, r, stat_h, stat_l, vh, vl)
        if a == 1 and r < rows - 1:
            ins.then_inc(done, 1)
    ins.then_inc(s_used, 1)


_INS = ["x", "c", "ctx", "c_ctx", "mod_w", "mod_b", "norm_g", "att_w_in", "att_sink", "sconv_w", "att_w_out",
        "mix_w_in", "pool_w_grp", "pool_scale", "mix_w_out", "ffn_w_up", "ffn_conv", "ffn_w_down"]


def kernel(**inputs):
    import concourse.bacc as _bacc
    from concourse.bass_utils import run_bass_kernel_spmd as _run

    nc = _bacc.Bacc("TRN2", target_bir_lowering=False, num_devices=1)
    arrays, args = {}, {}
    given = {name: np.ascontiguousarray(inputs[name]) for name in _INS}
    for name, a in {**given, **constants()}.items():
        arrays[f"in_{name}"] = a
        args[name] = nc.dram_tensor(f"in_{name}", a.shape, mybir.dt.from_np(a.dtype), kind="ExternalInput").ap()
    args["out"] = nc.dram_tensor("out", (1, T, D), F32, kind="ExternalOutput").ap()
    build(nc, **args)
    return _run(nc, [arrays], core_ids=[0]).results[0]["out"]
```
